# Optimizing a Trainium2 kernel written in Bass

```python
import jax, jax.numpy as jnp
from jax import lax
import numpy as np

D_MODEL = 1024
BATCH = 1
SEQ = 256
DEPTH = 1

ATTN_HEADS = 8
HEAD_DIM = D_MODEL // 16
ATTN_WIDTH = ATTN_HEADS * HEAD_DIM
ROPE_DIM = HEAD_DIM // 4
ROPE_THETA = 500000.0
MOBA_BLOCK = 256
MOBA_TOP_K = 3
QUERY_CHUNK = 64
POOL_WINDOWS = (2, 4, 8, 16)
POOL_GROUPS = len(POOL_WINDOWS)
POOL_WIDTH = D_MODEL // 2
POOL_GROUP_DIM = POOL_WIDTH // POOL_GROUPS
N_BRANCHES = 2
IN_WIDTH = 3 * ATTN_WIDTH + POOL_WIDTH + N_BRANCHES * D_MODEL
D_FF = 2816
CONV_WIDTH = 3
EPS = 1e-6
NEG_INF = -1e30


def rmsnorm(x, g):
    xf = x.astype(jnp.float32)
    y = xf * lax.rsqrt(jnp.mean(xf * xf, axis=-1, keepdims=True) + EPS)
    return (y * g.astype(jnp.float32)).astype(x.dtype)

def apply_partial_rotary(x, positions):
    half = ROPE_DIM // 2
    inv_freq = ROPE_THETA ** (-jnp.arange(half, dtype=jnp.float32) / half)
    ang = positions.astype(jnp.float32)[:, None] * inv_freq[None, :]
    cos = jnp.cos(ang).astype(x.dtype)
    sin = jnp.sin(ang).astype(x.dtype)
    x1 = x[..., :half]
    x2 = x[..., half:ROPE_DIM]
    return jnp.concatenate([x1 * cos - x2 * sin, x2 * cos + x1 * sin, x[..., ROPE_DIM:]], axis=-1)

def moba_attention(q, k, v):
    B, H, S, Dh = q.shape
    nb = -(-S // MOBA_BLOCK)
    pad = nb * MOBA_BLOCK - S
    k_p = jnp.pad(k, ((0, 0), (0, 0), (0, pad), (0, 0)))
    v_p = jnp.pad(v, ((0, 0), (0, 0), (0, pad), (0, 0)))
    k_blk = k_p.reshape(B, H, nb, MOBA_BLOCK, Dh)
    v_blk = v_p.reshape(B, H, nb, MOBA_BLOCK, Dh)
    k_mean = jnp.mean(k_blk.astype(jnp.float32), axis=3).astype(k.dtype)
    top_k = min(MOBA_TOP_K, nb)
    scale = Dh ** -0.5
    n_chunks = S // QUERY_CHUNK
    gather_blocks = jax.vmap(jax.vmap(lambda kb, idx: kb[idx]))

    def chunk(c):
        start = c * QUERY_CHUNK
        qc = lax.dynamic_slice_in_dim(q, start, QUERY_CHUNK, axis=2)
        q_pos = start + jnp.arange(QUERY_CHUNK)
        own = start // MOBA_BLOCK
        s_blk = jnp.einsum('bhqd,bhnd->bhqn', qc, k_mean).astype(jnp.float32)
        s_blk = jnp.where(jnp.arange(nb) < own, s_blk, -jnp.inf)
        _, sel = lax.top_k(s_blk, top_k)
        sel_valid = sel < own
        k_sel = gather_blocks(k_blk, sel)
        v_sel = gather_blocks(v_blk, sel)
        logit_sel = jnp.einsum('bhqd,bhqkld->bhqkl', qc, k_sel).astype(jnp.float32) * scale
        logit_sel = jnp.where(sel_valid[..., None], logit_sel, NEG_INF)
        k_own = lax.dynamic_index_in_dim(k_blk, own, axis=2, keepdims=False)
        v_own = lax.dynamic_index_in_dim(v_blk, own, axis=2, keepdims=False)
        logit_own = jnp.einsum('bhqd,bhld->bhql', qc, k_own).astype(jnp.float32) * scale
        k_pos_own = own * MOBA_BLOCK + jnp.arange(MOBA_BLOCK)
        logit_own = jnp.where(k_pos_own[None, :] <= q_pos[:, None], logit_own, NEG_INF)
        n_sel = top_k * MOBA_BLOCK
        logits = jnp.concatenate(
            [logit_sel.reshape(B, H, QUERY_CHUNK, n_sel), logit_own], axis=-1)
        p = jax.nn.softmax(logits, axis=-1).astype(v.dtype)
        p_sel = p[..., :n_sel].reshape(B, H, QUERY_CHUNK, top_k, MOBA_BLOCK)
        p_own = p[..., n_sel:]
        return (jnp.einsum('bhqkl,bhqkld->bhqd', p_sel, v_sel)
                + jnp.einsum('bhql,bhld->bhqd', p_own, v_own))

    outs = lax.map(chunk, jnp.arange(n_chunks))
    return outs.transpose(1, 2, 0, 3, 4).reshape(B, H, S, Dh)

def multiscale_pool_mixer(u, w_pool, pool_scale):
    B, S, _ = u.shape
    ug = u.reshape(B, S, POOL_GROUPS, POOL_GROUP_DIM).astype(jnp.float32)
    cs = jnp.cumsum(ug, axis=1)
    t = jnp.arange(S, dtype=jnp.float32)[None, :, None]
    groups = []
    for g, w in enumerate(POOL_WINDOWS):
        c = cs[:, :, g]
        c_prev = jnp.pad(c, ((0, 0), (w, 0), (0, 0)))[:, :S]
        count = jnp.minimum(t + 1.0, float(w))
        groups.append((c - c_prev) / count - ug[:, :, g])
    pooled = jnp.stack(groups, axis=2).astype(u.dtype)
    mixed = jnp.einsum('bsgc,gcd->bsgd', pooled, w_pool)
    return mixed.reshape(B, S, POOL_WIDTH) * pool_scale

def causal_depthwise_conv(u, w, b):
    S = u.shape[1]
    kw = w.shape[0]
    up = jnp.pad(u, ((0, 0), (kw - 1, 0), (0, 0)))
    out = up[:, 0:S] * w[0]
    for j in range(1, kw):
        out = out + up[:, j:j + S] * w[j]
    return out + b

def hybrid_layer(x, norm_mix_g, w_in, b_gate, q_norm_g, k_norm_g, w_pool, pool_scale,
                 w_branch_attn, w_branch_pool, w_out, norm_ffn_g, w_up, conv_w, conv_b, w_down):
    B, S, D = x.shape
    h = rmsnorm(x, norm_mix_g)
    proj = h @ w_in
    q, k, v, u_pool, gate_logits = jnp.split(
        proj, [ATTN_WIDTH, 2 * ATTN_WIDTH, 3 * ATTN_WIDTH, 3 * ATTN_WIDTH + POOL_WIDTH], axis=-1)

    def heads(t):
        return t.reshape(B, S, ATTN_HEADS, HEAD_DIM).transpose(0, 2, 1, 3)

    pos = jnp.arange(S)
    q = apply_partial_rotary(rmsnorm(heads(q), q_norm_g), pos)
    k = apply_partial_rotary(rmsnorm(heads(k), k_norm_g), pos)
    attn = moba_attention(q, k, heads(v)).transpose(0, 2, 1, 3).reshape(B, S, ATTN_WIDTH)
    pooled = multiscale_pool_mixer(u_pool, w_pool, pool_scale)

    gates = jax.nn.sigmoid(gate_logits + b_gate).reshape(B, S, N_BRANCHES, D)
    mixed = gates[:, :, 0] * (attn @ w_branch_attn) + gates[:, :, 1] * (pooled @ w_branch_pool)
    x = x + mixed @ w_out

    h2 = rmsnorm(x, norm_ffn_g)
    up = causal_depthwise_conv(h2 @ w_up, conv_w, conv_b)
    gate, val = jnp.split(up, 2, axis=-1)
    return x + (jax.nn.silu(gate) * val) @ w_down

def first_inputs(seed: int = 0) -> dict:
    key = jax.random.key(seed)
    ks = jax.random.split(key, 17)
    L = DEPTH
    f32 = jnp.float32

    def nrm(k, shape, scale):
        return jax.random.normal(k, shape, f32) * scale

    return {
        "x": nrm(ks[0], (BATCH, SEQ, D_MODEL), 1.0),
        "norm_mix_g": 1.0 + nrm(ks[1], (L, D_MODEL), 0.02),
        "w_in": nrm(ks[2], (L, D_MODEL, IN_WIDTH), D_MODEL ** -0.5),
        "b_gate": nrm(ks[3], (L, N_BRANCHES * D_MODEL), 0.1),
        "q_norm_g": 1.0 + nrm(ks[4], (L, HEAD_DIM), 0.02),
        "k_norm_g": 1.0 + nrm(ks[5], (L, HEAD_DIM), 0.02),
        "w_pool": nrm(ks[6], (L, POOL_GROUPS, POOL_GROUP_DIM, POOL_GROUP_DIM), POOL_GROUP_DIM ** -0.5),
        "pool_scale": 1.0 + nrm(ks[7], (L, POOL_WIDTH), 0.1),
        "w_branch_attn": nrm(ks[8], (L, ATTN_WIDTH, D_MODEL), ATTN_WIDTH ** -0.5),
        "w_branch_pool": nrm(ks[9], (L, POOL_WIDTH, D_MODEL), POOL_WIDTH ** -0.5),
        "w_out": nrm(ks[10], (L, D_MODEL, D_MODEL), D_MODEL ** -0.5),
        "norm_ffn_g": 1.0 + nrm(ks[11], (L, D_MODEL), 0.02),
        "w_up": nrm(ks[12], (L, D_MODEL, 2 * D_FF), D_MODEL ** -0.5),
        "conv_w": nrm(ks[13], (L, CONV_WIDTH, 2 * D_FF), CONV_WIDTH ** -0.5),
        "conv_b": nrm(ks[14], (L, 2 * D_FF), 0.02),
        "w_down": nrm(ks[15], (L, D_FF, D_MODEL), D_FF ** -0.5),
    }

def first_block(x, norm_mix_g, w_in, b_gate, q_norm_g, k_norm_g, w_pool, pool_scale,
              w_branch_attn, w_branch_pool, w_out, norm_ffn_g, w_up, conv_w, conv_b, w_down):
    for l in range(DEPTH):
        x = hybrid_layer(x, norm_mix_g[l], w_in[l], b_gate[l], q_norm_g[l], k_norm_g[l],
                         w_pool[l], pool_scale[l], w_branch_attn[l], w_branch_pool[l], w_out[l],
                         norm_ffn_g[l], w_up[l], conv_w[l], conv_b[l], w_down[l])
    return x


MIX_WIDTH = D_MODEL
CONV_CH = MIX_WIDTH // 2
RWKV_CH = MIX_WIDTH - CONV_CH
RWKV_HEAD = 64
RWKV_HEADS = RWKV_CH // RWKV_HEAD
CONV_WIDTH_2 = 31
LORA_W = 64
LORA_A = 64
LORA_G = 128
RWKV_PROJ = 3 * RWKV_CH + LORA_W + LORA_A + LORA_G
IN_PROJ = 2 * CONV_CH + RWKV_PROJ
RWKV_SPLITS = [RWKV_CH, 2 * RWKV_CH, 3 * RWKV_CH, 3 * RWKV_CH + LORA_W, 3 * RWKV_CH + LORA_W + LORA_A]
PEER_HEADS = 8
PEER_NKEYS = 128
PEER_EXPERTS = PEER_NKEYS * PEER_NKEYS
PEER_DQ = 256
PEER_TOPK = 16
PEER_CHUNK = 128
RMS_EPS = 1e-6
LN_EPS = 1e-5
GN_EPS = 64e-5


F32 = jnp.float32

def rmsnorm_2(x, g):
    xf = x.astype(F32)
    y = xf * lax.rsqrt(jnp.mean(xf * xf, axis=-1, keepdims=True) + RMS_EPS)
    return (y * g.astype(F32)).astype(x.dtype)

def modulate(x, shift, scale):
    return x * (1 + scale[:, None, :]) + shift[:, None, :]

def conformer_conv(p_conv, w_dw, b_dw, ln_w, ln_b):
    a, b = jnp.split(p_conv, 2, axis=-1)
    y = a * jax.nn.sigmoid(b)
    y = lax.conv_general_dilated(
        y, w_dw[:, None, :], window_strides=(1,), padding=[(CONV_WIDTH_2 - 1, 0)],
        dimension_numbers=('NWC', 'WIO', 'NWC'), feature_group_count=CONV_CH) + b_dw
    yf = y.astype(F32)
    mu = jnp.mean(yf, axis=-1, keepdims=True)
    var = jnp.mean(jnp.square(yf - mu), axis=-1, keepdims=True)
    yf = (yf - mu) * lax.rsqrt(var + LN_EPS) * ln_w.astype(F32) + ln_b.astype(F32)
    return jax.nn.silu(yf).astype(p_conv.dtype)

def token_shift(p, mu):
    prev = jnp.pad(p, ((0, 0), (1, 0), (0, 0)))[:, :-1]
    return p + mu * (prev - p)

def rwkv7_mix(p_rwkv, mu, w0, w2, a0, a2, g2, k_k, k_a, r_k, gn_w, gn_b):
    B, S, _ = p_rwkv.shape
    xs = token_shift(p_rwkv, mu)
    r, k, v, wl, al, gl = jnp.split(xs, RWKV_SPLITS, axis=-1)
    w = -jax.nn.softplus(-(w0 + jnp.tanh(wl) @ w2)) - 0.5
    decay = jnp.exp(-jnp.exp(w.astype(F32)))
    a = jax.nn.sigmoid(a0 + al @ a2)
    g = jax.nn.sigmoid(gl) @ g2
    kk = k * k_k
    k = k * (1 + (a - 1) * k_a)

    def heads(t):
        return t.reshape(B, S, RWKV_HEADS, RWKV_HEAD).astype(F32)

    kk_h = heads(kk)
    kk_h = kk_h / jnp.maximum(jnp.sqrt(jnp.sum(kk_h * kk_h, axis=-1, keepdims=True)), 1e-12)
    r_h, k_h, v_h, w_h, a_h = heads(r), heads(k), heads(v), decay.reshape(B, S, RWKV_HEADS, RWKV_HEAD), heads(a)

    def step(state, inp):
        r_t, k_t, v_t, w_t, kk_t, a_t = inp
        sa = jnp.einsum('bhij,bhj->bhi', state, -kk_t)
        state = (state * w_t[:, :, None, :]
                 + sa[..., None] * (kk_t * a_t)[:, :, None, :]
                 + v_t[..., None] * k_t[:, :, None, :])
        y_t = jnp.einsum('bhij,bhj->bhi', state, r_t)
        return state, y_t

    def seq_first(t):
        return jnp.moveaxis(t, 1, 0)

    state0 = jnp.zeros((B, RWKV_HEADS, RWKV_HEAD, RWKV_HEAD), F32)
    _, y = lax.scan(step, state0, (seq_first(r_h), seq_first(k_h), seq_first(v_h),
                                   seq_first(w_h), seq_first(kk_h), seq_first(a_h)))
    y = jnp.moveaxis(y, 0, 1)
    mean = jnp.mean(y, axis=-1, keepdims=True)
    var = jnp.mean(jnp.square(y - mean), axis=-1, keepdims=True)
    y = ((y - mean) * lax.rsqrt(var + GN_EPS)).reshape(B, S, RWKV_CH) * gn_w.astype(F32) + gn_b.astype(F32)
    bonus = jnp.sum(r_h * k_h * r_k.astype(F32), axis=-1, keepdims=True) * v_h
    y = y + bonus.reshape(B, S, RWKV_CH)
    return (y * g.astype(F32)).astype(p_rwkv.dtype)

def peer_ffn(u, w_q, sub_keys, expert_u, expert_v):
    B, S, D = u.shape
    tokens = u.reshape(-1, PEER_CHUNK, D)

    def chunk(xc):
        tc = xc.shape[0]
        q = (xc @ w_q).reshape(tc, PEER_HEADS, 2, PEER_DQ // 2)
        s = jnp.einsum('thpd,hpkd->thpk', q, sub_keys).astype(F32)
        s_top, i_top = lax.top_k(s, PEER_TOPK)
        cand = s_top[:, :, 0, :, None] + s_top[:, :, 1, None, :]
        cand_idx = i_top[:, :, 0, :, None] * PEER_NKEYS + i_top[:, :, 1, None, :]
        best, pos = lax.top_k(cand.reshape(tc, PEER_HEADS, PEER_TOPK * PEER_TOPK), PEER_TOPK)
        expert = jnp.take_along_axis(cand_idx.reshape(tc, PEER_HEADS, PEER_TOPK * PEER_TOPK), pos, axis=-1)
        gate = jax.nn.softmax(best, axis=-1)
        ue = jnp.take(expert_u, expert, axis=0)
        ve = jnp.take(expert_v, expert, axis=0)
        h = jax.nn.gelu(jnp.einsum('thkd,td->thk', ue, xc).astype(F32), approximate=False)
        return jnp.einsum('thk,thkd->td', (gate * h).astype(xc.dtype), ve)

    out = lax.map(chunk, tokens)
    return out.reshape(B, S, D)

def second_inputs(seed: int = 0) -> dict:
    key = jax.random.key(seed)
    ks = iter(jax.random.split(key, 32))

    def nrm(shape, scale):
        return scale * jax.random.normal(next(ks), shape, jnp.float32)

    def gain(shape):
        return 1.0 + nrm(shape, 0.02)

    L = DEPTH
    return {
        'x': nrm((BATCH, SEQ, D_MODEL), 1.0),
        'c': nrm((BATCH, D_MODEL), 1.0),
        'ada_w': nrm((L, D_MODEL, 6 * D_MODEL), D_MODEL ** -0.5),
        'ada_b': nrm((L, 6 * D_MODEL), 0.02),
        'norm_mix_g': gain((L, D_MODEL)),
        'w_in': nrm((L, D_MODEL, IN_PROJ), D_MODEL ** -0.5),
        'conv_dw_w': nrm((L, CONV_WIDTH_2, CONV_CH), CONV_WIDTH_2 ** -0.5),
        'conv_dw_b': nrm((L, CONV_CH), 0.02),
        'conv_ln_w': gain((L, CONV_CH)),
        'conv_ln_b': nrm((L, CONV_CH), 0.02),
        'rwkv_mu': jax.random.uniform(next(ks), (L, RWKV_PROJ), jnp.float32),
        'rwkv_w0': jax.random.uniform(next(ks), (L, RWKV_CH), jnp.float32, -6.0, 1.0),
        'rwkv_w2': nrm((L, LORA_W, RWKV_CH), 0.5 * LORA_W ** -0.5),
        'rwkv_a0': nrm((L, RWKV_CH), 0.1),
        'rwkv_a2': nrm((L, LORA_A, RWKV_CH), 0.5 * LORA_A ** -0.5),
        'rwkv_g2': nrm((L, LORA_G, RWKV_CH), LORA_G ** -0.5),
        'rwkv_k_k': 0.85 + nrm((L, RWKV_CH), 0.02),
        'rwkv_k_a': gain((L, RWKV_CH)),
        'rwkv_r_k': nrm((L, RWKV_HEADS, RWKV_HEAD), 0.1),
        'rwkv_gn_w': gain((L, RWKV_CH)),
        'rwkv_gn_b': nrm((L, RWKV_CH), 0.02),
        'w_out': nrm((L, MIX_WIDTH, D_MODEL), MIX_WIDTH ** -0.5),
        'norm_ffn_g': gain((L, D_MODEL)),
        'peer_w_q': nrm((L, D_MODEL, PEER_HEADS * PEER_DQ), D_MODEL ** -0.5),
        'peer_sub_keys': nrm((L, PEER_HEADS, 2, PEER_NKEYS, PEER_DQ // 2), (PEER_DQ // 2) ** -0.5),
        'peer_u': nrm((L, PEER_EXPERTS, D_MODEL), D_MODEL ** -0.5),
        'peer_v': nrm((L, PEER_EXPERTS, D_MODEL), (PEER_HEADS * PEER_TOPK) ** -0.5),
        'final_g': gain((D_MODEL,)),
    }

def second_block(x, c, ada_w, ada_b, norm_mix_g, w_in, conv_dw_w, conv_dw_b, conv_ln_w, conv_ln_b,
              rwkv_mu, rwkv_w0, rwkv_w2, rwkv_a0, rwkv_a2, rwkv_g2, rwkv_k_k, rwkv_k_a, rwkv_r_k,
              rwkv_gn_w, rwkv_gn_b, w_out, norm_ffn_g, peer_w_q, peer_sub_keys, peer_u, peer_v, final_g):
    for l in range(DEPTH):
        mod = jax.nn.silu(c) @ ada_w[l] + ada_b[l]
        sh_mix, sc_mix, gt_mix, sh_ffn, sc_ffn, gt_ffn = jnp.split(mod, 6, axis=-1)

        u = modulate(rmsnorm_2(x, norm_mix_g[l]), sh_mix, sc_mix)
        p = u @ w_in[l]
        y_conv = conformer_conv(p[..., :2 * CONV_CH], conv_dw_w[l], conv_dw_b[l], conv_ln_w[l], conv_ln_b[l])
        y_rwkv = rwkv7_mix(p[..., 2 * CONV_CH:], rwkv_mu[l], rwkv_w0[l], rwkv_w2[l], rwkv_a0[l], rwkv_a2[l],
                           rwkv_g2[l], rwkv_k_k[l], rwkv_k_a[l], rwkv_r_k[l], rwkv_gn_w[l], rwkv_gn_b[l])
        mix = jnp.concatenate([y_conv, y_rwkv], axis=-1) @ w_out[l]
        x = x + gt_mix[:, None, :] * mix

        u = modulate(rmsnorm_2(x, norm_ffn_g[l]), sh_ffn, sc_ffn)
        x = x + gt_ffn[:, None, :] * peer_ffn(u, peer_w_q[l], peer_sub_keys[l], peer_u[l], peer_v[l])
    return rmsnorm_2(x, final_g)


def setup_inputs(seed=0):
    out = dict(first_inputs(seed))
    for name, value in second_inputs(seed + 1).items():
        if name != "x":
            out[name + "_2"] = value
    return out


def reference(
    x, norm_mix_g, w_in, b_gate, q_norm_g, k_norm_g, w_pool, pool_scale, w_branch_attn,
    w_branch_pool, w_out, norm_ffn_g, w_up, conv_w, conv_b, w_down, c_2, ada_w_2, ada_b_2,
    norm_mix_g_2, w_in_2, conv_dw_w_2, conv_dw_b_2, conv_ln_w_2, conv_ln_b_2, rwkv_mu_2,
    rwkv_w0_2, rwkv_w2_2, rwkv_a0_2, rwkv_a2_2, rwkv_g2_2, rwkv_k_k_2, rwkv_k_a_2, rwkv_r_k_2,
    rwkv_gn_w_2, rwkv_gn_b_2, w_out_2, norm_ffn_g_2, peer_w_q_2, peer_sub_keys_2, peer_u_2,
    peer_v_2, final_g_2,
):
    x = first_block(
        x, norm_mix_g, w_in, b_gate, q_norm_g, k_norm_g, w_pool, pool_scale, w_branch_attn,
        w_branch_pool, w_out, norm_ffn_g, w_up, conv_w, conv_b, w_down,
    )
    return second_block(
        x, c_2, ada_w_2, ada_b_2, norm_mix_g_2, w_in_2, conv_dw_w_2, conv_dw_b_2, conv_ln_w_2,
        conv_ln_b_2, rwkv_mu_2, rwkv_w0_2, rwkv_w2_2, rwkv_a0_2, rwkv_a2_2, rwkv_g2_2,
        rwkv_k_k_2, rwkv_k_a_2, rwkv_r_k_2, rwkv_gn_w_2, rwkv_gn_b_2, w_out_2, norm_ffn_g_2,
        peer_w_q_2, peer_sub_keys_2, peer_u_2, peer_v_2, final_g_2,
    )


_drawn_inputs = setup_inputs


def setup_inputs(seed=0):
    import zlib

    import numpy as np

    out = dict(_drawn_inputs(seed))
    spreads = {}
    factors = {'norm_mix_g': 4.576,
     'b_gate': 2.944,
     'q_norm_g': 8.0,
     'k_norm_g': 8.0,
     'norm_ffn_g': 3.805,
     'conv_b': 3.99,
     'ada_b_2': 3.942,
     'norm_mix_g_2': 7.234,
     'conv_dw_b_2': 64.0,
     'conv_ln_w_2': 64.0,
     'conv_ln_b_2': 64.0,
     'rwkv_w2_2': 35.688,
     'rwkv_a0_2': 5.326,
     'rwkv_k_k_2': 41.128,
     'rwkv_k_a_2': 5.36,
     'rwkv_gn_w_2': 64.0,
     'rwkv_gn_b_2': 64.0,
     'norm_ffn_g_2': 64.0,
     'final_g_2': 8.066,
     'conv_dw_w_2': 4.813,
     'rwkv_w0_2': 7.643,
     'peer_w_q_2': 8.0,
     'peer_sub_keys_2': 8.0,
     'peer_u_2': 8.0,
     'peer_v_2': 8.0}
    for name, (base, spread) in spreads.items():
        noise = np.random.default_rng([zlib.crc32(name.encode()), seed]).standard_normal(out[name].shape)
        drawn = base * np.exp(spread * noise) if base else spread * noise
        out[name] = __import__('jax').numpy.asarray(drawn.astype(out[name].dtype))
    for name, factor in factors.items():
        out[name] = (out[name] * factor).astype(out[name].dtype)
    return out
```

```python
from contextlib import ExitStack

import concourse.bass as bass
from concourse import mybir

F32 = mybir.dt.float32
F32R = mybir.dt.float32r
U32 = mybir.dt.uint32
ACT = mybir.ActivationFunctionType
ALU = mybir.AluOpType
AX = mybir.AxisListType.X

P = 128
TOK = 256
D = 1024
KT = D // P
CHUNK = 1024
RING = 4
AHEAD = 3
HEADS = 8
FF = 2816
NF = FF // P
TOPK = 16
NKEY = 128
LAMBDA = 0.6065306597126334

ADA = 6 * D // P
W_IN = 0
BRANCH = W_IN + 4096 // P
W_OUT = BRANCH + 8
FFN = W_OUT + KT
MIX = FFN + 4 * NF + 1
ADA_REST = MIX + 4 * (2816 // P // 2)
W_OUT2 = ADA_REST + 3
W_Q = W_OUT2 + KT
EXP_U = W_Q + 2048 // P
EXP_V = EXP_U + NKEY
CHUNKS = EXP_V + NKEY
ADA_FFN = NF + 1
assert ADA == ADA_FFN + 22 + 3 and W_OUT2 % RING == 0

VECTORS = [
    ("norm_mix_g", 8), ("b_gate", 16), ("q_norm_g", 1), ("k_norm_g", 1), ("pool_scale", 4),
    ("norm_ffn_g", 8), ("conv_w", 3 * 2 * NF), ("conv_b", 2 * NF), ("c_2", 8), ("ada_b_2", ADA),
    ("norm_mix_g_2", 8), ("conv_dw_w_2", 31 * 4), ("conv_dw_b_2", 4), ("conv_ln_w_2", 4),
    ("conv_ln_b_2", 4), ("rwkv_mu_2", 14), ("rwkv_w0_2", 4), ("rwkv_a0_2", 4), ("rwkv_k_k_2", 4),
    ("rwkv_k_a_2", 4), ("rwkv_r_k_2", 4), ("rwkv_gn_w_2", 4), ("rwkv_gn_b_2", 4),
    ("norm_ffn_g_2", 8), ("final_g_2", 8), ("eps", 3),
]
COL = {}
_at = 0
for _name, _n in VECTORS:
    COL[_name] = _at
    _at += _n
NVEC = _at

CONSTS = [
    ("ident", 128), ("ones", 128), ("iota", 128),
    ("head", 128), ("rot", 128), ("m16u", 128), ("m16l", 128), ("mel", 128), ("msu", 128),
    ("miu", 128), ("eye64", 64), ("cos", 256), ("sin", 256), ("inv_count", 1024), ("reset", 256),
    ("causal", 384),
]
CAT = {}
_at = 0
for _name, _n in CONSTS:
    CAT[_name] = _at
    _at += _n
NCONST = _at
KEPT = 384


GRAM = [
    (("B", "Z"), [("DU", "m16u")]),
    (("Z", "B"), [("DL", "m16l"), ("EL", "mel")]),
    (("K", "Z"), [("AK", "msu")]),
    (("B", "R"), [("RB", "miu")]),
    (("K", "R"), [("RK", "miu")]),
]
NEUMANN = [
    [("DL", "DU", "D2U", "act"), ("DU", "DL", "D2L", "act")],
    [("D2L", "R", "R", "add"), ("D2L", "D2U", "DU", "act")],
    [("D2U", "D2L", "DL", "act")],
    [("DL", "R", "R", "add"), ("DU", "DL", "D2L", "act")],
    [("D2L", "R", "R", "add")],
    [("R", "turn", "D2U", "act"), ("R", "EL", "DU", "copy")],
    [("EL", "R", "DL", "act"), ("EL", "R", "R", "eye")],
    [("DL", "DU", "EL", "act")],
    [("EL", "R", "DL", "add")],
    [("D2U", "DL", "R", "act")],
]


def count_products():
    prod, done, n, on_dve, on_act = {}, {}, 0, [0] * 4, [0] * 4
    dve = act = 0
    for s, step in enumerate(NEUMANN):
        for b in range(4):
            done[s, b] = on_dve[b], on_act[b]
        for b in range(4):
            for k, entry in enumerate(step):
                n += 1
                prod[s, b, k] = n
                if entry[3] == "act":
                    act += 1
                    on_act[b] = act
                else:
                    dve += 1
                    on_dve[b] = dve
    return prod, done


PROD, DONE = count_products()


class Chain:

    def __init__(self, eng, sem):
        self.eng, self.sem, self.n, self.i, self.per, self.n0 = eng, sem, 0, None, 0, 0

    def mark(self, ins):
        ins.then_inc(self.sem, 1)
        self.n += 1

    def wait(self):
        self.eng.wait_ge(self.sem, self.n if self.i is None else self.i * self.per + self.n)

    def after(self, ins):
        self.mark(ins)
        self.wait()

    def enter(self, i, per):
        self.i, self.per, self.n0 = i, per, self.n

    def leave(self, count):
        assert self.n - self.n0 == self.per, (self.n - self.n0, self.per)
        self.n = self.n0 + self.per * count
        self.i = None


def build(nc, ins, out):
    with ExitStack() as ctx:
        def sb(name, shape, dt=F32):
            return ctx.enter_context(nc.sbuf_tensor(name, shape, dt))

        sems = {}

        def sem(name):
            if name not in sems:
                sems[name] = ctx.enter_context(nc.semaphore(name))
            return sems[name]

        bank = [ctx.enter_context(nc.psum_tensor(f"bank{b}", [P, 512], F32)) for b in range(8)]

        raw = sb("raw", [P, RING, CHUNK])
        w_hi = sb("w_hi", [P, RING, CHUNK], F32R)
        w_lo = sb("w_lo", [P, RING, CHUNK], F32R)
        x_hi = sb("x_hi", [P, KT, TOK], F32R)
        x_lo = sb("x_lo", [P, KT, TOK], F32R)
        f_hi = sb("f_hi", [P, TOK], F32R)
        f_lo = sb("f_lo", [P, TOK], F32R)
        c_hi = sb("c_hi", [P, KT, 2], F32R)
        c_lo = sb("c_lo", [P, KT, 2], F32R)
        xres = sb("xres", [P, KT, TOK])
        vec = sb("vec", [P, NVEC])
        mod = sb("mod", [P, ADA])
        gain = sb("gain", [P, KT])
        gain2 = sb("gain2", [P, 4])
        csil = sb("csil", [P, KT])
        kept = sb("kept", [P, KEPT])
        arena = sb("arena", [P, 32768])
        i0T = sb("i0T", [P, TOK])

        def V(name, n=1, at=0):
            return vec[:, COL[name] + at:COL[name] + at + n]

        ident = kept[:, 0:128]
        ones = kept[:, 128:256]
        iota = kept[:, 256:384]

        def C(name, n=None):
            a = CAT[name] - KEPT
            return arena[:, a:a + (n or dict(CONSTS)[name])]

        class Arena:
            def __init__(self, at, end=32768):
                self.at, self.end = at, end

            def __call__(self, n):
                a = self.at
                self.at += n
                assert self.at <= self.end, (self.at, self.end)
                return arena[:, a:a + n]

        def tiles(ap, n, w=TOK):
            return ap.rearrange("p (n t) -> p n t", n=n, t=w)

        A = Arena(NCONST - KEPT)
        qkv = tiles(A(12 * TOK), 12)
        upool = tiles(A(4 * 272), 4, 272)
        gates = tiles(A(16 * TOK), 16)
        sq = tiles(A(8 * TOK), 8)
        rs = tiles(A(8 * TOK), 8)
        rt = tiles(A(8 * TOK), 8)
        v_tok = tiles(A(2 * 512), 2, 512)
        wpool = tiles(A(512), 4, 128)
        sm = tiles(A(2 * 384), 2, 384)
        pex = tiles(A(2 * 384), 2, 384)
        pT = tiles(A(2 * 384), 2, 384)
        pw1 = tiles(A(4 * 272), 4, 272)
        pw2 = tiles(A(4 * 272), 4, 272)
        mixed = tiles(A(8 * TOK), 8)
        mixb = tiles(A(8 * TOK), 8)
        stats = A(16)
        rstd = A(TOK)
        upad = tiles(A(2 * 258), 2, 258)
        cv = tiles(A(2 * TOK), 2)
        sil = A(TOK)
        fa = A(TOK)

        xT, packed, consts, lora, wpool_d, keys_d = (ins[k] for k in ("xT", "vec", "consts", "lora", "w_pool", "keys"))

        B = Arena(NCONST - KEPT)
        pb = tiles(B(14 * 257), 14, 257)
        sgb = tiles(B(4 * TOK), 4)
        cy = tiles(B(4 * 286), 4, 286)
        co = tiles(B(4 * TOK), 4)
        xs = tiles(B(14 * TOK), 14)
        sw = tiles(B(4 * TOK), 4)
        cum = tiles(B(4 * TOK), 4)
        aa = tiles(B(4 * TOK), 4)
        kk = tiles(B(4 * TOK), 4)
        e2 = tiles(B(4 * TOK), 4)
        zf = tiles(B(4 * TOK), 4)
        bf = tiles(B(4 * TOK), 4)
        kf = tiles(B(4 * TOK), 4)
        gg = tiles(B(4 * TOK), 4)
        e1 = tiles(B(4 * TOK), 4)
        rf = tiles(B(4 * TOK), 4)
        bon = tiles(B(4 * TOK), 4)
        zt, bt, kt_, vt = (tiles(B(2 * 512), 2, 512) for _ in range(4))
        lora_sb = B(1024)
        rstd2 = B(TOK)
        U = Arena(NCONST - KEPT, NCONST - KEPT + 18600)

        def unit():
            return U(2048).rearrange("p (b h s) -> p b h s", b=4, h=4)

        AK, RB, RK, EL, R_, DU, DL, D2U, D2L = (unit() for _ in range(9))
        MAT = dict(EL=EL, R=R_, DU=DU, DL=DL, D2U=D2U, D2L=D2L)
        W = Arena(NCONST - KEPT + 3 * 2048, NCONST - KEPT + 4 * 2048)
        m1 = tiles(W(1024), 2, 512)
        m2 = tiles(W(1024), 2, 512)
        W = Arena(NCONST - KEPT + 5 * 2048, NCONST - KEPT + 9 * 2048)
        m1T = tiles(W(1024), 4)
        w1 = tiles(W(1024), 2, 512)
        phi = W(1024).rearrange("p (c f j) -> p c f j", c=4, f=4)
        u0 = W(1024).rearrange("p (c f j) -> p c f j", c=4, f=4)
        st = W(1024).rearrange("p (c f j) -> p c f j", c=4, f=4)
        sa = tiles(W(1024), 2, 512)
        yy = tiles(W(1024), 4)
        ysq = tiles(W(1024), 4)

        hbuf = arena
        K = Arena(32768 - 14336)
        s_sb = K(4096).rearrange("p (a b k) -> p a b k", a=2, b=16)
        cand_flat = K(4096)
        cand = cand_flat.rearrange("p (a h k) -> p a h k", a=2, h=8)
        qT = tiles(cand_flat, 16)
        keys_flat = K(2048)
        keys = tiles(keys_flat, 16, 128)
        onehot = keys_flat.rearrange("p (h k j) -> p h k j", h=8, k=16)
        vals = K(512).rearrange("p (a b k) -> p a b k", a=2, b=16)
        idx = K(512).rearrange("p (a b k) -> p a b k", a=2, b=16)
        idf = K(512).rearrange("p (a b k) -> p a b k", a=2, b=16)
        best = K(256).rearrange("p (a h k) -> p a h k", a=2, h=8)
        pos = K(256).rearrange("p (a h k) -> p a h k", a=2, h=8)
        poshl = K(512).rearrange("p (c a h k) -> p c a h k", c=2, a=2, h=8)
        poshu = K(512).rearrange("p (c a h k) -> p c a h k", c=2, a=2, h=8)
        isel = K(512).rearrange("p (c a h k) -> p c a h k", c=2, a=2, h=8)
        gate = K(256).rearrange("p (a h k) -> p a h k", a=2, h=8)
        gsum = K(16).rearrange("p (a h) -> p a h", a=2)
        TOP_FIRST = (32768 - 14336) // TOK
        hot = xres[:].rearrange("p a b -> p (a b)").rearrange("p (b k s) -> p b k s", b=4, k=4)
        hotA, hotB = hot[:, 0:2], hot[:, 2:4]

        x_flat = xres[:].rearrange("p a b -> p (a b)")
        spill = ins["spill"]

        S = sem
        landed = [S(f"landed{s}") for s in range(RING)]
        hi_ready, lo_ready, chunk_used = S("hi_ready"), S("lo_ready"), S("chunk_used")

        block = ctx.enter_context(nc.Block())

        @block.sync
        def _(sp):
            def load(b, src, n, i=0):
                if b >= RING:
                    sp.wait_ge(lo_ready, b - RING + 1 + 4 * i)
                if isinstance(n, int):
                    src = src[n]
                else:
                    src = src[bass.ds(n, 1)].rearrange("a p n -> p (a n)")
                sp.dma_start(raw[:, b % RING], src).then_inc(landed[b % RING], 16)

            def load_all(b, src, n0, count):
                assert count % RING == 0
                with sp.Fori(0, count // RING) as i:
                    for p in range(RING):
                        load(b + p, src, 4 * i + (n0 + p), i)

            sp.dma_start(x_flat, xT).then_inc(S("x_landed"), 16)
            for j in range(RING):
                load(W_IN + j, ins["w_in"], j)
            load_all(W_IN + RING, ins["w_in"], RING, 32 - RING)
            load_all(BRANCH, ins["w_branch"], 0, 8)
            load_all(W_OUT, ins["w_out"], 0, KT)
            up, ada, down = ins["w_up"], ins["ada"], ins["w_down"]
            load(FFN, up, 0)
            load(FFN + 1, up, 1)
            load(FFN + 2, ada, 0)
            load(FFN + 3, ada, NF)
            with sp.Fori(0, NF - 1) as i:
                load(FFN + 4, up, 2 * i + 2, i)
                load(FFN + 5, up, 2 * i + 3, i)
                load(FFN + 6, ada, i + 1, i)
                load(FFN + 7, down, i, i)
            load(MIX - 1, down, NF - 1)
            with sp.Fori(0, 11) as i:
                load(MIX, ins["w_in2"], 2 * i, i)
                load(MIX + 1, ada, 2 * i + ADA_FFN, i)
                load(MIX + 2, ins["w_in2"], 2 * i + 1, i)
                load(MIX + 3, ada, 2 * i + (ADA_FFN + 1), i)
            for n in range(3):
                load(ADA_REST + n, ada, ADA_FFN + 22 + n)
            load_all(W_OUT2, ins["w_out2"], 0, KT)
            load_all(W_Q, ins["w_q"], 0, 16)
            load_all(EXP_U, ins["u"], 0, NKEY)
            load_all(EXP_V, ins["v"], 0, NKEY)
            sp.wait_ge(S("out_ready"), 1)
            sp.dma_start(out, arena[:, 0:2048]).then_inc(S("out_stored"), 16)
            sp.wait_ge(S("out_stored"), 16)

        @block.scalar
        def _(act):
            own = Chain(act, S("act_step"))

            def split(b, i=0):
                if b >= CHUNKS:
                    return
                s = b % RING
                act.wait_ge(landed[s], 16 * (b // RING + 1) + 16 * i)
                if b >= RING:
                    act.wait_ge(chunk_used, b - RING + 1 + 4 * i)
                act.activation(w_hi[:, s], raw[:, s], ACT.Copy).then_inc(hi_ready, 1)

            def splits(b, count):
                assert count % RING == 0
                with act.Fori(0, count // RING) as i:
                    for p in range(RING):
                        split(b + p + AHEAD, i)

            def norm(n, shift=None):
                for k in range(KT):
                    act.activation(sq_[:, k], xres[:, k], ACT.Square).then_inc(S("norm_sq"), 1)
                act.wait_ge(S("norm_ssq"), n + 1)
                act.activation(rstd_[:, :], bank[7][:, 0:TOK], ACT.Sqrt, bias=V("eps"), scale=1.0 / D)\
                   .then_inc(S("norm_std"), 1)
                for k in range(KT):
                    act.wait_ge(S("norm_y"), KT * n + k + 1)
                    if shift is None:
                        act.activation(x_hi[:, k], y_[:, k], ACT.Copy).then_inc(S("norm_hi"), 1)
                    else:
                        act.activation(x_hi[:, k], y_[:, k], ACT.Identity, bias=shift[:, k:k + 1])\
                           .then_inc(S("norm_hi"), 1)

            act.dma_start(vec[:, :], packed).then_inc(S("vec_landed"), 16)
            act.dma_start(kept[:, :], consts[:, 0:KEPT]).then_inc(S("kept_landed"), 16)
            act.dma_start(arena[:, 0:NCONST - KEPT], consts[:, KEPT:NCONST]).then_inc(S("consts_landed"), 16)
            act.dma_start(wpool[:, :, :].rearrange("p a b -> p (a b)"), wpool_d).then_inc(S("wpool_landed"), 16)

            act.wait_ge(S("x_landed"), 16)
            act.wait_ge(S("vec_landed"), 16)
            sq_, rstd_, y_ = sq, rstd, mixed
            norm(0)
            for j in range(AHEAD):
                split(j)
            act.activation(csil[:, :], V("c_2", 8), ACT.Silu).then_inc(S("csil"), 1)
            act.wait_ge(S("csil"), 1)
            for c in range(2):
                act.activation(c_hi[:, :, c], csil[:, :], ACT.Copy).then_inc(S("c_hi"), 1)

            def taken(b, dst, i=0, func=ACT.Copy, **kw):
                act.wait_ge(chunk_used, b + 1 + 4 * i)
                act.activation(dst, bank[b % RING][:, 0:TOK], func, **kw).then_inc(S("tile_taken"), 1)

            for j in range(4):
                split(j + AHEAD)
                taken(j, qkv[:, j])
            with act.Fori(0, 2) as i:
                for p in range(4):
                    split(4 + p + AHEAD, i)
                    taken(4 + p, arena[:, bass.ds(i * 1024 + (NCONST - KEPT + (4 + p) * TOK), TOK)], i)
            act.wait_ge(S("upad_zero"), 1)
            for j in range(12, 16):
                split(j + AHEAD)
                taken(j, upool[:, j - 12, 16:272])
            for j in range(16, 32):
                split(j + AHEAD)
                taken(j, gates[:, j - 16], func=ACT.Sigmoid, bias=V("b_gate", 1, j - 16))

            for h in range(4):
                act.activation(sq[:, 2 * h:2 * h + 2], qkv[:, 2 * h:2 * h + 2], ACT.Square).then_inc(S("qk_sq"), 1)
            for h in range(4):
                act.wait_ge(S("qk_ssq"), h + 1)
                act.activation(rs[:, 2 * h:2 * h + 2].rearrange("p a b -> p (a b)"), bank[4 + h][:, :], ACT.Sqrt,
                               bias=V("eps"), scale=1.0 / 64).then_inc(S("qk_std"), 1)
            for t in range(2):
                act.wait_ge(S("v_turned"), t + 1)
                act.activation(v_tok[:, t], bank[t][:, :], ACT.Copy).then_inc(S("v_tok"), 1)
            for h in range(HEADS):
                b = h % 2
                act.wait_ge(S("neg_max"), h + 1)
                if h >= 2:
                    act.wait_ge(S("p_turned"), h - 1)
                act.activation(pex[:, b, 0:128], sm[:, b, 0:128], ACT.Exp, bias=stats[:, 4 * b:4 * b + 1],
                               accum_out=stats[:, 4 * b + 2:4 * b + 3]).then_inc(S("p_exp"), 1)
                act.activation(pex[:, b, 128:384], sm[:, b, 128:384], ACT.Exp, bias=stats[:, 4 * b + 1:4 * b + 2],
                               accum_out=stats[:, 4 * b + 3:4 * b + 4]).then_inc(S("p_exp"), 1)
                act.wait_ge(S("p_turned"), h + 1)
                if h >= 2:
                    act.wait_ge(S("head_out"), h - 1)
                act.activation(pT[:, b], bank[2 + b][:, 0:384], ACT.Copy).then_inc(S("pT"), 1)
            for f in range(4):
                act.wait_ge(S("head_out"), 4 * (f // 2) + 4)
                if f == 0:
                    act.wait_ge(chunk_used, 32)
                act.activation(x_hi[:, f], bank[4 + f // 2][:, (f % 2) * TOK:(f % 2) * TOK + TOK], ACT.Copy)\
                   .then_inc(S("attn_hi"), 1)
            for g in range(4):
                act.wait_ge(S("pool_mixed"), 1)
                act.activation(x_hi[:, 4 + g], bank[6 + g // 2][:, (g % 2) * TOK:(g % 2) * TOK + TOK], ACT.Copy,
                               scale=V("pool_scale", 1, g)).then_inc(S("attn_hi"), 1)
            splits(BRANCH, 8)
            for k in range(KT):
                act.wait_ge(S("mixed"), k // 2 + 1)
                if k == 0:
                    act.wait_ge(chunk_used, BRANCH + 8)
                act.activation(x_hi[:, k], mixed[:, k], ACT.Copy).then_inc(S("mixed_hi"), 1)
            splits(W_OUT, 8)
            act.wait_ge(S("x_added"), KT)
            norm(1)
            act.wait_ge(S("ffn_pad"), 1)

            def ffn_step(b, i=0, last=False):
                n = i
                split(b + AHEAD, i)
                for h in range(2):
                    if h == 1:
                        split(b + 1 + AHEAD, i)
                    act.wait_ge(chunk_used, b + h + 1 + 4 * i)
                    if not (isinstance(i, int) and b == FFN):
                        act.wait_ge(S("conv_done"), 2 * ((b - FFN) // 4 - 1) + h + 1 + 2 * i)
                    act.activation(upad[:, h, 2:258], bank[h][:, 0:TOK], ACT.Copy).then_inc(S("up_taken"), 1)
                split(b + 2 + AHEAD, i)
                q = (b - FFN) // 4
                act.wait_ge(S("conv_done"), 2 * q + 1 + 2 * i)
                if not (isinstance(i, int) and b == FFN):
                    act.wait_ge(S("ffn_act"), q + i)
                act.activation(sil, cv[:, 0], ACT.Silu).then_inc(S("silu"), 1)
                act.wait_ge(S("ffn_act"), q + 1 + i)
                if not (isinstance(i, int) and b == FFN):
                    act.wait_ge(chunk_used, b + 4 + 4 * i)
                act.activation(f_hi[:, :], fa, ACT.Copy).then_inc(S("ffn_hi"), 1)
                split(b + 3 + AHEAD, i)

            ffn_step(FFN)
            with act.Fori(0, NF - 1) as i:
                ffn_step(FFN + 4, i)
            split(MIX - 1 + AHEAD)
            act.wait_ge(S("x_ffn"), 4)
            act.wait_ge(S("gain"), 1)
            sq_, rstd_, y_ = tiles(arena[:, 8000:8000 + 2048], 8), rstd2, tiles(arena[:, 10048:10048 + 2048], 8)
            norm(2, mod[:, 0:8])
            act.dma_start(lora_sb, lora).then_inc(S("lora_landed"), 16)
            act.wait_ge(S("pads2"), 2)

            def mix_taken(b, dst, h, i=0, **kw):
                split(b + AHEAD, i)
                act.wait_ge(chunk_used, b + 1 + 4 * i)
                act.activation(dst, bank[h][:, 0:TOK], kw.pop("func", ACT.Copy), **kw).then_inc(S("mix_taken"), 1)
                split(b + 1 + AHEAD, i)

            with act.Fori(0, 7) as i:
                for h in range(2):
                    mix_taken(MIX + 2 * h, arena[:, bass.ds(i * 514 + (NCONST - KEPT + 257 * h + 1), TOK)], h, i)
            for n in range(4):
                mix_taken(MIX + 28 + 2 * n, sgb[:, n], n % 2, func=ACT.Sigmoid)
            for n in range(4):
                split(MIX + 36 + 2 * n + AHEAD)
                split(MIX + 36 + 2 * n + 1 + AHEAD)
            for n in range(3):
                split(ADA_REST + n + AHEAD)
            act.wait_ge(S("shifted"), 2)
            act.activation(xs[0:64, 0], xs[0:64, 0], ACT.Tanh).then_inc(S("lora_in"), 1)
            act.activation(xs[:, 1], xs[:, 1], ACT.Sigmoid).then_inc(S("lora_in"), 1)
            for f in range(4):
                act.wait_ge(S("lora_out"), 1)
                half = slice((f % 2) * TOK, (f % 2) * TOK + TOK)
                act.activation(sw[:, f], bank[f // 2][:, half], ACT.Sigmoid, bias=V("rwkv_w0_2", 1, f)).then_inc(S("decay"), 1)
            for f in range(4):
                half = slice((f % 2) * TOK, (f % 2) * TOK + TOK)
                act.activation(aa[:, f], bank[2 + f // 2][:, half], ACT.Sigmoid, bias=V("rwkv_a0_2", 1, f)).then_inc(S("rate"), 1)
            act.wait_ge(S("lora_out"), 2)
            for f in range(2):
                act.activation(gg[:, 2 * f:2 * f + 2].rearrange("p a b -> p (a b)"), bank[4 + f][:, :], ACT.Copy).then_inc(S("g_out"), 1)
            act.wait_ge(S("kk"), 4)
            act.activation(rf[:, :, :], kk[:, :, :], ACT.Square).then_inc(S("kk_sq"), 1)
            for f in range(2):
                act.wait_ge(S("kk_ssq"), f + 1)
                act.activation(rf[:, 2 * f:2 * f + 2].rearrange("p a b -> p (a b)"), bank[6 + f][:, :], ACT.Sqrt).then_inc(S("kk_norm"), 1)
            act.wait_ge(S("cum"), 4)
            act.activation(e1[:, :, :], cum[:, :, :], ACT.Exp, scale=-LAMBDA).then_inc(S("e1"), 1)
            act.activation(e2[:, :, :], cum[:, :, :], ACT.Exp, scale=LAMBDA).then_inc(S("e2"), 1)
            act.wait_ge(S("cum"), 5)
            act.activation(sw[:, :, :], sw[:, :, :], ACT.Exp, scale=-LAMBDA).then_inc(S("e3"), 1)
            for n in range(8):
                act.wait_ge(S("turned"), n + 1)
                dst = (zt, bt, kt_, vt)[n // 2]
                act.activation(dst[:, n % 2], bank[n][:, :], ACT.Copy).then_inc(S("tok_major"), 1)
            act.wait_ge(S("ln_centred"), 4)
            for f in range(4):
                act.activation(cy[:, f, 0:TOK], co[:, f], ACT.Square).then_inc(S("ln_sq"), 1)
            act.wait_ge(S("ln_var"), 1)
            act.activation(rstd2, bank[7][:, 0:TOK], ACT.Sqrt, bias=V("eps", 1, 2), scale=1.0 / 512).then_inc(S("ln_std"), 1)
            for f in range(4):
                act.wait_ge(S("ln_y"), f + 1)
                act.activation(co[:, f], co[:, f], ACT.Silu, scale=V("conv_ln_w_2", 1, f), bias=V("conv_ln_b_2", 1, f))\
                   .then_inc(S("conv_silu"), 1)
                act.wait_ge(S("conv_silu"), f + 1)
                act.activation(x_hi[:, f], co[:, f], ACT.Copy).then_inc(S("mix_hi"), 1)
            n = 0
            for s, step in enumerate(NEUMANN):
                for b in range(4):
                    for k, (lhs, rhs, dst, how) in enumerate(step):
                        if how != "act":
                            continue
                        act.wait_ge(S("neu_prod"), PROD[s, b, k])
                        act.activation(MAT[dst][:, b].rearrange("p a b -> p (a b)"), bank[2 * b + k][:, :], ACT.Copy)\
                           .then_inc(S("neu_act"), 1)
            for t in range(2):
                act.wait_ge(S("m1T_prod"), t + 1)
                act.activation(m1T[:, :, t * 128:t * 128 + 128], bank[2 + t][:, :].rearrange("p (f s) -> p f s", f=4), ACT.Copy)\
                   .then_inc(S("m1T"), 1)
            for t in range(2):
                act.wait_ge(S("m2_prod"), t + 1)
                act.activation(m2[:, t], bank[6 + t][:, :], ACT.Copy).then_inc(S("m2"), 1)
            for f in range(2):
                act.wait_ge(S("y_prod"), 1)
                act.activation(yy[:, 2 * f:2 * f + 2].rearrange("p a b -> p (a b)"), bank[f][:, :], ACT.Copy).then_inc(S("y_out"), 1)
            act.wait_ge(S("y_centred"), 2)
            act.activation(ysq[:, :, :], yy[:, :, :], ACT.Square).then_inc(S("y_sq"), 1)
            for f in range(2):
                act.wait_ge(S("y_var"), f + 1)
                act.activation(ysq[:, 2 * f:2 * f + 2].rearrange("p a b -> p (a b)"), bank[4 + f][:, :], ACT.Sqrt,
                               bias=V("eps", 1, 1), scale=1.0 / 64).then_inc(S("y_std"), 1)
            act.wait_ge(S("y_done"), 1)
            for f in range(4):
                act.activation(x_hi[:, 4 + f], yy[:, f], ACT.Copy).then_inc(S("mix_hi"), 1)
            splits(W_OUT2, 8)
            act.wait_ge(S("x_mixed2"), KT)
            norm(3, mod[:, 24:32])
            act.dma_start(spill, x_flat).then_inc(S("spilled"), 16)
            act.dma_start(keys_flat, keys_d).then_inc(S("keys_landed"), 16)
            for j in range(16):
                split(W_Q + j + AHEAD)
                act.wait_ge(chunk_used, W_Q + j + 1)
                act.activation(qT[:, j], bank[j % 4][:, 0:TOK], ACT.Copy).then_inc(S("q_taken"), 1)
            for n in range(8):
                act.wait_ge(S("scored"), n + 1)
                act.activation(s_sb[:, n // 4, 4 * (n % 4):4 * (n % 4) + 4].rearrange("p a b -> p (a b)"), bank[n][:, :], ACT.Copy)\
                   .then_inc(S("scores"), 1)
            def h_step(b, i=0):
                split(b + AHEAD, i)
                act.wait_ge(chunk_used, b + 1 + 4 * i)
                at = (b - EXP_U) * TOK
                dst = arena[:, at:at + TOK] if isinstance(i, int) else arena[:, bass.ds(i * 1024 + at, TOK)]
                act.activation(dst, bank[b % RING][:, 0:TOK], ACT.Gelu).then_inc(S("h_taken"), 1)

            with act.Fori(0, TOP_FIRST // 4) as i:
                for p in range(4):
                    h_step(EXP_U + p, i)
            act.wait_ge(S("best_shifted"), 1)
            act.activation(gate[:, :, :, :], gate[:, :, :, :], ACT.Exp).then_inc(S("gate_exp"), 1)
            act.wait_ge(S("routing_turned"), 1)
            with act.Fori(0, (NKEY - TOP_FIRST) // 4) as i:
                for p in range(4):
                    h_step(EXP_U + TOP_FIRST + p, i)
            def hots(b, i=0):
                act.wait_ge(S("hot_diff"), b + 1 + 2 * i)
                act.activation(hotA[:, b % 2], hotA[:, b % 2], ACT.Square).then_inc(S("hot_sq"), 1)
                act.wait_ge(S("hot_sq"), b + 1 + 2 * i)
                act.activation(hotA[:, b % 2], hotA[:, b % 2], ACT.Relu, scale=-1.0, bias=1.0).then_inc(S("hotA"), 1)

            with act.Fori(0, 32) as i:
                for b in range(2):
                    hots(b, i)
            def v_hi(n, i=0):
                at = n * TOK
                src = arena[:, at:at + TOK] if isinstance(i, int) else arena[:, bass.ds(i * 1024 + at, TOK)]
                act.wait_ge(chunk_used, EXP_V + n - 3 + 4 * i)
                act.activation(x_hi[:, n % 4], src, ACT.Copy).then_inc(S("g_hi"), 1)

            act.wait_ge(S("g_mixed"), 64)
            act.dma_start(x_flat, spill).then_inc(S("x_back"), 16)
            for n in range(3):
                v_hi(n)
            with act.Fori(0, NKEY // 4 - 1) as i:
                for p in range(4):
                    split(EXP_V + p + AHEAD, i)
                    v_hi(p + 3, i)
            for p in range(4):
                n = NKEY - 4 + p
                split(EXP_V + n + AHEAD)
                if n + 3 < NKEY:
                    v_hi(n + 3)
            for k in range(KT):
                act.wait_ge(S("x_final"), k + 1)
                act.activation(arena[:, 2048 + k * TOK:2304 + k * TOK], xres[:, k], ACT.Square).then_inc(S("norm_sq"), 1)
            act.wait_ge(S("norm_ssq"), 5)
            act.activation(arena[:, 4096:4096 + TOK], bank[0][:, 0:TOK], ACT.Sqrt, bias=V("eps"), scale=1.0 / D)\
               .then_inc(S("norm_std"), 1)

        @block.vector
        def _(dve):
            own = Chain(dve, S("dve_step"))

            def split(b, i=0):
                if b >= CHUNKS:
                    return
                s = b % RING
                dve.wait_ge(hi_ready, b + 1 + 4 * i)
                if b >= RING:
                    dve.wait_ge(chunk_used, b - RING + 1 + 4 * i)
                dve.tensor_tensor(w_lo[:, s], raw[:, s], w_hi[:, s].bitcast(F32), ALU.subtract).then_inc(lo_ready, 1)

            def splits(b, count):
                assert count % RING == 0
                with dve.Fori(0, count // RING) as i:
                    for p in range(RING):
                        split(b + p + AHEAD, i)

            def norm(n, g, shift=None):
                dve.wait_ge(S("norm_std"), n + 1)
                own.after(dve.reciprocal(rstd_, rstd_))
                for k in range(KT):
                    dve.scalar_tensor_tensor(y_[:, k], xres[:, k], g[:, k:k + 1], rstd_, ALU.mult, ALU.mult)\
                       .then_inc(S("norm_y"), 1)
                for k in range(KT):
                    dve.wait_ge(S("norm_hi"), KT * n + k + 1)
                    if shift is None:
                        dve.tensor_tensor(x_lo[:, k], y_[:, k], x_hi[:, k].bitcast(F32), ALU.subtract)\
                           .then_inc(S("norm_lo"), 1)
                    else:
                        dve.scalar_tensor_tensor(x_lo[:, k], y_[:, k], shift[:, k:k + 1], x_hi[:, k].bitcast(F32),
                                                 ALU.add, ALU.subtract).then_inc(S("norm_lo"), 1)

            dve.memset(upool[:, :, 0:16], 0.0).then_inc(S("upad_zero"), 1)
            sq_, rstd_, y_ = sq, rstd, mixed
            norm(0, V("norm_mix_g", 8))
            for j in range(AHEAD):
                split(j)
            for c in range(2):
                dve.wait_ge(S("c_hi"), c + 1)
                dve.tensor_tensor(c_lo[:, :, c], csil[:, :], c_hi[:, :, c].bitcast(F32), ALU.subtract).then_inc(S("c_lo"), 1)
            for j in range(4):
                split(j + AHEAD)
            splits(4, 28)
            dve.wait_ge(S("consts_landed"), 16)
            for h in range(2):
                dve.wait_ge(S("qk_std"), 2 * h + 2)
                v = slice(4 * h, 4 * h + 4)
                own.after(dve.reciprocal(rs[:, v], rs[:, v]))
                dve.scalar_tensor_tensor(rs[:, v], qkv[:, v], V(("q_norm_g", "k_norm_g")[h]), rs[:, v], ALU.mult, ALU.mult)\
                   .then_inc(S("qk_normed"), 1)
            cosb = C("cos").rearrange("p (a t) -> p a t", a=1)
            sinb = C("sin").rearrange("p (a t) -> p a t", a=1)
            for h in range(4):
                v = slice(2 * h, 2 * h + 2)
                dve.wait_ge(S("qk_turned"), h + 1)
                own.mark(dve.tensor_tensor(rt[:, v], bank[4 + h][:, :].rearrange("p (a t) -> p a t", a=2),
                                           sinb.broadcast_to([P, 2, TOK]), ALU.mult))
                own.after(dve.tensor_tensor(qkv[:, v], rs[:, v], cosb.broadcast_to([P, 2, TOK]), ALU.mult))
                dve.tensor_tensor(qkv[:, v], qkv[:, v], rt[:, v], ALU.add).then_inc(S("qk_rotated"), 1)
            def scores(h):
                b = h % 2
                dve.wait_ge(S("qk_scored"), h + 1)
                if h >= 2:
                    dve.wait_ge(S("p_exp"), 2 * (h - 1))
                own.after(dve.scalar_tensor_tensor(sm[:, b], bank[b][:, 0:384], 0.125, C("causal"), ALU.mult, ALU.add))
                own.mark(dve.tensor_reduce(stats[:, 4 * b:4 * b + 1], sm[:, b, 0:128], AX, ALU.max))
                own.after(dve.tensor_reduce(stats[:, 4 * b + 1:4 * b + 2], sm[:, b, 128:384], AX, ALU.max))
                dve.tensor_scalar(stats[:, 4 * b:4 * b + 2], stats[:, 4 * b:4 * b + 2], -1.0, None, ALU.mult)\
                   .then_inc(S("neg_max"), 1)

            def rows(h):
                b = h % 2
                dve.wait_ge(S("p_exp"), 2 * h + 2)
                own.after(dve.reciprocal(stats[:, 8 + 2 * b:10 + 2 * b], stats[:, 4 * b + 2:4 * b + 4]))
                own.mark(dve.tensor_scalar(pex[:, b, 0:128], pex[:, b, 0:128], stats[:, 8 + 2 * b:9 + 2 * b], None, ALU.mult))
                dve.tensor_scalar(pex[:, b, 128:384], pex[:, b, 128:384], stats[:, 9 + 2 * b:10 + 2 * b], None, ALU.mult)\
                   .then_inc(S("p_rows"), 1)

            scores(0)
            for h in range(HEADS):
                if h + 1 < HEADS:
                    scores(h + 1)
                rows(h)
            for f in range(4):
                dve.wait_ge(S("attn_hi"), 2 * (f // 2) + 2)
                dve.tensor_tensor(x_lo[:, f], bank[4 + f // 2][:, (f % 2) * TOK:(f % 2) * TOK + TOK], x_hi[:, f].bitcast(F32),
                                  ALU.subtract).then_inc(S("attn_lo"), 1)
            for g in range(4):
                dve.wait_ge(S("attn_hi"), 6 + 2 * (g // 2))
                dve.scalar_tensor_tensor(x_lo[:, 4 + g], bank[6 + g // 2][:, (g % 2) * TOK:(g % 2) * TOK + TOK],
                                         V("pool_scale", 1, g), x_hi[:, 4 + g].bitcast(F32), ALU.mult, ALU.subtract)\
                   .then_inc(S("attn_lo"), 1)
            splits(BRANCH, 4)
            dve.wait_ge(chunk_used, BRANCH + 4)
            for n in range(4):
                v = slice(2 * n, 2 * n + 2)
                own.mark(dve.tensor_tensor(mixed[:, v], bank[n][:, :].rearrange("p (a t) -> p a t", a=2), gates[:, v], ALU.mult))
            splits(BRANCH + 4, 4)
            dve.wait_ge(chunk_used, BRANCH + 8)
            for n in range(4):
                v = slice(2 * n, 2 * n + 2)
                w = slice(8 + 2 * n, 10 + 2 * n)
                own.after(dve.tensor_tensor(mixb[:, v], bank[4 + n][:, :].rearrange("p (a t) -> p a t", a=2), gates[:, w], ALU.mult))
                dve.tensor_tensor(mixed[:, v], mixed[:, v], mixb[:, v], ALU.add).then_inc(S("mixed"), 1)
            dve.wait_ge(S("mixed"), 4)
            for k in range(KT):
                dve.wait_ge(S("mixed_hi"), k + 1)
                dve.tensor_tensor(x_lo[:, k], mixed[:, k], x_hi[:, k].bitcast(F32), ALU.subtract).then_inc(S("mixed_lo"), 1)
            for k in range(KT):
                split(W_OUT + k + AHEAD)
                dve.wait_ge(chunk_used, W_OUT + k + 1)
                dve.tensor_tensor(xres[:, k], bank[k % 4][:, 0:TOK], xres[:, k], ALU.add).then_inc(S("x_added"), 1)
            dve.memset(upad[:, :, 0:2], 0.0).then_inc(S("ffn_pad"), 1)
            dve.wait_ge(S("x_added"), KT)
            norm(1, V("norm_ffn_g", 8))

            def ffn_step(b, i=0):
                q = (b - FFN) // 4
                first = isinstance(i, int) and b == FFN
                for h in range(2):
                    split(b + h + AHEAD, i)
                    dve.wait_ge(S("up_taken"), 2 * q + h + 1 + 2 * i)
                    if h == 0 and not first:
                        dve.wait_ge(S("silu"), q + i)
                    def col(t):
                        base = COL["conv_w"] + (2 * q + h) * 3 + t
                        return vec[:, base:base + 1] if isinstance(i, int) else vec[:, bass.ds(i * 6 + base, 1)]
                    cb = COL["conv_b"] + 2 * q + h
                    bias = vec[:, cb:cb + 1] if isinstance(i, int) else vec[:, bass.ds(i * 2 + cb, 1)]
                    own.after(dve.tensor_scalar(cv[:, h], upad[:, h, 2:258], col(2), bias, ALU.mult, ALU.add))
                    own.after(dve.scalar_tensor_tensor(cv[:, h], upad[:, h, 1:257], col(1), cv[:, h], ALU.mult, ALU.add))
                    dve.scalar_tensor_tensor(cv[:, h], upad[:, h, 0:256], col(0), cv[:, h], ALU.mult, ALU.add)\
                       .then_inc(S("conv_done"), 1)
                split(b + 2 + AHEAD, i)
                dve.wait_ge(S("silu"), q + 1 + i)
                dve.wait_ge(S("conv_done"), 2 * q + 2 + 2 * i)
                dve.tensor_tensor(fa, sil, cv[:, 1], ALU.mult).then_inc(S("ffn_act"), 1)
                dve.wait_ge(S("ffn_hi"), q + 1 + i)
                dve.tensor_tensor(f_lo[:, :], fa, f_hi[:, :].bitcast(F32), ALU.subtract).then_inc(S("ffn_lo"), 1)
                split(b + 3 + AHEAD, i)

            ffn_step(FFN)
            with dve.Fori(0, NF - 1) as i:
                own.enter(i, 4)
                ffn_step(FFN + 4, i)
                own.leave(NF - 1)
            split(MIX - 1 + AHEAD)
            dve.wait_ge(chunk_used, MIX)
            for n in range(4):
                v = slice(2 * n, 2 * n + 2)
                dve.tensor_tensor(xres[:, v], bank[4 + n][:, :].rearrange("p (a t) -> p a t", a=2), xres[:, v], ALU.add)\
                   .then_inc(S("x_ffn"), 1)
            ada_cols = bank[2][:, 0:2 * ADA].rearrange("p (n c) -> p n c", c=2)
            own.after(dve.tensor_tensor(mod[:, 0:ADA_FFN], ada_cols[:, 0:ADA_FFN, 0], V("ada_b_2", ADA_FFN), ALU.add))
            dve.scalar_tensor_tensor(gain[:, :], mod[:, 8:16], 1.0, V("norm_mix_g_2", 8), ALU.add, ALU.mult)\
               .then_inc(S("gain"), 1)
            dve.wait_ge(S("gain"), 1)
            sq_, rstd_, y_ = tiles(arena[:, 8000:8000 + 2048], 8), rstd2, tiles(arena[:, 10048:10048 + 2048], 8)
            norm(2, gain, mod[:, 0:8])
            dve.memset(pb[:, :, 0:1], 0.0).then_inc(S("pads2"), 1)
            dve.memset(cy[:, :, 0:30], 0.0).then_inc(S("pads2"), 1)
            def shift(n):
                dve.wait_ge(S("mix_taken"), n + 1)
                own.after(dve.tensor_tensor(xs[:, n], pb[:, n, 0:256], pb[:, n, 1:257], ALU.subtract))
                dve.scalar_tensor_tensor(xs[:, n], xs[:, n], V("rwkv_mu_2", 1, n), pb[:, n, 1:257], ALU.mult, ALU.add)\
                   .then_inc(S("shifted"), 1)

            for n in range(14):
                split(MIX + 2 * n + AHEAD)
                shift(n)
                split(MIX + 2 * n + 1 + AHEAD)
            for n in range(4):
                split(MIX + 28 + 2 * n + AHEAD)
                split(MIX + 28 + 2 * n + 1 + AHEAD)
            for n in range(4):
                split(MIX + 36 + 2 * n + AHEAD)
                dve.wait_ge(chunk_used, MIX + 36 + 2 * n + 1)
                dve.wait_ge(S("mix_taken"), 18)
                own.after(dve.tensor_tensor(cy[:, n, 30:286], bank[n % 2][:, 0:TOK], sgb[:, n], ALU.mult))
                dve.sem_inc(S("conv_in"), 1)
                split(MIX + 36 + 2 * n + 1 + AHEAD)
            for n in range(3):
                split(ADA_REST + n + AHEAD)
            dve.wait_ge(chunk_used, W_OUT2)
            own.after(dve.tensor_tensor(mod[:, ADA_FFN:ADA], ada_cols[:, ADA_FFN:ADA, 0], V("ada_b_2", ADA - ADA_FFN, ADA_FFN), ALU.add))
            own.after(dve.scalar_tensor_tensor(gain[:, :], mod[:, 32:40], 1.0, V("norm_ffn_g_2", 8), ALU.add, ALU.mult))
            dve.sem_inc(S("mod_done"), 1)
            dve.wait_ge(S("shifted"), 14)
            xk, xr, xv = xs[:, 2:6], xs[:, 6:10], xs[:, 10:14]
            for f in range(4):
                dve.tensor_scalar(kk[:, f], xk[:, f], V("rwkv_k_k_2", 1, f), None, ALU.mult).then_inc(S("kk"), 1)
            reset = C("reset")
            for f in range(4):
                dve.wait_ge(S("decay"), f + 1)
                dve.tensor_tensor_scan(cum[:, f], reset, sw[:, f], 0.0, ALU.mult, ALU.add).then_inc(S("cum"), 1)
            dve.wait_ge(S("cum"), 4)
            dve.tensor_tensor(sw[:, :, :], cum[:, :, :], sw[:, :, :], ALU.subtract).then_inc(S("cum"), 1)
            dve.wait_ge(S("kk_norm"), 2)
            own.after(dve.tensor_scalar(rf[:, :, :], rf[:, :, :], 1e-12, None, ALU.max))
            own.after(dve.reciprocal(rf[:, :, :], rf[:, :, :]))
            own.after(dve.tensor_tensor(kk[:, :, :], kk[:, :, :], rf[:, :, :], ALU.mult))
            own.after(dve.tensor_scalar(gain2[:, :], V("rwkv_k_a_2", 4), -1.0, 1.0, ALU.mult, ALU.add))
            dve.wait_ge(S("rate"), 4)
            for f in range(4):
                own.mark(dve.tensor_scalar(bon[:, f], aa[:, f], V("rwkv_k_a_2", 1, f), gain2[:, f:f + 1], ALU.mult, ALU.add))
            own.wait()
            own.mark(dve.tensor_tensor(xk, xk, bon[:, :, :], ALU.mult))
            own.after(dve.tensor_tensor(bf[:, :, :], kk[:, :, :], aa[:, :, :], ALU.mult))
            for f in range(4):
                own.mark(dve.scalar_tensor_tensor(aa[:, f], xr[:, f], V("rwkv_r_k_2", 1, f), xk[:, f], ALU.mult, ALU.mult))
            own.wait()
            dve.sem_inc(S("rk"), 1)
            dve.wait_ge(S("e2"), 1)
            own.mark(dve.tensor_tensor(bf[:, :, :], bf[:, :, :], e2[:, :, :], ALU.mult))
            own.mark(dve.tensor_tensor(kf[:, :, :], xk, e2[:, :, :], ALU.mult))
            own.mark(dve.tensor_tensor(rf[:, :, :], xr, e1[:, :, :], ALU.mult))
            dve.wait_ge(S("e3"), 1)
            own.after(dve.scalar_tensor_tensor(zf[:, :, :].rearrange("p a b -> p (a b)"), kk[:, :, :].rearrange("p a b -> p (a b)"), -1.0,
                                               sw[:, :, :].rearrange("p a b -> p (a b)"), ALU.mult, ALU.mult))
            dve.sem_inc(S("factors"), 1)
            for f in range(2):
                dve.wait_ge(S("bonus_sum"), f + 1)
                own.mark(dve.tensor_tensor(bon[:, 2 * f:2 * f + 2], bank[6 + f][:, :].rearrange("p (a t) -> p a t", a=2), xv[:, 2 * f:2 * f + 2], ALU.mult))
            own.wait()
            dve.sem_inc(S("bonus_read"), 1)
            for f in range(4):
                own.after(dve.tensor_scalar(co[:, f], cy[:, f, 0:256], V("conv_dw_w_2", 1, 31 * f), V("conv_dw_b_2", 1, f), ALU.mult, ALU.add))
            for tap in range(1, 31):
                for f in range(4):
                    own.mark(dve.scalar_tensor_tensor(co[:, f], cy[:, f, tap:tap + 256], V("conv_dw_w_2", 1, 31 * f + tap), co[:, f],
                                                      ALU.mult, ALU.add))
                own.wait()
            dve.sem_inc(S("conv_out"), 1)
            dve.wait_ge(S("ln_mean"), 1)
            for f in range(4):
                dve.scalar_tensor_tensor(co[:, f], bank[7][:, 0:TOK], -1.0 / 512, co[:, f], ALU.mult, ALU.add).then_inc(S("ln_centred"), 1)
            dve.wait_ge(S("ln_std"), 1)
            own.after(dve.reciprocal(rstd2, rstd2))
            for f in range(4):
                dve.tensor_tensor(co[:, f], co[:, f], rstd2, ALU.mult).then_inc(S("ln_y"), 1)
            for f in range(4):
                dve.wait_ge(S("mix_hi"), f + 1)
                dve.tensor_tensor(x_lo[:, f], co[:, f], x_hi[:, f].bitcast(F32), ALU.subtract).then_inc(S("mix_lo"), 1)
            def mask(name):
                return C(name).rearrange("p (a s) -> p a s", a=1).broadcast_to([P, 4, 128])

            dve.wait_ge(S("tok_major"), 8)
            for n, (kind, dst) in enumerate(GRAM):
                for b in range(4):
                    dve.wait_ge(S("gram"), 4 * n + b + 1)
                    src = bank[2 * b + n % 2][:, :].rearrange("p (h s) -> p h s", h=4)
                    for d_, m in dst:
                        ins_ = dve.tensor_tensor(dict(AK=AK, RB=RB, RK=RK, **MAT)[d_][:, b], src, mask(m), ALU.mult)
                        own.mark(ins_)
                    own.wait()
                    dve.sem_inc(S("gram_masked"), 1)
            for b in range(4):
                own.mark(dve.tensor_tensor(R_[:, b], DU[:, b], ident.rearrange("p (a s) -> p a s", a=1).broadcast_to([P, 4, 128]), ALU.add))
            own.wait()
            dve.sem_inc(S("neu_start"), 1)
            for s, step in enumerate(NEUMANN):
                for b in range(4):
                    for k, (lhs, rhs, dst, how) in enumerate(step):
                        if how == "act":
                            continue
                        dve.wait_ge(S("neu_prod"), PROD[s, b, k])
                        src = bank[2 * b + k][:, :].rearrange("p (h s) -> p h s", h=4)
                        if how == "copy":
                            dve.tensor_copy(MAT[dst][:, b], src).then_inc(S("neu_dve"), 1)
                        elif how == "eye":
                            dve.tensor_tensor(MAT[dst][:, b], src, ident.rearrange("p (a s) -> p a s", a=1).broadcast_to([P, 4, 128]), ALU.add)\
                               .then_inc(S("neu_dve"), 1)
                        else:
                            dve.tensor_tensor(MAT[dst][:, b], src, MAT[rhs][:, b], ALU.add).then_inc(S("neu_dve"), 1)
            for t in range(2):
                dve.wait_ge(S("m1_prod"), t + 1)
                dve.tensor_copy(m1[:, t], bank[t][:, :]).then_inc(S("m1"), 1)
            for t in range(2):
                dve.wait_ge(S("w1_prod"), t + 1)
                dve.tensor_copy(w1[:, t], bank[4 + t][:, :]).then_inc(S("w1"), 1)
            for c in range(4):
                dve.wait_ge(S("phi_prod"), c + 1)
                src = bank[c][:, 0:TOK].rearrange("p (f j) -> p f j", f=4)
                dve.tensor_tensor(phi[:, c], src, C("eye64").rearrange("p (a s) -> p a s", a=1).broadcast_to([P, 4, 64]), ALU.add)\
                   .then_inc(S("phi"), 1)

            def decay_of(c):
                return e1[:, :, 64 * c + 63:64 * c + 64].broadcast_to([P, 4, 64])

            for c in range(4):
                dve.wait_ge(S("u_prod"), c + 1)
                src = bank[4 + c][:, 0:TOK].rearrange("p (f j) -> p f j", f=4)
                own.mark(dve.tensor_tensor(u0[:, c], src, decay_of(c), ALU.mult))
            own.after(dve.memset(st[:, 0], 0.0))
            dve.tensor_copy(st[:, 1], u0[:, 0]).then_inc(S("state"), 1)
            for c in range(1, 3):
                dve.wait_ge(S("phi_state"), c)
                src = bank[0][:, 0:TOK].rearrange("p (f j) -> p f j", f=4)
                own.after(dve.tensor_tensor(st[:, c + 1], src, decay_of(c), ALU.mult))
                dve.tensor_tensor(st[:, c + 1], st[:, c + 1], u0[:, c], ALU.add).then_inc(S("state"), 1)
            for t in range(2):
                dve.wait_ge(S("sa_prod"), t + 1)
                for e in range(2):
                    half = (x.rearrange("p (f e i) -> p e f i", f=4, e=2)[:, e] for x in (sa[:, t], m2[:, t]))
                    dve.tensor_tensor(next(half), bank[4 + 2 * t + e][:, 0:TOK].rearrange("p (f i) -> p f i", f=4), next(half), ALU.add)\
                       .then_inc(S("sa"), 1)
            for f in range(2):
                dve.wait_ge(S("y_mean"), f + 1)
                v = slice(2 * f, 2 * f + 2)
                dve.scalar_tensor_tensor(yy[:, v].rearrange("p a b -> p (a b)"), bank[2 + f][:, :], -1.0 / 64,
                                         yy[:, v].rearrange("p a b -> p (a b)"), ALU.mult, ALU.add).then_inc(S("y_centred"), 1)
            dve.wait_ge(S("y_std"), 2)
            own.after(dve.reciprocal(ysq[:, :, :], ysq[:, :, :]))
            own.after(dve.tensor_tensor(yy[:, :, :], yy[:, :, :], ysq[:, :, :], ALU.mult))
            for f in range(4):
                own.mark(dve.tensor_scalar(yy[:, f], yy[:, f], V("rwkv_gn_w_2", 1, f), V("rwkv_gn_b_2", 1, f), ALU.mult, ALU.add))
            own.wait()
            own.after(dve.tensor_tensor(yy[:, :, :], yy[:, :, :], bon[:, :, :], ALU.add))
            own.after(dve.tensor_tensor(yy[:, :, :], yy[:, :, :], gg[:, :, :], ALU.mult))
            dve.sem_inc(S("y_done"), 1)
            for f in range(4):
                dve.wait_ge(S("mix_hi"), 5 + f)
                dve.tensor_tensor(x_lo[:, 4 + f], yy[:, f], x_hi[:, 4 + f].bitcast(F32), ALU.subtract).then_inc(S("mix_lo"), 1)
            for k in range(KT):
                split(W_OUT2 + k + AHEAD)
                dve.wait_ge(chunk_used, W_OUT2 + k + 1)
                dve.scalar_tensor_tensor(xres[:, k], bank[k % 4][:, 0:TOK], mod[:, 16 + k:17 + k], xres[:, k], ALU.mult, ALU.add)\
                   .then_inc(S("x_mixed2"), 1)
            dve.wait_ge(S("x_mixed2"), KT)
            norm(3, gain, mod[:, 24:32])
            splits(W_Q, 16)
            def top16(values, out_v, out_i):
                own.after(dve.max(out_v[0], values))
                own.after(dve.max_index(out_i[0], out_v[0], values))
                own.after(dve.match_replace(values, out_v[0], values, -3.0e38))
                own.after(dve.max(out_v[1], values))
                own.after(dve.max_index(out_i[1], out_v[1], values))

            j = EXP_U
            idx_u = idx.bitcast(U32)
            pos_u = pos.bitcast(U32)
            for n in range(32):
                a, b = n // 16, n % 16
                split(j + AHEAD)
                j += 1
                dve.wait_ge(S("scores"), 4 * a + b // 4 + 1)
                top16(s_sb[:, a, b], [vals[:, a, b, 0:8], vals[:, a, b, 8:16]], [idx_u[:, a, b, 0:8], idx_u[:, a, b, 8:16]])
            own.after(dve.tensor_copy(idf[:, :, :, :], idx_u[:, :, :, :]))
            for a in range(2):
                for h in range(8):
                    split(j + AHEAD)
                    j += 1
                    c3 = cand[:, a, h].rearrange("p (x y) -> p x y", x=16)
                    v0 = vals[:, a, 2 * h].rearrange("p (x y) -> p x y", y=1).broadcast_to([P, 16, 16])
                    v1 = vals[:, a, 2 * h + 1].rearrange("p (x y) -> p x y", x=1).broadcast_to([P, 16, 16])
                    own.after(dve.tensor_tensor(c3, v0, v1, ALU.add))
                    top16(cand[:, a, h], [best[:, a, h, 0:8], best[:, a, h, 8:16]], [pos_u[:, a, h, 0:8], pos_u[:, a, h, 8:16]])
            own.after(dve.tensor_tensor(gate[:, :, :, :], best[:, :, :, :], best[:, :, :, 0:1].broadcast_to([P, 2, 8, 16]), ALU.subtract))
            dve.sem_inc(S("best_shifted"), 1)
            pu = poshu.bitcast(U32)
            own.mark(dve.tensor_scalar(pu[:, 0], pos_u[:, :, :, :], 4, None, ALU.logical_shift_right))
            own.after(dve.tensor_scalar(pu[:, 1], pos_u[:, :, :, :], 15, None, ALU.bitwise_and))
            own.after(dve.tensor_copy(poshl[:, :, :, :, :], pu[:, :, :, :, :]))
            for c in range(2):
                for a in range(2):
                    for _ in range(2):
                        if j + AHEAD < EXP_U + TOP_FIRST:
                            split(j + AHEAD)
                            j += 1
                    d_ = poshl[:, c, a].rearrange("p h (k y) -> p h k y", y=1).broadcast_to([P, 8, 16, 16])
                    lst = idf[:, a].rearrange("p (h c) j -> p c h j", c=2)[:, c]
                    for h in range(8):
                        own.mark(dve.tensor_tensor(onehot[:, h], iota[:, 0:16].rearrange("p (x y) -> p x y", x=1).broadcast_to([P, 16, 16]),
                                                   d_[:, h], ALU.is_equal))
                    own.wait()
                    for h in range(8):
                        own.mark(dve.tensor_tensor(onehot[:, h], onehot[:, h],
                                                   lst[:, h].rearrange("p (x j) -> p x j", x=1).broadcast_to([P, 16, 16]), ALU.mult))
                    own.wait()
                    own.after(dve.tensor_reduce(isel[:, c, a], onehot[:, :, :, :], AX, ALU.add))
            n = EXP_U + TOP_FIRST - j
            for _ in range(n % 4):
                split(j + AHEAD)
                j += 1
            if n // 4:
                splits(j, n // 4 * 4)
                j += n // 4 * 4
            dve.wait_ge(S("gate_exp"), 1)
            own.after(dve.tensor_reduce(gsum[:, :, :], gate[:, :, :, :], AX, ALU.add))
            own.after(dve.reciprocal(gsum[:, :, :], gsum[:, :, :]))
            own.after(dve.tensor_tensor(gate[:, :, :, :], gate[:, :, :, :],
                                        gsum.rearrange("p a (h y) -> p a h y", y=1).broadcast_to([P, 2, 8, 16]), ALU.mult))
            dve.sem_inc(S("gate_done"), 1)
            dve.wait_ge(S("routing_turned"), 1)
            dve.tensor_copy(i0T[:, :], bank[4][:, 0:TOK]).then_inc(S("i0T"), 1)
            splits(j, EXP_V - j)
            def hots(b, i=0):
                if b >= 2:
                    dve.wait_ge(S("dense"), b - 1 + 2 * i)
                for k in range(4):
                    if isinstance(i, int):
                        e, g = (bank[p_][:, off + 4 * b + k:off + 4 * b + k + 1] for p_, off in ((4, 256), (5, 0)))
                    else:
                        e, g = (bank[p_][:, bass.ds(i * 8 + (off + 4 * b + k), 1)] for p_, off in ((4, 256), (5, 0)))
                    ins_ = dve.tensor_scalar(hotB[:, b % 2, k], iota, e, g, ALU.is_equal, ALU.mult)
                ins_.then_inc(S("hotB"), 1)

            def mix(b, i=0):
                dve.wait_ge(S("dense"), b + 1 + 2 * i)
                at = 4 * b
                h3 = arena[:, :].rearrange("p (e t) -> p t e", t=TOK)
                dst = h3[:, at:at + 4] if isinstance(i, int) else h3[:, bass.ds(i * 8 + at, 4)]
                dve.tensor_tensor(dst, bank[b % 2][:, :].rearrange("p (t e) -> p t e", t=4), dst, ALU.mult).then_inc(S("g_mixed"), 1)

            dve.wait_ge(S("h_taken"), NKEY)
            dve.wait_ge(S("routing_turned"), 1)
            dve.wait_ge(S("spilled"), 16)
            hots(0)
            hots(1)
            with dve.Fori(0, 31) as i:
                for b in range(2):
                    mix(b, i)
                    hots(b + 2, i)
            mix(62)
            mix(63)

            def v_lo(n, i=0):
                at = n * TOK
                src = arena[:, at:at + TOK] if isinstance(i, int) else arena[:, bass.ds(i * 1024 + at, TOK)]
                dve.wait_ge(S("g_hi"), n + 1 + 4 * i)
                dve.tensor_tensor(x_lo[:, n % 4], src, x_hi[:, n % 4].bitcast(F32), ALU.subtract).then_inc(S("g_lo"), 1)

            for n in range(3):
                v_lo(n)
            with dve.Fori(0, NKEY // 4 - 1) as i:
                for p in range(4):
                    split(EXP_V + p + AHEAD, i)
                    v_lo(p + 3, i)
            for p in range(4):
                n = NKEY - 4 + p
                split(EXP_V + n + AHEAD)
                if n + 3 < NKEY:
                    v_lo(n + 3)
            dve.wait_ge(chunk_used, CHUNKS)
            dve.wait_ge(S("x_back"), 16)
            for k in range(KT):
                dve.scalar_tensor_tensor(xres[:, k], bank[4 + k // 2][:, (k % 2) * TOK:(k % 2) * TOK + TOK], mod[:, 40 + k:41 + k],
                                         xres[:, k], ALU.mult, ALU.add).then_inc(S("x_final"), 1)
            dve.wait_ge(S("norm_std"), 5)
            fr = arena[:, 4096:4096 + TOK]
            own.after(dve.reciprocal(fr, fr))
            for k in range(KT):
                own.mark(dve.scalar_tensor_tensor(arena[:, k * TOK:k * TOK + TOK], xres[:, k], V("final_g_2", 1, k), fr, ALU.mult, ALU.mult))
            own.wait()
            dve.sem_inc(S("out_ready"), 1)

        @block.gpsimd
        def _(pool):
            own = Chain(pool, S("pool_step"))
            pool.wait_ge(S("tile_taken"), 16)
            pool.wait_ge(S("consts_landed"), 16)
            own.after(pool.tensor_tensor(pw1[:, :, 1:272], upool[:, :, 1:272], upool[:, :, 0:271], ALU.add))
            own.after(pool.tensor_tensor(pw2[:, 1:4, 3:272], pw1[:, 1:4, 3:272], pw1[:, 1:4, 1:270], ALU.add))
            own.after(pool.tensor_tensor(pw1[:, 2:4, 7:272], pw2[:, 2:4, 7:272], pw2[:, 2:4, 3:268], ALU.add))
            own.after(pool.tensor_tensor(pw2[:, 3:4, 15:272], pw1[:, 3:4, 15:272], pw1[:, 3:4, 7:264], ALU.add))
            ic = C("inv_count").rearrange("p (g t) -> p g t", g=4)
            for g, w in enumerate((pw1, pw2, pw1, pw2)):
                own.mark(pool.tensor_tensor(w[:, g, 16:272], w[:, g, 16:272], ic[:, g], ALU.mult))
            own.wait()
            for g, w in enumerate((pw1, pw2, pw1, pw2)):
                own.mark(pool.tensor_tensor(w[:, g, 16:272], w[:, g, 16:272], upool[:, g, 16:272], ALU.subtract))
            own.wait()
            pool.sem_inc(S("pooled"), 1)
            def hots(b, i=0):
                if b >= 2:
                    pool.wait_ge(S("dense"), b - 1 + 2 * i)
                src = i0T[:, 4 * b:4 * b + 4] if isinstance(i, int) else i0T[:, bass.ds(i * 8 + 4 * b, 4)]
                pool.tensor_tensor(hotA[:, b % 2], iota.rearrange("p (a s) -> p a s", a=1).broadcast_to([P, 4, 128]),
                                   src.rearrange("p (a s) -> p a s", s=1).broadcast_to([P, 4, 128]), ALU.subtract)\
                    .then_inc(S("hot_diff"), 1)

            pool.wait_ge(S("i0T"), 1)
            pool.wait_ge(S("spilled"), 16)
            hots(0)
            hots(1)
            with pool.Fori(0, 31) as i:
                for b in range(2):
                    hots(b + 2, i)

        @block.tensor
        def _(pe):
            def three(o, w, wl, xh, xl, start, stop_):
                pe.matmul(o, w, xh, start=start, stop=False, skip_group_check=True)
                pe.matmul(o, w, xl, start=False, stop=False, skip_group_check=True)
                return pe.matmul(o, wl, xh, start=False, stop=stop_, skip_group_check=True)

            def reduce(b, o, i=0, xh=x_hi, xl=x_lo):
                s = b % RING
                pe.wait_ge(lo_ready, b + 1 + 4 * i)
                for k in range(KT):
                    c = slice(k * P, k * P + P)
                    m = three(o, w_hi[:, s, c], w_lo[:, s, c], xh[:, k], xl[:, k], k == 0, k == KT - 1)
                m.then_inc(chunk_used, 1)

            def spread(b, banks, xh, xl, first, last, i=0):
                s = b % RING
                pe.wait_ge(lo_ready, b + 1 + 4 * i)
                for n in range(8):
                    c = slice(n * P, n * P + P)
                    o = banks[n // 2][:, (n % 2) * TOK:(n % 2) * TOK + TOK]
                    m = three(o, w_hi[:, s, c], w_lo[:, s, c], xh, xl, first and n % 2 == 0, last)
                m.then_inc(chunk_used, 1)

            def modulation(b, n, i=0):
                col = 2 * n
                o = bank[2][:, col:col + 2] if isinstance(n, int) else bank[2][:, bass.ds(col, 2)]
                reduce(b, o, i, c_hi, c_lo)

            def norm(n):
                for k in range(KT):
                    pe.wait_ge(S("norm_sq"), KT * n + k + 1)
                    m = pe.matmul(bank[7][:, 0:TOK], ones, sq_[:, k], start=k == 0, stop=k == KT - 1)
                m.then_inc(S("norm_ssq"), 1)

            pe.wait_ge(S("kept_landed"), 16)
            sq_ = sq
            norm(0)
            pe.wait_ge(S("norm_lo"), 8)
            for j in range(4):
                reduce(j, bank[j][:, 0:TOK])
            with pe.Fori(0, 7) as i:
                for p in range(4):
                    pe.wait_ge(S("tile_taken"), p + 1 + 4 * i)
                    reduce(4 + p, bank[p][:, 0:TOK], i)
            pe.wait_ge(S("consts_landed"), 16)
            for n in range(8):
                pe.wait_ge(S("qk_sq"), n // 2 + 1)
                m = pe.matmul(bank[4 + n // 2][:, (n % 2) * TOK:(n % 2) * TOK + TOK], C("head"), sq[:, n], start=True, stop=True)
                if n % 2:
                    m.then_inc(S("qk_ssq"), 1)
            pe.wait_ge(S("tile_taken"), 32)
            for t in range(2):
                for f in range(4):
                    m = pe.transpose(bank[t][:, f * P:f * P + P], qkv[:, 8 + f, t * P:t * P + P], ident)
                m.then_inc(S("v_turned"), 1)
            for n in range(8):
                pe.wait_ge(S("qk_normed"), n // 4 + 1)
                m = pe.matmul(bank[4 + n // 2][:, (n % 2) * TOK:(n % 2) * TOK + TOK], C("rot"), rs[:, n], start=True, stop=True)
                if n % 2:
                    m.then_inc(S("qk_turned"), 1)

            def score(h):
                f, p0, b = h // 2, 64 * (h % 2), h % 2
                if h >= 2:
                    pe.wait_ge(S("neg_max"), h - 1)
                r = slice(p0, p0 + 64)
                pe.matmul(bank[b][:, 0:128], qkv[r, f, 0:128], qkv[r, 4 + f, 0:128], start=True, stop=True)
                pe.matmul(bank[b][:, 128:384], qkv[r, f, 128:256], qkv[r, 4 + f, :], start=True, stop=True)\
                  .then_inc(S("qk_scored"), 1)

            def turn(h):
                b = h % 2
                pe.wait_ge(S("p_rows"), h + 1)
                if h >= 2:
                    pe.wait_ge(S("pT"), h - 1)
                for n in range(3):
                    m = pe.transpose(bank[2 + b][:, n * P:n * P + P], pex[:, b, n * P:n * P + P], ident)
                m.then_inc(S("p_turned"), 1)

            def attend(h):
                f, p0, b = h // 2, 64 * (h % 2), h % 2
                pe.wait_ge(S("pT"), h + 1)
                o = bank[4 + f // 2][p0:p0 + 64, (f % 2) * TOK:(f % 2) * TOK + TOK]
                v = slice(h * 64, h * 64 + 64)
                pe.matmul(o[:, 0:128], v_tok[:, 0, v], pT[:, b, 0:128], start=True, stop=True)
                pe.matmul(o[:, 128:256], v_tok[:, 0, v], pT[:, b, 128:256], start=True, stop=False)
                pe.matmul(o[:, 128:256], v_tok[:, 1, v], pT[:, b, 256:384], start=False, stop=True).then_inc(S("head_out"), 1)

            pe.wait_ge(S("qk_rotated"), 4)
            pe.wait_ge(S("v_tok"), 2)
            score(0)
            for h in range(HEADS):
                if h + 1 < HEADS:
                    score(h + 1)
                turn(h)
                if h == 0:
                    pe.wait_ge(S("pooled"), 1)
                    pe.wait_ge(S("wpool_landed"), 16)
                    for g, w in enumerate((pw1, pw2, pw1, pw2)):
                        m = pe.matmul(bank[6 + g // 2][:, (g % 2) * TOK:(g % 2) * TOK + TOK], wpool[:, g], w[:, g, 16:272], start=True, stop=True)
                    m.then_inc(S("pool_mixed"), 1)
                attend(h)
            for k in range(4):
                pe.wait_ge(S("attn_lo"), 8 if k == 0 else 8)
                spread(BRANCH + k, bank[0:4], x_hi[:, k], x_lo[:, k], k == 0, k == 3)
            for k in range(4):
                spread(BRANCH + 4 + k, bank[4:8], x_hi[:, 4 + k], x_lo[:, 4 + k], k == 0, k == 3)
            pe.wait_ge(S("mixed_lo"), 8)
            for k in range(KT):
                if k >= 4:
                    pe.wait_ge(S("x_added"), k - 3)
                reduce(W_OUT + k, bank[k % 4][:, 0:TOK])
            norm(1)
            pe.wait_ge(S("norm_lo"), 16)
            reduce(FFN, bank[0][:, 0:TOK])
            reduce(FFN + 1, bank[1][:, 0:TOK])
            pe.wait_ge(S("c_lo"), 2)
            modulation(FFN + 2, 0)
            modulation(FFN + 3, NF)

            def ffn_step(b, first, i=0):
                q = (b - FFN) // 4
                pe.wait_ge(S("up_taken"), 2 * q - 1 + 2 * i)
                reduce(b, bank[0][:, 0:TOK], i)
                pe.wait_ge(S("up_taken"), 2 * q + 2 * i)
                reduce(b + 1, bank[1][:, 0:TOK], i)
                modulation(b + 2, q + i, i)
                pe.wait_ge(S("ffn_lo"), q + i)
                spread(b + 3, bank[4:8], f_hi[:, :], f_lo[:, :], first, False, i)

            ffn_step(FFN + 4, True)
            with pe.Fori(0, NF - 2) as i:
                ffn_step(FFN + 8, False, i)
            pe.wait_ge(S("ffn_lo"), NF)
            spread(MIX - 1, bank[4:8], f_hi[:, :], f_lo[:, :], False, True)
            sq_ = tiles(arena[:, 8000:8000 + 2048], 8)
            pe.wait_ge(S("x_ffn"), 4)
            norm(2)
            pe.wait_ge(S("norm_lo"), 24)
            for h in range(2):
                reduce(MIX + 2 * h, bank[h][:, 0:TOK])
                modulation(MIX + 2 * h + 1, ADA_FFN + h)
            with pe.Fori(0, 8) as i:
                for h in range(2):
                    pe.wait_ge(S("mix_taken"), h + 1 + 2 * i)
                    reduce(MIX + 4 + 2 * h, bank[h][:, 0:TOK], i)
                    modulation(MIX + 5 + 2 * h, 2 * i + (ADA_FFN + 2 + h), i)
            for n in range(4):
                if n >= 2:
                    pe.wait_ge(S("conv_in"), n - 1)
                else:
                    pe.wait_ge(S("mix_taken"), 17 + n)
                reduce(MIX + 36 + 2 * n, bank[n % 2][:, 0:TOK])
                modulation(MIX + 37 + 2 * n, ADA_FFN + 18 + n)
            for n in range(3):
                modulation(ADA_REST + n, ADA_FFN + 22 + n)
            pe.wait_ge(S("lora_in"), 1)
            pe.wait_ge(S("lora_landed"), 16)
            pe.wait_ge(S("conv_in"), 4)
            for f in range(4):
                pe.matmul(bank[f // 2][:, (f % 2) * TOK:(f % 2) * TOK + TOK], lora_sb[0:64, f * P:f * P + P], xs[0:64, 0], start=True, stop=True)
            pe.wait_ge(S("mod_done"), 1)
            for f in range(4):
                m = pe.matmul(bank[2 + f // 2][:, (f % 2) * TOK:(f % 2) * TOK + TOK], lora_sb[64:128, f * P:f * P + P], xs[64:128, 0],
                              start=True, stop=True)
            m.then_inc(S("lora_out"), 1)
            pe.wait_ge(S("lora_in"), 2)
            for f in range(4):
                m = pe.matmul(bank[4 + f // 2][:, (f % 2) * TOK:(f % 2) * TOK + TOK], lora_sb[:, 512 + f * P:512 + f * P + P], xs[:, 1],
                              start=True, stop=True)
            m.then_inc(S("lora_out"), 1)
            pe.wait_ge(S("kk_sq"), 1)
            for f in range(4):
                m = pe.matmul(bank[6 + f // 2][:, (f % 2) * TOK:(f % 2) * TOK + TOK], C("head"), rf[:, f], start=True, stop=True)
                if f % 2:
                    m.then_inc(S("kk_ssq"), 1)
            pe.wait_ge(S("rk"), 1)
            pe.wait_ge(S("kk_norm"), 2)
            for f in range(4):
                m = pe.matmul(bank[6 + f // 2][:, (f % 2) * TOK:(f % 2) * TOK + TOK], C("head"), aa[:, f], start=True, stop=True)
                if f % 2:
                    m.then_inc(S("bonus_sum"), 1)
            pe.wait_ge(S("factors"), 1)
            pe.wait_ge(S("g_out"), 2)
            for n, src in enumerate((zf, bf, kf, xs[:, 10:14])):
                for t in range(2):
                    if n == 3:
                        pe.wait_ge(S("bonus_read"), 1)
                    for f in range(4):
                        m = pe.transpose(bank[2 * n + t][:, f * P:f * P + P], src[:, f, t * P:t * P + P], ident)
                    m.then_inc(S("turned"), 1)
            pe.wait_ge(S("conv_out"), 1)
            pe.wait_ge(S("tok_major"), 8)
            for f in range(4):
                m = pe.matmul(bank[7][:, 0:TOK], ones, co[:, f], start=f == 0, stop=f == 3)
            m.then_inc(S("ln_mean"), 1)
            pe.wait_ge(S("ln_sq"), 4)
            for f in range(4):
                m = pe.matmul(bank[7][:, 0:TOK], ones, cy[:, f, 0:TOK], start=f == 0, stop=f == 3)
            m.then_inc(S("ln_var"), 1)
            pe.wait_ge(S("ln_std"), 1)
            feat = dict(Z=zf, B=bf, K=kf, R=rf)

            def fm(x, b, k):
                t, p0 = b // 2, 64 * (b % 2)
                return x[p0:p0 + 64, k, t * P:t * P + P]

            for n, ((l, r), _) in enumerate(GRAM):
                for b in range(4):
                    if n >= 2:
                        pe.wait_ge(S("gram_masked"), 4 * (n - 2) + b + 1)
                    for k in range(4):
                        m = pe.matmul(bank[2 * b + n % 2][:, k * P:k * P + P], fm(feat[l], b, k), fm(feat[r], b, k), start=True, stop=True)
                    m.then_inc(S("gram"), 1)
            pe.wait_ge(S("neu_start"), 1)
            for s, step in enumerate(NEUMANN):
                for b in range(4):
                    if s > 0:
                        nd, na = DONE[s, b]
                        if nd:
                            pe.wait_ge(S("neu_dve"), nd)
                        if na:
                            pe.wait_ge(S("neu_act"), na)
                    for k, (lhs, rhs, dst, how) in enumerate(step):
                        for u in range(4):
                            o = bank[2 * b + k][:, u * P:u * P + P]
                            if rhs == "turn":
                                m = pe.transpose(o, MAT[lhs][:, b, u], ident)
                            else:
                                m = pe.matmul(o, MAT[lhs][:, b, u], MAT[rhs][:, b, u], start=True, stop=True)
                        m.then_inc(S("neu_prod"), 1)
            pe.wait_ge(S("neu_act"), sum(h == "act" for s_ in NEUMANN for *_, h in s_) * 4)
            for t in range(2):
                for h in range(8):
                    b, k = 2 * t + h % 2, h // 2
                    m = pe.matmul(bank[t][:, h * 64:h * 64 + 64], R_[:, b, k], zt[:, t, h * 64:h * 64 + 64], start=True, stop=True)
                m.then_inc(S("m1_prod"), 1)
            for t in range(2):
                for h in range(8):
                    b, k, p0 = 2 * t + h % 2, h // 2, 64 * (h % 2)
                    m = pe.matmul(bank[2 + t][p0:p0 + 64, (h // 2) * P:(h // 2) * P + P], zt[:, t, h * 64:h * 64 + 64], R_[:, b, k],
                                  start=True, stop=True)
                m.then_inc(S("m1T_prod"), 1)
            for t in range(2):
                for h in range(8):
                    b, k = 2 * t + h % 2, h // 2
                    m = pe.matmul(bank[4 + t][:, h * 64:h * 64 + 64], AK[:, b, k], vt[:, t, h * 64:h * 64 + 64], start=True, stop=True)
                m.then_inc(S("w1_prod"), 1)
            for t in range(2):
                pe.wait_ge(S("w1"), t + 1)
                for h in range(8):
                    b, k = 2 * t + h % 2, h // 2
                    m = pe.matmul(bank[6 + t][:, h * 64:h * 64 + 64], R_[:, b, k], w1[:, t, h * 64:h * 64 + 64], start=True, stop=True)
                m.then_inc(S("m2_prod"), 1)
            pe.wait_ge(S("m1"), 2)
            pe.wait_ge(S("m1T"), 2)
            for c in range(4):
                t, r = c // 2, slice(64 * (c % 2), 64 * (c % 2) + 64)
                for h in range(8):
                    o = bank[c][64 * (h % 2):64 * (h % 2) + 64, (h // 2) * 64:(h // 2) * 64 + 64]
                    v = slice(h * 64, h * 64 + 64)
                    m = pe.matmul(o, m1[r, t, v], bt[r, t, v], start=True, stop=True)
                m.then_inc(S("phi_prod"), 1)
            pe.wait_ge(S("m2"), 2)
            for c in range(4):
                t, r = c // 2, slice(64 * (c % 2), 64 * (c % 2) + 64)
                for h in range(8):
                    o = bank[4 + c][64 * (h % 2):64 * (h % 2) + 64, (h // 2) * 64:(h // 2) * 64 + 64]
                    v = slice(h * 64, h * 64 + 64)
                    pe.matmul(o, bt[r, t, v], m2[r, t, v], start=True, stop=False)
                    m = pe.matmul(o, kt_[r, t, v], vt[r, t, v], start=False, stop=True)
                m.then_inc(S("u_prod"), 1)
            pe.wait_ge(S("phi"), 4)
            pe.wait_ge(S("w1"), 2)
            for c in range(1, 3):
                pe.wait_ge(S("state"), c)
                for h in range(8):
                    r = slice(64 * (h % 2), 64 * (h % 2) + 64)
                    m = pe.matmul(bank[0][r, (h // 2) * 64:(h // 2) * 64 + 64], phi[r, c, h // 2], st[r, c, h // 2], start=True, stop=True)
                m.then_inc(S("phi_state"), 1)
            pe.wait_ge(S("state"), 3)
            for c in range(4):
                t = c // 2
                for h in range(8):
                    r = slice(64 * (h % 2), 64 * (h % 2) + 64)
                    m = pe.matmul(bank[4 + 2 * t + h % 2][64 * (c % 2):64 * (c % 2) + 64, (h // 2) * 64:(h // 2) * 64 + 64], m1T[r, h // 2, 64 * c:64 * c + 64],
                                  st[r, c, h // 2], start=True, stop=True)
                if c % 2:
                    m.then_inc(S("sa_prod"), 1)
            for h in range(8):
                r, f = slice(64 * (h % 2), 64 * (h % 2) + 64), h // 2
                for t in range(2):
                    pe.wait_ge(S("sa"), 2 * t + 2)
                    o = bank[f // 2][r, (f % 2) * TOK + t * P:(f % 2) * TOK + t * P + P]
                    b, k, v = 2 * t + h % 2, h // 2, slice(h * 64, h * 64 + 64)
                    for c in range(2):
                        pe.matmul(o[:, 64 * c:64 * c + 64], st[r, 2 * t + c, f], rf[r, f, t * P + 64 * c:t * P + 64 * c + 64],
                                  start=c == 0, stop=False, skip_group_check=True)
                    pe.matmul(o, sa[:, t, v], RB[:, b, k], start=False, stop=False, skip_group_check=True)
                    m = pe.matmul(o, vt[:, t, v], RK[:, b, k], start=False, stop=True, skip_group_check=True)
            m.then_inc(S("y_prod"), 1)
            for f in range(4):
                pe.wait_ge(S("y_out"), f // 2 + 1)
                m = pe.matmul(bank[2 + f // 2][:, (f % 2) * TOK:(f % 2) * TOK + TOK], C("head"), yy[:, f], start=True, stop=True)
                if f % 2:
                    m.then_inc(S("y_mean"), 1)
            pe.wait_ge(S("y_sq"), 1)
            for f in range(4):
                m = pe.matmul(bank[4 + f // 2][:, (f % 2) * TOK:(f % 2) * TOK + TOK], C("head"), ysq[:, f], start=True, stop=True)
                if f % 2:
                    m.then_inc(S("y_var"), 1)
            pe.wait_ge(S("mix_lo"), 8)
            for k in range(KT):
                if k >= 4:
                    pe.wait_ge(S("x_mixed2"), k - 3)
                reduce(W_OUT2 + k, bank[k % 4][:, 0:TOK])
            pe.wait_ge(S("x_mixed2"), 8)
            norm(3)
            pe.wait_ge(S("norm_lo"), 32)
            for j in range(16):
                if j >= 4:
                    pe.wait_ge(S("q_taken"), j - 3)
                reduce(W_Q + j, bank[j % 4][:, 0:TOK])
            pe.wait_ge(S("q_taken"), 16)
            pe.wait_ge(S("keys_landed"), 16)
            for n in range(8):
                for k in range(4):
                    b = 4 * (n % 4) + k
                    m = pe.matmul(bank[n][:, k * P:k * P + P], qT[:, b, (n // 4) * P:(n // 4) * P + P], keys[:, b], start=True, stop=True)
                m.then_inc(S("scored"), 1)
            pe.wait_ge(S("scores"), 8)
            for j in range(4):
                reduce(EXP_U + j, bank[j][:, 0:TOK])
            def h_loop(n0, count):
                with pe.Fori(0, count // 4) as i:
                    for p in range(4):
                        pe.wait_ge(S("h_taken"), n0 - 3 + p + 4 * i)
                        reduce(EXP_U + n0 + p, bank[p][:, 0:TOK], i)

            h_loop(4, TOP_FIRST - 4)
            pe.wait_ge(S("gate_done"), 1)
            for c in range(2):
                for a in range(2):
                    pe.transpose(bank[4][:, c * TOK + a * P:c * TOK + a * P + P], isel[:, c, a].rearrange("p h k -> p (h k)"), ident)
            for a in range(2):
                m = pe.transpose(bank[5][:, a * P:a * P + P], gate[:, a].rearrange("p h k -> p (h k)"), ident)
            m.then_inc(S("routing_turned"), 1)
            h_loop(TOP_FIRST, NKEY - TOP_FIRST)
            def dense(b, i=0):
                pe.wait_ge(S("hotA"), b + 1 + 2 * i)
                pe.wait_ge(S("hotB"), b + 1 + 2 * i)
                if b >= 2:
                    pe.wait_ge(S("g_mixed"), b - 1 + 2 * i)
                for k in range(4):
                    m = pe.matmul(bank[b % 2][:, k * P:k * P + P], hotA[:, b % 2, k], hotB[:, b % 2, k], start=True, stop=True)
                m.then_inc(S("dense"), 1)

            pe.wait_ge(S("h_taken"), NKEY)
            dense(0)
            dense(1)
            with pe.Fori(0, 31) as i:
                for b in range(2):
                    dense(b + 2, i)
            def v_step(n, i=0, first=False, last=False):
                pe.wait_ge(S("g_lo"), n + 1 + 4 * i)
                spread(EXP_V + n, bank[4:8], x_hi[:, n % 4], x_lo[:, n % 4], first, last, i)

            v_step(0, first=True)
            for n in range(1, 4):
                v_step(n)
            with pe.Fori(0, NKEY // 4 - 2) as i:
                for p in range(4):
                    v_step(4 + p, i)
            for n in range(NKEY - 4, NKEY):
                v_step(n, last=n == NKEY - 1)
            for k in range(KT):
                pe.wait_ge(S("norm_sq"), 4 * KT + k + 1)
                m = pe.matmul(bank[0][:, 0:TOK], ones, arena[:, 2048 + k * TOK:2304 + k * TOK], start=k == 0, stop=k == KT - 1)
            m.then_inc(S("norm_ssq"), 1)


def constants():
    import numpy as np

    q = np.arange(P)
    p, f = q[:, None], q[None, :]
    c = {"ident": p == f, "ones": np.ones((P, P)), "iota": np.broadcast_to(f, (P, P)), "head": p // 64 == f // 64}
    rot = np.zeros((P, P))
    for h in range(2):
        for d in range(8):
            rot[64 * h + d + 8, 64 * h + d] = -1
            rot[64 * h + d, 64 * h + d + 8] = 1
    c["rot"] = rot
    same16, same64 = p // 16 == f // 16, p // 64 == f // 64
    c["m16u"] = same16 & (p < f)
    c["m16l"] = same16 & (f < p)
    c["mel"] = same64 & ~same16 & (f < p)
    c["msu"] = same64 & (p < f)
    c["miu"] = same64 & (p <= f)
    c["eye64"] = p % 64 == np.arange(64)[None, :]
    t = np.arange(TOK, dtype=np.float32)
    inv = np.float32(500000.0) ** (-np.arange(8, dtype=np.float32) / np.float32(8))
    ang = (t[None, :] * inv[:, None]).astype(np.float32)
    cos, sin = np.ones((64, TOK)), np.zeros((64, TOK))
    cos[0:8] = cos[8:16] = np.cos(ang)
    sin[0:8] = sin[8:16] = np.sin(ang)
    c["cos"], c["sin"] = np.tile(cos, (2, 1)), np.tile(sin, (2, 1))
    c["inv_count"] = np.broadcast_to(np.concatenate([1 / np.minimum(t + 1, w) for w in (2, 4, 8, 16)])[None], (P, 4 * TOK))
    c["reset"] = np.broadcast_to((t % 64 != 0)[None], (P, TOK))
    k = np.arange(TOK)[None, :]
    c["causal"] = np.concatenate([np.where(k[:, 0:P] <= p, 0, -1e30), np.where(k <= P + p, 0, -1e30)], 1)
    return np.concatenate([np.asarray(c[n], np.float32).reshape(P, w) for n, w in CONSTS], 1)


def kernel(**inputs):
    import concourse.bacc as bacc
    import numpy as np
    from concourse.bass_utils import run_bass_kernel_spmd

    g = {k: np.asarray(v) for k, v in inputs.items()}

    def reduce_tiles(w):
        return w.reshape(KT, P, -1, P).transpose(2, 1, 0, 3).reshape(-1, P, CHUNK)

    def columns(v):
        return v.reshape(-1, P).T

    up = reduce_tiles(g["w_up"][0]).reshape(2, NF, P, CHUNK).transpose(1, 0, 2, 3).reshape(2 * NF, P, CHUNK)
    conv_w = g["conv_w"][0].reshape(3, 2, NF, P).transpose(3, 2, 1, 0).reshape(P, -1)
    conv_b = g["conv_b"][0].reshape(2, NF, P).transpose(2, 1, 0).reshape(P, -1)
    order = list(range(20, 22)) + list(range(12, 16)) + list(range(8, 12)) + list(range(16, 20)) + list(range(4, 8)) + list(range(0, 4))
    mu = columns(g["rwkv_mu_2"])[:, [n - 8 for n in order[:14]]]
    vectors = {
        "q_norm_g": np.tile(g["q_norm_g"], 2).T, "k_norm_g": np.tile(g["k_norm_g"], 2).T,
        "conv_w": conv_w, "conv_b": conv_b,
        "conv_dw_w_2": g["conv_dw_w_2"][0].reshape(31, 4, P).transpose(2, 1, 0).reshape(P, -1), "rwkv_mu_2": mu,
        "eps": np.broadcast_to(np.array([[1e-6, 64e-5, 1e-5]], np.float32), (P, 3)),
    }
    lora = np.concatenate([np.concatenate([g["rwkv_w2_2"][0], g["rwkv_a2_2"][0]], 0), g["rwkv_g2_2"][0]], 1)
    arrays = {
        "xT": g["x"][0].T.reshape(KT, P, TOK).transpose(1, 0, 2).reshape(P, -1),
        "vec": np.concatenate([vectors[n] if n in vectors else columns(g[n]) for n, _ in VECTORS], 1),
        "consts": constants(),
        "lora": lora,
        "w_pool": g["w_pool"][0].transpose(1, 0, 2).reshape(P, -1),
        "keys": g["peer_sub_keys_2"].reshape(16, NKEY, P).transpose(2, 0, 1).reshape(P, -1),
        "w_in": reduce_tiles(g["w_in"][0]),
        "w_branch": np.concatenate([g["w_branch_attn"][0], g["w_branch_pool"][0]], 0).reshape(8, P, CHUNK),
        "w_out": reduce_tiles(g["w_out"][0]),
        "w_up": up,
        "w_down": g["w_down"].reshape(NF, P, CHUNK),
        "ada": reduce_tiles(g["ada_w_2"][0]),
        "w_in2": reduce_tiles(g["w_in_2"][0])[order],
        "w_out2": reduce_tiles(g["w_out_2"][0]),
        "w_q": reduce_tiles(g["peer_w_q_2"][0]),
        "u": g["peer_u_2"].reshape(NKEY, NKEY, KT, P).transpose(1, 3, 2, 0).reshape(NKEY, P, CHUNK),
        "v": g["peer_v_2"].reshape(NKEY, NKEY, D).transpose(1, 0, 2),
    }
    arrays = {"in_" + n: np.ascontiguousarray(a) for n, a in arrays.items()}
    nc = bacc.Bacc("TRN2", target_bir_lowering=False, num_devices=1)
    aps = {n[3:]: nc.dram_tensor(n, a.shape, F32, kind="ExternalInput").ap() for n, a in arrays.items()}
    aps["spill"] = nc.dram_tensor("x_spill", (P, KT * TOK), F32, kind="Internal").ap()
    out = nc.dram_tensor("out", (P, KT * TOK), F32, kind="ExternalOutput").ap()
    build(nc, aps, out)
    r = run_bass_kernel_spmd(nc, [arrays], core_ids=[0])
    got = np.asarray(r.results[0]["out"])
    return got.reshape(P, KT, TOK).transpose(2, 1, 0).reshape(1, TOK, D)
```

```python
from contextlib import ExitStack

import concourse.bass as bass
from concourse import mybir

F32 = mybir.dt.float32
F32R = mybir.dt.float32r
U32 = mybir.dt.uint32
ACT = mybir.ActivationFunctionType
ALU = mybir.AluOpType
AX = mybir.AxisListType.X

P = 128
TOK = 256
D = 1024
KT = D // P
CHUNK = 1024
RING = 4
AHEAD = 3
HEADS = 8
FF = 2816
NF = FF // P
NKEY = 128
LAMBDA = 0.6065306597126334

ADA = 6 * D // P
W_IN = 0
BRANCH = W_IN + 4096 // P
W_OUT = BRANCH + 8
FFN = W_OUT + KT
MIX = FFN + 3 * NF
W_OUT2 = MIX + 2816 // P
W_Q = W_OUT2 + KT
EXP_U = W_Q + 2048 // P
EXP_V = EXP_U + NKEY
CHUNKS = EXP_V + NKEY
assert W_OUT2 % RING == 0
ADA_RING = 3

ADA_BEFORE_ROT, ADA_BEFORE_SCORES, ADA_PER_HEAD = 6, 2, 5
assert ADA_BEFORE_ROT + ADA_BEFORE_SCORES + ADA_PER_HEAD * HEADS == ADA

VECTORS = [
    ("norm_mix_g", 8), ("b_gate", 16), ("q_norm_g", 1), ("k_norm_g", 1), ("pool_scale", 4),
    ("norm_ffn_g", 8), ("conv_w", 3 * 2 * NF), ("conv_b", 2 * NF), ("c_2", 8), ("ada_b_2", ADA),
    ("norm_mix_g_2", 8), ("conv_dw_w_2", 31 * 4), ("conv_dw_b_2", 4), ("conv_ln_w_2", 4),
    ("conv_ln_b_2", 4), ("rwkv_mu_2", 14), ("rwkv_w0_2", 4), ("rwkv_a0_2", 4), ("rwkv_k_k_2", 4),
    ("rwkv_k_a_2", 4), ("rwkv_r_k_2", 4), ("rwkv_gn_w_2", 4), ("rwkv_gn_b_2", 4),
    ("norm_ffn_g_2", 8), ("final_g_2", 8), ("eps", 3),
]
COL = {}
_at = 0
for _name, _n in VECTORS:
    COL[_name] = _at
    _at += _n
NVEC = _at

CONSTS = [
    ("ident", 128), ("ones", 128), ("iota", 128),
    ("head", 128), ("m16u", 128), ("m16l", 128), ("mel", 128), ("msu", 128), ("miu", 128),
    ("eye64", 64), ("reset", 256),
    ("rot", 128), ("cos", 256), ("sin", 256), ("inv_count", 1024), ("causal", 384),
]
CAT = {}
_at = 0
for _name, _n in CONSTS:
    CAT[_name] = _at
    _at += _n
NCONST = _at
KEPT = 384
PAST = CAT["rot"] - KEPT


GRAM = [
    (("B", "Z"), [("DU", "m16u")]),
    (("Z", "B"), [("DL", "m16l"), ("EL", "mel")]),
    (("K", "Z"), [("AK", "msu")]),
    (("B", "R"), [("RB", "miu")]),
    (("K", "R"), [("RK", "miu")]),
]
NEUMANN = [
    [("DL", "DU", "D2U", "act"), ("DU", "DL", "D2L", "act")],
    [("D2L", "R", "R", "add"), ("D2L", "D2U", "DU", "act")],
    [("D2U", "D2L", "DL", "act")],
    [("DL", "R", "R", "add"), ("DU", "DL", "D2L", "act")],
    [("D2L", "R", "R", "add")],
    [("R", "turn", "D2U", "act"), ("R", "EL", "DU", "copy")],
    [("EL", "R", "DL", "act"), ("EL", "R", "R", "eye")],
    [("DL", "DU", "EL", "act")],
    [("EL", "R", "DL", "add")],
    [("D2U", "DL", "R", "act")],
]


def count_products():
    prod, done, n, on_dve, on_act = {}, {}, 0, [0] * 4, [0] * 4
    dve = act = 0
    for s, step in enumerate(NEUMANN):
        for b in range(4):
            done[s, b] = on_dve[b], on_act[b]
        for b in range(4):
            for k, entry in enumerate(step):
                n += 1
                prod[s, b, k] = n
                if entry[3] == "act":
                    act += 1
                    on_act[b] = act
                else:
                    dve += 1
                    on_dve[b] = dve
    return prod, done


PROD, DONE = count_products()


class Chain:

    def __init__(self, eng, sem):
        self.eng, self.sem, self.n, self.i, self.per, self.n0 = eng, sem, 0, None, 0, 0

    def mark(self, ins):
        ins.then_inc(self.sem, 1)
        self.n += 1

    def wait(self):
        self.eng.wait_ge(self.sem, self.n if self.i is None else self.i * self.per + self.n)

    def after(self, ins):
        self.mark(ins)
        self.wait()

    def enter(self, i, per):
        self.i, self.per, self.n0 = i, per, self.n

    def leave(self, count):
        assert self.n - self.n0 == self.per, (self.n - self.n0, self.per)
        self.n = self.n0 + self.per * count
        self.i = None


def build(nc, ins, out):
    with ExitStack() as ctx:
        def sb(name, shape, dt=F32):
            return ctx.enter_context(nc.sbuf_tensor(name, shape, dt))

        sems = {}

        def sem(name):
            if name not in sems:
                sems[name] = ctx.enter_context(nc.semaphore(name))
            return sems[name]

        bank = [ctx.enter_context(nc.psum_tensor(f"bank{b}", [P, 512], F32)) for b in range(8)]

        raw = sb("raw", [P, RING, CHUNK])
        w_hi = sb("w_hi", [P, RING, CHUNK], F32R)
        w_lo = sb("w_lo", [P, RING, CHUNK], F32R)
        x_hi = sb("x_hi", [P, KT, TOK], F32R)
        x_lo = sb("x_lo", [P, KT, TOK], F32R)
        f_hi = sb("f_hi", [P, TOK], F32R)
        f_lo = sb("f_lo", [P, TOK], F32R)
        xres = sb("xres", [P, KT, TOK])
        vec = sb("vec", [P, NVEC])
        mod = sb("mod", [P, ADA])
        gain = sb("gain", [P, KT])
        gain2 = sb("gain2", [P, 4])
        csil = sb("csil", [P, KT])
        warm = sb("warm", [P, 1])
        kept = sb("kept", [P, KEPT])
        arena = sb("arena", [P, 32768])
        i0T = sb("i0T", [P, TOK])

        def V(name, n=1, at=0):
            return vec[:, COL[name] + at:COL[name] + at + n]

        ident = kept[:, 0:128]
        ones = kept[:, 128:256]
        iota = kept[:, 256:384]

        def C(name, n=None):
            a = CAT[name] - KEPT
            return arena[:, a:a + (n or dict(CONSTS)[name])]

        class Arena:
            def __init__(self, at, end=32768):
                self.at, self.end = at, end

            def __call__(self, n):
                a = self.at
                self.at += n
                assert self.at <= self.end, (self.at, self.end)
                return arena[:, a:a + n]

        def column(name, at, each, i):
            at += COL[name]
            return vec[:, at:at + 1] if isinstance(i, int) else vec[:, bass.ds(i * each + at, 1)]

        def tiles(ap, n, w=TOK):
            return ap.rearrange("p (n t) -> p n t", n=n, t=w)

        A = Arena(NCONST - KEPT)
        qkv = tiles(A(12 * TOK), 12)
        upool = tiles(A(4 * 272), 4, 272)
        gates = tiles(A(16 * TOK), 16)
        sq = tiles(A(8 * TOK), 8)
        rs = tiles(A(8 * TOK), 8)
        rt = tiles(A(8 * TOK), 8)
        v_tok = tiles(A(2 * 512), 2, 512)
        wpool = tiles(A(512), 4, 128)
        sm = tiles(A(2 * 384), 2, 384)
        pex = tiles(A(2 * 384), 2, 384)
        pT = tiles(A(2 * 384), 2, 384)
        pw1 = tiles(A(4 * 272), 4, 272)
        pw2 = tiles(A(4 * 272), 4, 272)
        mixed = tiles(A(8 * TOK), 8)
        mixb = tiles(A(8 * TOK), 8)
        stats = A(16)
        rstd = A(TOK)
        upad = tiles(A(2 * 258), 2, 258)
        cv = tiles(A(2 * TOK), 2)
        sil = A(TOK)
        fa = A(TOK)
        ada_at = 32768 - ADA_RING * CHUNK
        assert A.at <= ada_at
        ada_raw = arena[:, ada_at:].rearrange("p (r n) -> p r n", r=ADA_RING)
        c_wide = tiles(mixb[:, 0:4].rearrange("p a t -> p (a t)"), KT, P)
        picked = tiles(mixb[:, 4:8].rearrange("p a t -> p (a t)"), KT, P)

        xT, packed, consts, lora, wpool_d, keys_d = (ins[k] for k in ("xT", "vec", "consts", "lora", "w_pool", "keys"))

        B = Arena(PAST)
        U = Arena(PAST, PAST + 9 * 2048)
        pb = tiles(B(14 * 257), 14, 257)
        sgb = tiles(B(4 * TOK), 4)
        xs = tiles(B(14 * TOK), 14)
        sw = tiles(B(4 * TOK), 4)
        cum = tiles(B(4 * TOK), 4)
        aa = tiles(B(4 * TOK), 4)
        kk = tiles(B(4 * TOK), 4)
        e2 = tiles(B(4 * TOK), 4)
        B.at = max(B.at, PAST + 7 * 2048)
        zf = tiles(B(4 * TOK), 4)
        bf = tiles(B(4 * TOK), 4)
        kf = tiles(B(4 * TOK), 4)
        B.at = max(B.at, U.end)
        cy = tiles(B(4 * 286), 4, 286)
        co = tiles(B(4 * TOK), 4)
        gg = tiles(B(4 * TOK), 4)
        e1 = tiles(B(4 * TOK), 4)
        rf = tiles(B(4 * TOK), 4)
        bon = tiles(B(4 * TOK), 4)
        zt, bt, kt_, vt = (tiles(B(2 * 512), 2, 512) for _ in range(4))
        lora_sb = B(1024)
        rstd2 = B(TOK)
        tap_product = tiles(B(3 * TOK), 3)

        def unit():
            return U(2048).rearrange("p (b h s) -> p b h s", b=4, h=4)

        AK, RB, RK, EL, R_, DU, DL, D2U, D2L = (unit() for _ in range(9))
        MAT = dict(EL=EL, R=R_, DU=DU, DL=DL, D2U=D2U, D2L=D2L)
        W = Arena(PAST + 3 * 2048, PAST + 4 * 2048)
        m1 = tiles(W(1024), 2, 512)
        m2 = tiles(W(1024), 2, 512)
        W = Arena(PAST + 5 * 2048, PAST + 9 * 2048)
        m1T = tiles(W(1024), 4)
        w1 = tiles(W(1024), 2, 512)
        phi = W(1024).rearrange("p (c f j) -> p c f j", c=4, f=4)
        u0 = W(1024).rearrange("p (c f j) -> p c f j", c=4, f=4)
        st = W(1024).rearrange("p (c f j) -> p c f j", c=4, f=4)
        sa = tiles(W(1024), 2, 512)
        yy = tiles(W(1024), 4)
        ysq = tiles(W(1024), 4)
        yf = rf

        sq3, y3, rstd3 = tiles(arena[:, 8192:10240], 8), tiles(arena[:, 10240:12288], 8), arena[:, 12288:12544]

        hbuf = arena
        K = Arena(32768 - 14336)
        s_sb = K(4096).rearrange("p (a b k) -> p a b k", a=2, b=16)
        cand_flat = K(4096)
        cand = cand_flat.rearrange("p (a h k) -> p a h k", a=2, h=8)
        qT = tiles(cand_flat, 16)
        keys_flat = K(2048)
        keys = tiles(keys_flat, 16, 128)
        onehot = keys_flat.rearrange("p (h k j) -> p h k j", h=8, k=16)
        vals = K(512).rearrange("p (a b k) -> p a b k", a=2, b=16)
        idx = K(512).rearrange("p (a b k) -> p a b k", a=2, b=16)
        idf = K(512).rearrange("p (a b k) -> p a b k", a=2, b=16)
        best = K(256).rearrange("p (a h k) -> p a h k", a=2, h=8)
        pos = K(256).rearrange("p (a h k) -> p a h k", a=2, h=8)
        poshl = K(512).rearrange("p (c a h k) -> p c a h k", c=2, a=2, h=8)
        poshu = K(512).rearrange("p (c a h k) -> p c a h k", c=2, a=2, h=8)
        isel = K(512).rearrange("p (c a h k) -> p c a h k", c=2, a=2, h=8)
        gate = K(256).rearrange("p (a h k) -> p a h k", a=2, h=8)
        gsum = K(16).rearrange("p (a h) -> p a h", a=2)
        TOP_FIRST = (32768 - 14336) // TOK
        POOL_SPLITS = 56
        hot = xres[:].rearrange("p a b -> p (a b)").rearrange("p (b k s) -> p b k s", b=4, k=4)
        hotA, hotB = hot[:, 0:2], hot[:, 2:4]
        hot_d = x_hi[:, 0:4].rearrange("p a b -> p (a b)").rearrange("p (b k s) -> p b k s", b=2, k=4)

        x_flat = xres[:].rearrange("p a b -> p (a b)")
        spill = ins["spill"]

        S = sem
        landed = [S(f"landed{s}") for s in range(RING)]
        hi_ready, lo_ready, chunk_used = S("hi_ready"), S("lo_ready"), S("chunk_used")
        ada_landed = [S(f"ada_landed{s}") for s in range(ADA_RING)]

        block = ctx.enter_context(nc.Block())

        @block.sync
        def _(sp):
            def load(b, src, n, i=0, per=RING):
                if b >= RING:
                    sp.wait_ge(lo_ready, b - RING + 1 + per * i)
                if isinstance(n, int):
                    src = src[n]
                else:
                    src = src[bass.ds(n, 1)].rearrange("a p n -> p (a n)")
                sp.dma_start(raw[:, b % RING], src).then_inc(landed[b % RING], 16)

            def load_all(b, src, n0, count):
                assert count % RING == 0
                with sp.Fori(0, count // RING) as i:
                    for p in range(RING):
                        load(b + p, src, 4 * i + (n0 + p), i)

            def ada_load(n, i=0):
                if n >= ADA_RING:
                    sp.wait_ge(S("ada_used"), n - ADA_RING + 1 + ADA_RING * i)
                src = ins["ada"][n] if isinstance(i, int) else ins["ada"][bass.ds(ADA_RING * i + n, 1)].rearrange("a p n -> p (a n)")
                sp.dma_start(ada_raw[:, n % ADA_RING], src).then_inc(ada_landed[n % ADA_RING], 16)

            sp.dma_start(x_flat, xT).then_inc(S("x_landed"), 16)
            for j in range(RING):
                load(W_IN + j, ins["w_in"], j)
            load_all(W_IN + RING, ins["w_in"], RING, 32 - RING)
            for j in range(7):
                load(BRANCH + j, ins["w_branch"], j)
            for n in range(ADA_RING):
                ada_load(n)
            with sp.Fori(0, ADA // ADA_RING - 1) as i:
                for n in range(ADA_RING, 2 * ADA_RING):
                    ada_load(n, i)
            load(BRANCH + 7, ins["w_branch"], 7)
            load_all(W_OUT, ins["w_out"], 0, KT)
            up, down = ins["w_up"], ins["w_down"]

            def ffn_loads(q, i=0):
                b = FFN + 3 * q - 1
                load(b, up, 8 * i + 2 * q, i, 12)
                load(b + 1, up, 8 * i + (2 * q + 1), i, 12)
                load(b + 2, down, 4 * i + (q - 1), i, 12)

            load(FFN, up, 0)
            load(FFN + 1, up, 1)
            ffn_loads(1)
            with sp.Fori(0, (NF - 2) // 4) as i:
                for q in range(2, 6):
                    ffn_loads(q, i)
            load(MIX - 1, down, NF - 1)
            for n in range(2):
                load(MIX + n, ins["w_in2"], n)
            load_all(MIX + 2, ins["w_in2"], 2, 20)
            load_all(W_OUT2, ins["w_out2"], 0, KT)
            load_all(W_Q, ins["w_q"], 0, 16)
            load_all(EXP_U, ins["u"], 0, NKEY)
            load_all(EXP_V, ins["v"], 0, NKEY)
            sp.wait_ge(S("out_ready"), 1)
            sp.dma_start(out, arena[:, 0:2048]).then_inc(S("out_stored"), 16)
            sp.wait_ge(S("out_stored"), 16)

        @block.scalar
        def _(act):
            own = Chain(act, S("act_step"))

            def split(b, i=0, per=RING):
                if b >= CHUNKS:
                    return
                s = b % RING
                act.wait_ge(landed[s], 16 * (b // RING + 1) + 16 * (per // RING) * i)
                if b >= RING:
                    act.wait_ge(chunk_used, b - RING + 1 + per * i)
                act.activation(w_hi[:, s], raw[:, s], ACT.Copy).then_inc(hi_ready, 1)

            def splits(b, count):
                assert count % RING == 0
                with act.Fori(0, count // RING) as i:
                    for p in range(RING):
                        split(b + p + AHEAD, i)

            def square(k, dst):
                act.activation(dst[:, k], xres[:, k], ACT.Square).then_inc(S("norm_sq"), 1)

            def load_sqrt():
                act.activation(warm[:, :], V("eps"), ACT.Sqrt)

            def norm(n, shift=None):
                act.wait_ge(S("norm_ssq"), n + 1)
                act.activation(rstd_[:, :], bank[7][:, 0:TOK], ACT.Sqrt, bias=V("eps"), scale=1.0 / D)\
                   .then_inc(S("norm_std"), 1)
                for k in range(KT):
                    act.wait_ge(S("norm_y"), KT * n + k + 1)
                    if shift is None:
                        act.activation(x_hi[:, k], y_[:, k], ACT.Copy).then_inc(S("norm_hi"), 1)
                    else:
                        act.activation(x_hi[:, k], y_[:, k], ACT.Identity, bias=shift[:, k:k + 1])\
                           .then_inc(S("norm_hi"), 1)

            act.dma_start(vec[:, :], packed).then_inc(S("vec_landed"), 16)
            act.dma_start(kept[:, :], consts[:, 0:KEPT]).then_inc(S("kept_landed"), 16)

            act.wait_ge(S("x_landed"), 16)
            act.wait_ge(S("vec_landed"), 16)
            load_sqrt()
            rstd_, y_ = rstd, mixed
            for k in range(KT):
                square(k, sq)
            for j in range(AHEAD):
                split(j)
            norm(0)
            act.dma_start(arena[:, 0:NCONST - KEPT], consts[:, KEPT:NCONST]).then_inc(S("consts_landed"), 16)
            act.dma_start(wpool[:, :, :].rearrange("p a b -> p (a b)"), wpool_d).then_inc(S("wpool_landed"), 16)
            act.activation(csil[:, :], V("c_2", 8), ACT.Silu).then_inc(S("csil"), 1)

            act.wait_ge(S("csil"), 1)
            for k in range(KT):
                act.activation(c_wide[:, k], ones, ACT.Copy, scale=csil[:, k:k + 1]).then_inc(S("c_wide"), 1)

            def taken(b, dst, i=0, func=ACT.Copy, **kw):
                act.wait_ge(chunk_used, b + 1 + 4 * i)
                act.activation(dst, bank[b % RING][:, 0:TOK], func, **kw).then_inc(S("tile_taken"), 1)

            for j in range(4):
                split(j + AHEAD)
                taken(j, qkv[:, j])
            with act.Fori(0, 2) as i:
                for p in range(4):
                    split(4 + p + AHEAD, i)
                    taken(4 + p, arena[:, bass.ds(i * 1024 + (NCONST - KEPT + (4 + p) * TOK), TOK)], i)
            act.wait_ge(S("upad_zero"), 1)
            for j in range(12, 16):
                split(j + AHEAD)
                taken(j, upool[:, j - 12, 16:272])
            for j in range(16, 32):
                split(j + AHEAD)
                taken(j, gates[:, j - 16], func=ACT.Sigmoid, bias=V("b_gate", 1, j - 16))

            act.wait_ge(S("pool_mixed"), 1)
            for g in range(4):
                act.activation(x_hi[:, 4 + g], bank[6 + g // 2][:, (g % 2) * TOK:(g % 2) * TOK + TOK], ACT.Copy,
                               scale=V("pool_scale", 1, g)).then_inc(S("pool_hi"), 1)
            for h in range(4):
                act.activation(sq[:, 2 * h:2 * h + 2], qkv[:, 2 * h:2 * h + 2], ACT.Square).then_inc(S("qk_sq"), 1)
            for h in range(4):
                act.wait_ge(S("qk_ssq"), h + 1)
                act.activation(rs[:, 2 * h:2 * h + 2].rearrange("p a b -> p (a b)"), bank[2 + h][:, :], ACT.Sqrt,
                               bias=V("eps"), scale=1.0 / 64).then_inc(S("qk_std"), 1)
            for t in range(2):
                act.wait_ge(S("v_turned"), t + 1)
                act.activation(v_tok[:, t], bank[t][:, :], ACT.Copy).then_inc(S("v_tok"), 1)
            for h in range(HEADS):
                b = h % 2
                act.wait_ge(S("neg_max"), h + 1)
                if h >= 2:
                    act.wait_ge(S("p_turned"), h - 1)
                act.activation(pex[:, b, 0:128], sm[:, b, 0:128], ACT.Exp, bias=stats[:, 4 * b:4 * b + 1],
                               accum_out=stats[:, 4 * b + 2:4 * b + 3]).then_inc(S("p_exp"), 1)
                act.activation(pex[:, b, 128:384], sm[:, b, 128:384], ACT.Exp, bias=stats[:, 4 * b + 1:4 * b + 2],
                               accum_out=stats[:, 4 * b + 3:4 * b + 4]).then_inc(S("p_exp"), 1)
                act.wait_ge(S("p_turned"), h + 1)
                if h >= 2:
                    act.wait_ge(S("head_out"), h - 1)
                act.activation(pT[:, b], bank[2 + b][:, 0:384], ACT.Copy).then_inc(S("pT"), 1)
            for f in range(4):
                act.wait_ge(S("head_out"), 4 * (f // 2) + 4)
                act.activation(x_hi[:, f], bank[4 + f // 2][:, (f % 2) * TOK:(f % 2) * TOK + TOK], ACT.Copy)\
                   .then_inc(S("attn_hi"), 1)
            splits(BRANCH, 8)
            for k in range(KT):
                act.wait_ge(S("mixed"), k // 2 + 1)
                if k == 0:
                    act.wait_ge(chunk_used, BRANCH + 8)
                act.activation(x_hi[:, k], mixed[:, k], ACT.Copy).then_inc(S("mixed_hi"), 1)
            load_sqrt()
            for k in range(KT):
                split(W_OUT + k + AHEAD)
                act.wait_ge(S("x_added"), k + 1)
                square(k, sq)
            norm(1)
            act.wait_ge(S("ffn_pad"), 1)

            def ffn_step(q, i=0):
                b = FFN + 3 * q - 1 if q else FFN
                for h in range(2):
                    split(b + h + AHEAD, i, 12)
                    act.wait_ge(chunk_used, b + h + 1 + 12 * i)
                    if q:
                        act.wait_ge(S("conv_done"), 2 * (q - 1) + h + 1 + 8 * i)
                        act.wait_ge(S(("silu", "ffn_act")[h]), q + 4 * i)
                    act.activation(upad[:, h, 2:258], bank[h][:, 0:TOK], ACT.Copy)
                    act.activation(cv[:, h], bank[h][:, 0:TOK], ACT.Identity, scale=column("conv_w", (2 * q + h) * 3 + 2, 24, i),
                                   bias=column("conv_b", 2 * q + h, 8, i)).then_inc(S("up_taken"), 1)
                act.wait_ge(S("conv_done"), 2 * q + 1 + 8 * i)
                if q:
                    act.wait_ge(S("ffn_act"), q + 4 * i)
                act.activation(sil, cv[:, 0], ACT.Silu).then_inc(S("silu"), 1)
                if q:
                    split(b + 2 + AHEAD, i, 12)
                act.wait_ge(S("ffn_act"), q + 1 + 4 * i)
                if q:
                    act.wait_ge(chunk_used, b + 3 + 12 * i)
                act.activation(f_hi[:, :], fa, ACT.Copy).then_inc(S("ffn_hi"), 1)

            ffn_step(0)
            ffn_step(1)
            with act.Fori(0, (NF - 2) // 4) as i:
                for q in range(2, 6):
                    ffn_step(q, i)
            split(MIX - 1 + AHEAD)
            load_sqrt()
            for k in range(KT):
                act.wait_ge(S("x_ffn"), k // 2 + 1)
                square(k, sq3)
            rstd_, y_ = rstd3, y3
            norm(2, mod[:, 0:8])
            act.dma_start(lora_sb, lora).then_inc(S("lora_landed"), 16)
            act.wait_ge(S("pads2"), 2)

            def mix_taken(n, dst, i=0, func=ACT.Copy):
                split(MIX + n + AHEAD, i)
                act.wait_ge(chunk_used, MIX + n + 1 + 4 * i)
                act.activation(dst, bank[n % 2][:, 0:TOK], func).then_inc(S("mix_taken"), 1)

            for n in range(6):
                mix_taken(n, pb[:, n, 1:257])
            act.wait_ge(S("shifted"), 2)
            act.activation(xs[0:64, 0], xs[0:64, 0], ACT.Tanh).then_inc(S("lora_in"), 1)
            act.activation(xs[:, 1], xs[:, 1], ACT.Sigmoid).then_inc(S("lora_in"), 1)
            for n in range(6, 8):
                mix_taken(n, pb[:, n, 1:257])
            act.wait_ge(S("lora_out"), 1)
            for f in range(4):
                half = slice((f % 2) * TOK, (f % 2) * TOK + TOK)
                act.activation(sw[:, f], bank[2 + f // 2][:, half], ACT.Sigmoid, bias=V("rwkv_w0_2", 1, f)).then_inc(S("decay"), 1)
            for f in range(4):
                half = slice((f % 2) * TOK, (f % 2) * TOK + TOK)
                act.activation(aa[:, f], bank[4 + f // 2][:, half], ACT.Sigmoid, bias=V("rwkv_a0_2", 1, f)).then_inc(S("rate"), 1)
            mix_taken(8, pb[:, 8, 1:257])
            act.wait_ge(S("lora_out"), 2)
            for f in range(2):
                act.activation(gg[:, 2 * f:2 * f + 2].rearrange("p a b -> p (a b)"), bank[6 + f][:, :], ACT.Copy).then_inc(S("g_out"), 1)
            act.wait_ge(S("kk"), 4)
            act.activation(rf[:, :, :], kk[:, :, :], ACT.Square).then_inc(S("kk_sq"), 1)
            for n in range(9, 11):
                mix_taken(n, pb[:, n, 1:257])
            for f in range(2):
                act.wait_ge(S("kk_ssq"), f + 1)
                act.activation(rf[:, 2 * f:2 * f + 2].rearrange("p a b -> p (a b)"), bank[2 + f][:, :], ACT.Sqrt).then_inc(S("kk_norm"), 1)
            mix_taken(11, pb[:, 11, 1:257])
            act.wait_ge(S("cum"), 4)
            act.activation(e1[:, :, :], cum[:, :, :], ACT.Exp, scale=-LAMBDA).then_inc(S("e1"), 1)
            mix_taken(12, pb[:, 12, 1:257])
            act.activation(e2[:, :, :], cum[:, :, :], ACT.Exp, scale=LAMBDA).then_inc(S("e2"), 1)
            mix_taken(13, pb[:, 13, 1:257])
            act.wait_ge(S("cum"), 5)
            act.activation(sw[:, :, :], sw[:, :, :], ACT.Exp, scale=-LAMBDA).then_inc(S("e3"), 1)
            for n in range(14, 18):
                mix_taken(n, sgb[:, n - 14], func=ACT.Sigmoid)
            for n in range(18, 22):
                split(MIX + n + AHEAD)
            for n in range(8):
                act.wait_ge(S("turned"), n + 1)
                dst = (zt, bt, kt_, vt)[n // 2]
                act.activation(dst[:, n % 2], bank[(n + 2) % 8][:, :], ACT.Copy).then_inc(S("tok_major"), 1)
            n = 0
            for s, step in enumerate(NEUMANN):
                for b in range(4):
                    for k, (lhs, rhs, dst, how) in enumerate(step):
                        if how != "act":
                            continue
                        act.wait_ge(S("neu_prod"), PROD[s, b, k])
                        act.activation(MAT[dst][:, b].rearrange("p a b -> p (a b)"), bank[2 * b + k][:, :], ACT.Copy)\
                           .then_inc(S("neu_act"), 1)
            for t in range(2):
                act.wait_ge(S("m1T_prod"), t + 1)
                act.activation(m1T[:, :, t * 128:t * 128 + 128], bank[2 + t][:, :].rearrange("p (f s) -> p f s", f=4), ACT.Copy)\
                   .then_inc(S("m1T"), 1)
            for t in range(2):
                act.wait_ge(S("m2_prod"), t + 1)
                act.activation(m2[:, t], bank[6 + t][:, :], ACT.Copy).then_inc(S("m2"), 1)
            act.wait_ge(S("ln_centred"), 4)
            for f in range(4):
                act.activation(cy[:, f, 0:TOK], co[:, f], ACT.Square).then_inc(S("ln_sq"), 1)
            act.wait_ge(S("ln_var"), 1)
            act.activation(rstd2, bank[1][:, 0:TOK], ACT.Sqrt, bias=V("eps", 1, 2), scale=1.0 / 512).then_inc(S("ln_std"), 1)
            for f in range(4):
                act.wait_ge(S("ln_y"), f + 1)
                act.activation(co[:, f], co[:, f], ACT.Silu, scale=V("conv_ln_w_2", 1, f), bias=V("conv_ln_b_2", 1, f))\
                   .then_inc(S("conv_silu"), 1)
            for f in range(4):
                act.wait_ge(S("conv_silu"), f + 1)
                act.activation(x_hi[:, f], co[:, f], ACT.Copy).then_inc(S("mix_hi"), 1)
            for f in range(2):
                act.wait_ge(S("y_prod"), 1)
                act.activation(yy[:, 2 * f:2 * f + 2].rearrange("p a b -> p (a b)"), bank[f][:, :], ACT.Copy).then_inc(S("y_out"), 1)
            act.wait_ge(S("y_centred"), 2)
            act.activation(ysq[:, :, :], yy[:, :, :], ACT.Square).then_inc(S("y_sq"), 1)
            for f in range(2):
                act.wait_ge(S("y_var"), f + 1)
                act.activation(ysq[:, 2 * f:2 * f + 2].rearrange("p a b -> p (a b)"), bank[4 + f][:, :], ACT.Sqrt,
                               bias=V("eps", 1, 1), scale=1.0 / 64).then_inc(S("y_std"), 1)
            for f in range(4):
                act.wait_ge(S("y_done"), f // 2 + 1)
                act.activation(x_hi[:, 4 + f], yf[:, f], ACT.Copy).then_inc(S("mix_hi"), 1)
            load_sqrt()
            for k in range(KT):
                split(W_OUT2 + k + AHEAD)
                act.wait_ge(S("x_mixed2"), k + 1)
                square(k, sq3)
            norm(3, mod[:, 24:32])
            act.dma_start(spill, x_flat).then_inc(S("spilled"), 16)
            act.dma_start(keys_flat, keys_d).then_inc(S("keys_landed"), 16)
            for j in range(16):
                split(W_Q + j + AHEAD)
                act.wait_ge(chunk_used, W_Q + j + 1)
                act.activation(qT[:, j], bank[j % 4][:, 0:TOK], ACT.Copy).then_inc(S("q_taken"), 1)
            for n in range(8):
                act.wait_ge(S("scored"), n + 1)
                act.activation(s_sb[:, n // 4, 4 * (n % 4):4 * (n % 4) + 4].rearrange("p a b -> p (a b)"), bank[n][:, :], ACT.Copy)\
                   .then_inc(S("scores"), 1)
            def h_step(b, i=0):
                split(b + AHEAD, i)
                act.wait_ge(chunk_used, b + 1 + 4 * i)
                at = (b - EXP_U) * TOK
                dst = arena[:, at:at + TOK] if isinstance(i, int) else arena[:, bass.ds(i * 1024 + at, TOK)]
                act.activation(dst, bank[b % RING][:, 0:TOK], ACT.Gelu).then_inc(S("h_taken"), 1)

            with act.Fori(0, TOP_FIRST // 4) as i:
                for p in range(4):
                    h_step(EXP_U + p, i)
            act.wait_ge(S("best_shifted"), 1)
            act.activation(gate[:, :, :, :], gate[:, :, :, :], ACT.Exp).then_inc(S("gate_exp"), 1)
            act.wait_ge(S("routing_turned"), 1)
            with act.Fori(0, (NKEY - TOP_FIRST) // 4) as i:
                for p in range(4):
                    h_step(EXP_U + TOP_FIRST + p, i)
            def hots(b, i=0):
                act.wait_ge(S("hot_diff"), b + 1 + 2 * i)
                if b >= 2:
                    act.wait_ge(S("dense"), b - 1 + 2 * i)
                act.activation(hotA[:, b % 2], hot_d[:, b % 2].bitcast(F32), ACT.Square).then_inc(S("hot_sq"), 1)
                act.wait_ge(S("hot_sq"), b + 1 + 2 * i)
                act.activation(hotA[:, b % 2], hotA[:, b % 2], ACT.Relu, scale=-1.0, bias=1.0).then_inc(S("hotA"), 1)

            act.wait_ge(S("spilled"), 16)
            hots(0)
            hots(1)
            with act.Fori(0, 31) as i:
                for b in range(2, 4):
                    hots(b, i)
            def v_hi(n, i=0):
                at = n * TOK
                src = arena[:, at:at + TOK] if isinstance(i, int) else arena[:, bass.ds(i * 1024 + at, TOK)]
                act.wait_ge(chunk_used, EXP_V + n - 3 + 4 * i)
                act.activation(x_hi[:, n % 4], src, ACT.Copy).then_inc(S("g_hi"), 1)

            act.wait_ge(S("g_mixed"), 64)
            act.dma_start(x_flat, spill).then_inc(S("x_back"), 16)
            for n in range(3):
                v_hi(n)
            with act.Fori(0, NKEY // 4 - 1) as i:
                for p in range(4):
                    split(EXP_V + p + AHEAD, i)
                    v_hi(p + 3, i)
            for p in range(4):
                n = NKEY - 4 + p
                split(EXP_V + n + AHEAD)
                if n + 3 < NKEY:
                    v_hi(n + 3)
            for k in range(KT):
                act.wait_ge(S("x_final"), k + 1)
                act.activation(arena[:, 2048 + k * TOK:2304 + k * TOK], xres[:, k], ACT.Square).then_inc(S("norm_sq"), 1)
            act.wait_ge(S("norm_ssq"), 5)
            act.activation(arena[:, 4096:4096 + TOK], bank[0][:, 0:TOK], ACT.Sqrt, bias=V("eps"), scale=1.0 / D)\
               .then_inc(S("norm_std"), 1)

        @block.vector
        def _(dve):
            own = Chain(dve, S("dve_step"))

            def split(b, i=0, per=RING):
                if b >= CHUNKS:
                    return
                s = b % RING
                dve.wait_ge(hi_ready, b + 1 + per * i)
                if b >= RING:
                    dve.wait_ge(chunk_used, b - RING + 1 + per * i)
                dve.tensor_tensor(w_lo[:, s], raw[:, s], w_hi[:, s].bitcast(F32), ALU.subtract).then_inc(lo_ready, 1)

            def splits(b, count):
                assert count % RING == 0
                with dve.Fori(0, count // RING) as i:
                    for p in range(RING):
                        split(b + p + AHEAD, i)

            def sum_squares(n, s_):
                dve.wait_ge(S("norm_sq"), KT * (n + 1))
                for w in (4, 2, 1):
                    own.after(dve.tensor_tensor(s_[:, 0:w], s_[:, 0:w], s_[:, w:2 * w], ALU.add))
                dve.sem_inc(S("norm_sum"), 1)

            def norm(n, g, shift=None):
                dve.wait_ge(S("norm_std"), n + 1)
                own.after(dve.reciprocal(rstd_, rstd_))
                for step in range(KT + 2):
                    if step < KT:
                        dve.scalar_tensor_tensor(y_[:, step], xres[:, step], g[:, step:step + 1], rstd_, ALU.mult, ALU.mult)\
                           .then_inc(S("norm_y"), 1)
                    k = step - 2
                    if k < 0:
                        continue
                    dve.wait_ge(S("norm_hi"), KT * n + k + 1)
                    if shift is None:
                        dve.tensor_tensor(x_lo[:, k], y_[:, k], x_hi[:, k].bitcast(F32), ALU.subtract)\
                           .then_inc(S("norm_lo"), 1)
                    else:
                        dve.scalar_tensor_tensor(x_lo[:, k], y_[:, k], shift[:, k:k + 1], x_hi[:, k].bitcast(F32),
                                                 ALU.add, ALU.subtract).then_inc(S("norm_lo"), 1)

            dve.memset(upool[:, :, 0:16], 0.0).then_inc(S("upad_zero"), 1)
            rstd_, y_ = rstd, mixed
            sum_squares(0, sq)
            split(0)
            norm(0, V("norm_mix_g", 8))
            for j in range(1, AHEAD):
                split(j)
            for j in range(4):
                split(j + AHEAD)
            splits(4, 28)
            dve.wait_ge(S("consts_landed"), 16)
            for g in range(4):
                dve.wait_ge(S("pool_hi"), 2 + 2 * (g // 2))
                dve.scalar_tensor_tensor(x_lo[:, 4 + g], bank[6 + g // 2][:, (g % 2) * TOK:(g % 2) * TOK + TOK],
                                         V("pool_scale", 1, g), x_hi[:, 4 + g].bitcast(F32), ALU.mult, ALU.subtract)\
                   .then_inc(S("pool_lo"), 1)
            for h in range(2):
                dve.wait_ge(S("qk_std"), 2 * h + 2)
                v = slice(4 * h, 4 * h + 4)
                own.after(dve.reciprocal(rs[:, v], rs[:, v]))
                dve.scalar_tensor_tensor(rs[:, v], qkv[:, v], V(("q_norm_g", "k_norm_g")[h]), rs[:, v], ALU.mult, ALU.mult)\
                   .then_inc(S("qk_normed"), 1)
            cosb = C("cos").rearrange("p (a t) -> p a t", a=1)
            sinb = C("sin").rearrange("p (a t) -> p a t", a=1)
            for h in range(4):
                v = slice(2 * h, 2 * h + 2)
                dve.wait_ge(S("qk_turned"), h + 1)
                own.mark(dve.tensor_tensor(rt[:, v], bank[2 + h][:, :].rearrange("p (a t) -> p a t", a=2),
                                           sinb.broadcast_to([P, 2, TOK]), ALU.mult))
                own.after(dve.tensor_tensor(qkv[:, v], rs[:, v], cosb.broadcast_to([P, 2, TOK]), ALU.mult))
                dve.tensor_tensor(qkv[:, v], qkv[:, v], rt[:, v], ALU.add).then_inc(S("qk_rotated"), 1)
            def scores(h):
                b = h % 2
                dve.wait_ge(S("qk_scored"), h + 1)
                if h >= 2:
                    dve.wait_ge(S("p_exp"), 2 * (h - 1))
                own.after(dve.scalar_tensor_tensor(sm[:, b], bank[b][:, 0:384], 0.125, C("causal"), ALU.mult, ALU.add))
                own.mark(dve.tensor_reduce(stats[:, 4 * b:4 * b + 1], sm[:, b, 0:128], AX, ALU.max))
                own.after(dve.tensor_reduce(stats[:, 4 * b + 1:4 * b + 2], sm[:, b, 128:384], AX, ALU.max))
                dve.tensor_scalar(stats[:, 4 * b:4 * b + 2], stats[:, 4 * b:4 * b + 2], -1.0, None, ALU.mult)\
                   .then_inc(S("neg_max"), 1)

            def rows(h):
                b = h % 2
                dve.wait_ge(S("p_exp"), 2 * h + 2)
                own.after(dve.reciprocal(stats[:, 8 + 2 * b:10 + 2 * b], stats[:, 4 * b + 2:4 * b + 4]))
                own.mark(dve.tensor_scalar(pex[:, b, 0:128], pex[:, b, 0:128], stats[:, 8 + 2 * b:9 + 2 * b], None, ALU.mult))
                dve.tensor_scalar(pex[:, b, 128:384], pex[:, b, 128:384], stats[:, 9 + 2 * b:10 + 2 * b], None, ALU.mult)\
                   .then_inc(S("p_rows"), 1)

            def modulation(g):
                dve.wait_ge(S("ada_used"), 8 * (g + 1))
                for n in range(2):
                    own.mark(dve.tensor_tensor(picked[:, 4 * n:4 * n + 4], bank[6 + n][:, :].rearrange("p (a s) -> p a s", a=4),
                                               ident.rearrange("p (a s) -> p a s", a=1).broadcast_to([P, 4, 128]), ALU.mult))
                own.wait()
                dve.sem_inc(S("ada_read"), 1)
                cols = mod[:, 8 * g:8 * g + 8]
                own.after(dve.tensor_reduce(cols, picked[:, :, :], AX, ALU.add))
                own.mark(dve.tensor_tensor(cols, cols, V("ada_b_2", 8, 8 * g), ALU.add))

            scores(0)
            modulation(0)
            g = 1
            for h in range(HEADS):
                if h + 1 < HEADS:
                    scores(h + 1)
                rows(h)
                if ADA_BEFORE_ROT + ADA_BEFORE_SCORES + ADA_PER_HEAD * (h + 1) >= 8 * (g + 1):
                    modulation(g)
                    g += 1
            assert g == ADA // 8
            for f in range(4):
                dve.wait_ge(S("attn_hi"), 2 * (f // 2) + 2)
                dve.tensor_tensor(x_lo[:, f], bank[4 + f // 2][:, (f % 2) * TOK:(f % 2) * TOK + TOK], x_hi[:, f].bitcast(F32),
                                  ALU.subtract).then_inc(S("attn_lo"), 1)
            splits(BRANCH, 4)
            dve.wait_ge(chunk_used, BRANCH + 4)
            for n in range(4):
                v = slice(2 * n, 2 * n + 2)
                own.mark(dve.tensor_tensor(mixed[:, v], bank[n][:, :].rearrange("p (a t) -> p a t", a=2), gates[:, v], ALU.mult))
            splits(BRANCH + 4, 4)
            dve.wait_ge(chunk_used, BRANCH + 8)
            for n in range(5):
                if n < 4:
                    v = slice(2 * n, 2 * n + 2)
                    w = slice(8 + 2 * n, 10 + 2 * n)
                    own.after(dve.tensor_tensor(mixb[:, v], bank[4 + n][:, :].rearrange("p (a t) -> p a t", a=2), gates[:, w], ALU.mult))
                    dve.tensor_tensor(mixed[:, v], mixed[:, v], mixb[:, v], ALU.add).then_inc(S("mixed"), 1)
                for k in range(2 * n - 2, 2 * n) if n else ():
                    dve.wait_ge(S("mixed_hi"), k + 1)
                    dve.tensor_tensor(x_lo[:, k], mixed[:, k], x_hi[:, k].bitcast(F32), ALU.subtract).then_inc(S("mixed_lo"), 1)
            for k in range(KT):
                split(W_OUT + k + AHEAD)
                dve.wait_ge(chunk_used, W_OUT + k + 1)
                dve.tensor_tensor(xres[:, k], bank[k % 4][:, 0:TOK], xres[:, k], ALU.add).then_inc(S("x_added"), 1)
            dve.memset(upad[:, :, 0:2], 0.0).then_inc(S("ffn_pad"), 1)
            dve.wait_ge(S("x_added"), KT)
            norm(1, V("norm_ffn_g", 8))

            def ffn_step(q, i=0):
                b = FFN + 3 * q - 1 if q else FFN
                for h in range(2):
                    dve.wait_ge(S("up_taken"), 2 * q + h + 1 + 8 * i)
                    tap = [column("conv_w", (2 * q + h) * 3 + t, 24, i) for t in range(2)]
                    own.mark(dve.scalar_tensor_tensor(cv[:, h], upad[:, h, 1:257], tap[1], cv[:, h], ALU.mult, ALU.add))
                    split(b + h + AHEAD, i, 12)
                    own.wait()
                    dve.scalar_tensor_tensor(cv[:, h], upad[:, h, 0:256], tap[0], cv[:, h], ALU.mult, ALU.add)\
                       .then_inc(S("conv_done"), 1)
                if q:
                    split(b + 2 + AHEAD, i, 12)
                dve.wait_ge(S("silu"), q + 1 + 4 * i)
                dve.wait_ge(S("conv_done"), 2 * q + 2 + 8 * i)
                dve.tensor_tensor(fa, sil, cv[:, 1], ALU.mult).then_inc(S("ffn_act"), 1)
                dve.wait_ge(S("ffn_hi"), q + 1 + 4 * i)
                dve.tensor_tensor(f_lo[:, :], fa, f_hi[:, :].bitcast(F32), ALU.subtract).then_inc(S("ffn_lo"), 1)

            ffn_step(0)
            ffn_step(1)
            with dve.Fori(0, (NF - 2) // 4) as i:
                own.enter(i, 8)
                for q in range(2, 6):
                    ffn_step(q, i)
                own.leave((NF - 2) // 4)
            split(MIX - 1 + AHEAD)
            dve.wait_ge(chunk_used, MIX)
            for n in range(4):
                v = slice(2 * n, 2 * n + 2)
                dve.tensor_tensor(xres[:, v], bank[4 + n][:, :].rearrange("p (a t) -> p a t", a=2), xres[:, v], ALU.add)\
                   .then_inc(S("x_ffn"), 1)
            dve.scalar_tensor_tensor(gain[:, :], mod[:, 8:16], 1.0, V("norm_mix_g_2", 8), ALU.add, ALU.mult)\
               .then_inc(S("gain"), 1)
            dve.wait_ge(S("gain"), 1)
            sum_squares(2, sq3)
            rstd_, y_ = rstd3, y3
            norm(2, gain, mod[:, 0:8])
            dve.memset(pb[:, :, 0:1], 0.0).then_inc(S("pads2"), 1)
            dve.memset(cy[:, :, 0:30], 0.0).then_inc(S("pads2"), 1)
            def shift(n):
                dve.wait_ge(S("mix_taken"), n + 1)
                own.after(dve.tensor_tensor(xs[:, n], pb[:, n, 0:256], pb[:, n, 1:257], ALU.subtract))
                dve.scalar_tensor_tensor(xs[:, n], xs[:, n], V("rwkv_mu_2", 1, n), pb[:, n, 1:257], ALU.mult, ALU.add)\
                   .then_inc(S("shifted"), 1)

            for n in range(6):
                shift(n)
            xk, xr, xv = xs[:, 2:6], xs[:, 6:10], xs[:, 10:14]
            dve.wait_ge(S("shifted"), 6)
            for f in range(4):
                dve.tensor_scalar(kk[:, f], xk[:, f], V("rwkv_k_k_2", 1, f), None, ALU.mult).then_inc(S("kk"), 1)
            own.mark(dve.tensor_scalar(gain2[:, :], V("rwkv_k_a_2", 4), -1.0, 1.0, ALU.mult, ALU.add))
            own.mark(dve.scalar_tensor_tensor(gain[:, :], mod[:, 32:40], 1.0, V("norm_ffn_g_2", 8), ALU.add, ALU.mult))
            shift(6)
            shift(7)
            reset = C("reset")
            for f in range(4):
                dve.wait_ge(S("decay"), f + 1)
                dve.tensor_tensor_scan(cum[:, f], reset, sw[:, f], 0.0, ALU.mult, ALU.add).then_inc(S("cum"), 1)
            dve.wait_ge(S("cum"), 4)
            dve.tensor_tensor(sw[:, :, :], cum[:, :, :], sw[:, :, :], ALU.subtract).then_inc(S("cum"), 1)
            shift(8)
            shift(9)
            dve.wait_ge(S("rate"), 4)
            for f in range(4):
                own.mark(dve.tensor_scalar(bon[:, f], aa[:, f], V("rwkv_k_a_2", 1, f), gain2[:, f:f + 1], ALU.mult, ALU.add))
            own.wait()
            own.after(dve.tensor_tensor(xk, xk, bon[:, :, :], ALU.mult))
            shift(10)
            dve.wait_ge(S("kk_norm"), 2)
            own.after(dve.tensor_scalar(rf[:, :, :], rf[:, :, :], 1e-12, None, ALU.max))
            own.after(dve.reciprocal(rf[:, :, :], rf[:, :, :]))
            own.after(dve.tensor_tensor(kk[:, :, :], kk[:, :, :], rf[:, :, :], ALU.mult))
            shift(11)
            own.after(dve.tensor_tensor(bf[:, :, :], kk[:, :, :], aa[:, :, :], ALU.mult))
            dve.wait_ge(S("shifted"), 10)
            for f in range(4):
                own.mark(dve.scalar_tensor_tensor(aa[:, f], xr[:, f], V("rwkv_r_k_2", 1, f), xk[:, f], ALU.mult, ALU.mult))
            own.wait()
            dve.sem_inc(S("rk"), 1)
            shift(12)
            dve.wait_ge(S("e2"), 1)
            own.mark(dve.tensor_tensor(bf[:, :, :], bf[:, :, :], e2[:, :, :], ALU.mult))
            own.mark(dve.tensor_tensor(kf[:, :, :], xk, e2[:, :, :], ALU.mult))
            own.mark(dve.tensor_tensor(rf[:, :, :], xr, e1[:, :, :], ALU.mult))
            shift(13)
            dve.wait_ge(S("e3"), 1)
            own.after(dve.scalar_tensor_tensor(zf[:, :, :].rearrange("p a b -> p (a b)"), kk[:, :, :].rearrange("p a b -> p (a b)"), -1.0,
                                               sw[:, :, :].rearrange("p a b -> p (a b)"), ALU.mult, ALU.mult))
            dve.sem_inc(S("factors"), 1)
            dve.wait_ge(S("shifted"), 14)
            for f in range(2):
                dve.wait_ge(S("bonus_sum"), f + 1)
                own.mark(dve.tensor_tensor(bon[:, 2 * f:2 * f + 2], bank[4 + f][:, :].rearrange("p (a t) -> p a t", a=2), xv[:, 2 * f:2 * f + 2], ALU.mult))
            own.wait()
            dve.sem_inc(S("bonus_read"), 1)
            dve.wait_ge(S("mix_taken"), 18)
            for n in range(4):
                dve.wait_ge(chunk_used, MIX + 18 + n + 1)
                own.after(dve.tensor_tensor(cy[:, n, 30:286], bank[n % 2][:, 0:TOK], sgb[:, n], ALU.mult))
                dve.sem_inc(S("conv_in"), 1)
            for f in range(4):
                dve.tensor_scalar(co[:, f], cy[:, f, 0:256], V("conv_dw_w_2", 1, 31 * f), V("conv_dw_b_2", 1, f), ALU.mult, ALU.add)\
                   .then_inc(S("conv_begun"), 1)
            taps = iter(range(1, 31))

            def conv_taps(count):
                for _, tap in zip(range(count), taps):
                    dve.wait_ge(S("conv_begun"), 3 + tap)
                    dve.scalar_tensor_tensor(co[:, 3], cy[:, 3, tap:tap + 256], V("conv_dw_w_2", 1, 31 * 3 + tap), co[:, 3], ALU.mult, ALU.add)\
                       .then_inc(S("conv_begun"), 1)

            def mask(name):
                return C(name).rearrange("p (a s) -> p a s", a=1).broadcast_to([P, 4, 128])

            dve.wait_ge(S("tok_major"), 8)
            for n, (kind, dst) in enumerate(GRAM):
                for b in range(4):
                    dve.wait_ge(S("gram"), 4 * n + b + 1)
                    src = bank[2 * b + n % 2][:, :].rearrange("p (h s) -> p h s", h=4)
                    for d_, m in dst:
                        ins_ = dve.tensor_tensor(dict(AK=AK, RB=RB, RK=RK, **MAT)[d_][:, b], src, mask(m), ALU.mult)
                        own.mark(ins_)
                    own.wait()
                    dve.sem_inc(S("gram_masked"), 1)
            for b in range(4):
                own.mark(dve.tensor_tensor(R_[:, b], DU[:, b], ident.rearrange("p (a s) -> p a s", a=1).broadcast_to([P, 4, 128]), ALU.add))
            own.wait()
            dve.sem_inc(S("neu_start"), 1)
            for s, step in enumerate(NEUMANN):
                for b in range(4):
                    for k, (lhs, rhs, dst, how) in enumerate(step):
                        if how == "act":
                            continue
                        dve.wait_ge(S("neu_prod"), PROD[s, b, k])
                        src = bank[2 * b + k][:, :].rearrange("p (h s) -> p h s", h=4)
                        if how == "copy":
                            dve.tensor_copy(MAT[dst][:, b], src).then_inc(S("neu_dve"), 1)
                        elif how == "eye":
                            dve.tensor_tensor(MAT[dst][:, b], src, ident.rearrange("p (a s) -> p a s", a=1).broadcast_to([P, 4, 128]), ALU.add)\
                               .then_inc(S("neu_dve"), 1)
                        else:
                            dve.tensor_tensor(MAT[dst][:, b], src, MAT[rhs][:, b], ALU.add).then_inc(S("neu_dve"), 1)
                        conv_taps(1)
            conv_taps(31)
            for f in range(4):
                own.after(dve.scalar_tensor_tensor(bon[:, f], bon[:, f], V("rwkv_gn_b_2", 1, f), gg[:, f], ALU.add, ALU.mult))
                own.mark(dve.tensor_scalar(gg[:, f], gg[:, f], V("rwkv_gn_w_2", 1, f), None, ALU.mult))
            for t in range(2):
                dve.wait_ge(S("m1_prod"), t + 1)
                dve.tensor_copy(m1[:, t], bank[t][:, :]).then_inc(S("m1"), 1)
            for t in range(2):
                dve.wait_ge(S("w1_prod"), t + 1)
                dve.tensor_copy(w1[:, t], bank[4 + t][:, :]).then_inc(S("w1"), 1)
            for c in range(4):
                dve.wait_ge(S("phi_prod"), c + 1)
                src = bank[c][:, 0:TOK].rearrange("p (f j) -> p f j", f=4)
                dve.tensor_tensor(phi[:, c], src, C("eye64").rearrange("p (a s) -> p a s", a=1).broadcast_to([P, 4, 64]), ALU.add)\
                   .then_inc(S("phi"), 1)

            def decay_of(c):
                return e1[:, :, 64 * c + 63:64 * c + 64].broadcast_to([P, 4, 64])

            for c in range(4):
                dve.wait_ge(S("u_prod"), c + 1)
                src = bank[4 + c][:, 0:TOK].rearrange("p (f j) -> p f j", f=4)
                own.mark(dve.tensor_tensor(u0[:, c], src, decay_of(c), ALU.mult))
            own.after(dve.memset(st[:, 0], 0.0))
            dve.tensor_copy(st[:, 1], u0[:, 0]).then_inc(S("state"), 1)
            dve.wait_ge(S("ln_mean"), 1)
            for f in range(4):
                dve.scalar_tensor_tensor(co[:, f], bank[1][:, 0:TOK], -1.0 / 512, co[:, f], ALU.mult, ALU.add).then_inc(S("ln_centred"), 1)
            for c in range(1, 3):
                dve.wait_ge(S("phi_state"), c)
                src = bank[0][:, 0:TOK].rearrange("p (f j) -> p f j", f=4)
                own.after(dve.tensor_tensor(st[:, c + 1], src, decay_of(c), ALU.mult))
                dve.tensor_tensor(st[:, c + 1], st[:, c + 1], u0[:, c], ALU.add).then_inc(S("state"), 1)
            for t in range(2):
                dve.wait_ge(S("sa_prod"), t + 1)
                for e in range(2):
                    half = (x.rearrange("p (f e i) -> p e f i", f=4, e=2)[:, e] for x in (sa[:, t], m2[:, t]))
                    dve.tensor_tensor(next(half), bank[4 + 2 * t + e][:, 0:TOK].rearrange("p (f i) -> p f i", f=4), next(half), ALU.add)\
                       .then_inc(S("sa"), 1)
            dve.wait_ge(S("ln_std"), 1)
            own.after(dve.reciprocal(rstd2, rstd2))
            for f in range(4):
                dve.tensor_tensor(co[:, f], co[:, f], rstd2, ALU.mult).then_inc(S("ln_y"), 1)
            for f in range(2):
                dve.wait_ge(S("y_mean"), f + 1)
                v = slice(2 * f, 2 * f + 2)
                dve.scalar_tensor_tensor(yy[:, v].rearrange("p a b -> p (a b)"), bank[2 + f][:, :], -1.0 / 64,
                                         yy[:, v].rearrange("p a b -> p (a b)"), ALU.mult, ALU.add).then_inc(S("y_centred"), 1)
            dve.wait_ge(S("y_centred"), 2)
            own.mark(dve.tensor_tensor(yf[:, :, :], yy[:, :, :], gg[:, :, :], ALU.mult))
            for f in range(4):
                dve.wait_ge(S("mix_hi"), f + 1)
                dve.tensor_tensor(x_lo[:, f], co[:, f], x_hi[:, f].bitcast(F32), ALU.subtract).then_inc(S("mix_lo"), 1)
            for f in range(2):
                v = slice(2 * f, 2 * f + 2)
                dve.wait_ge(S("y_std"), f + 1)
                own.after(dve.reciprocal(ysq[:, v], ysq[:, v]))
                own.after(dve.tensor_tensor(yf[:, v], yf[:, v], ysq[:, v], ALU.mult))
                dve.tensor_tensor(yf[:, v], yf[:, v], bon[:, v], ALU.add).then_inc(S("y_done"), 1)
            for f in range(4):
                dve.wait_ge(S("mix_hi"), 5 + f)
                dve.tensor_tensor(x_lo[:, 4 + f], yf[:, f], x_hi[:, 4 + f].bitcast(F32), ALU.subtract).then_inc(S("mix_lo"), 1)
            dve.wait_ge(lo_ready, W_OUT2 + AHEAD)
            for k in range(KT):
                split(W_OUT2 + k + AHEAD)
                dve.wait_ge(chunk_used, W_OUT2 + k + 1)
                dve.scalar_tensor_tensor(xres[:, k], bank[k % 4][:, 0:TOK], mod[:, 16 + k:17 + k], xres[:, k], ALU.mult, ALU.add)\
                   .then_inc(S("x_mixed2"), 1)
            dve.wait_ge(S("x_mixed2"), KT)
            norm(3, gain, mod[:, 24:32])
            splits(W_Q, 16)
            def top16(values, out_v, out_i):
                own.after(dve.max(out_v[0], values))
                own.after(dve.max_index(out_i[0], out_v[0], values))
                own.after(dve.match_replace(values, out_v[0], values, -3.0e38))
                own.after(dve.max(out_v[1], values))
                own.after(dve.max_index(out_i[1], out_v[1], values))

            idx_u = idx.bitcast(U32)
            pos_u = pos.bitcast(U32)
            for n in range(32):
                a, b = n // 16, n % 16
                dve.wait_ge(S("scores"), 4 * a + b // 4 + 1)
                top16(s_sb[:, a, b], [vals[:, a, b, 0:8], vals[:, a, b, 8:16]], [idx_u[:, a, b, 0:8], idx_u[:, a, b, 8:16]])
            own.after(dve.tensor_copy(idf[:, :, :, :], idx_u[:, :, :, :]))
            for a in range(2):
                for h in range(8):
                    c3 = cand[:, a, h].rearrange("p (x y) -> p x y", x=16)
                    v0 = vals[:, a, 2 * h].rearrange("p (x y) -> p x y", y=1).broadcast_to([P, 16, 16])
                    v1 = vals[:, a, 2 * h + 1].rearrange("p (x y) -> p x y", x=1).broadcast_to([P, 16, 16])
                    own.after(dve.tensor_tensor(c3, v0, v1, ALU.add))
                    top16(cand[:, a, h], [best[:, a, h, 0:8], best[:, a, h, 8:16]], [pos_u[:, a, h, 0:8], pos_u[:, a, h, 8:16]])
            own.after(dve.tensor_tensor(gate[:, :, :, :], best[:, :, :, :], best[:, :, :, 0:1].broadcast_to([P, 2, 8, 16]), ALU.subtract))
            dve.sem_inc(S("best_shifted"), 1)
            pu = poshu.bitcast(U32)
            own.mark(dve.tensor_scalar(pu[:, 0], pos_u[:, :, :, :], 4, None, ALU.logical_shift_right))
            own.after(dve.tensor_scalar(pu[:, 1], pos_u[:, :, :, :], 15, None, ALU.bitwise_and))
            own.after(dve.tensor_copy(poshl[:, :, :, :, :], pu[:, :, :, :, :]))
            for c in range(2):
                for a in range(2):
                    d_ = poshl[:, c, a].rearrange("p h (k y) -> p h k y", y=1).broadcast_to([P, 8, 16, 16])
                    lst = idf[:, a].rearrange("p (h c) j -> p c h j", c=2)[:, c]
                    for h in range(8):
                        own.mark(dve.tensor_tensor(onehot[:, h], iota[:, 0:16].rearrange("p (x y) -> p x y", x=1).broadcast_to([P, 16, 16]),
                                                   d_[:, h], ALU.is_equal))
                    own.wait()
                    for h in range(8):
                        own.mark(dve.tensor_tensor(onehot[:, h], onehot[:, h],
                                                   lst[:, h].rearrange("p (x j) -> p x j", x=1).broadcast_to([P, 16, 16]), ALU.mult))
                    own.wait()
                    own.after(dve.tensor_reduce(isel[:, c, a], onehot[:, :, :, :], AX, ALU.add))
            dve.wait_ge(lo_ready, EXP_U + POOL_SPLITS + AHEAD)
            splits(EXP_U + POOL_SPLITS, TOP_FIRST - POOL_SPLITS)
            dve.wait_ge(S("gate_exp"), 1)
            own.after(dve.tensor_reduce(gsum[:, :, :], gate[:, :, :, :], AX, ALU.add))
            own.after(dve.reciprocal(gsum[:, :, :], gsum[:, :, :]))
            own.after(dve.tensor_tensor(gate[:, :, :, :], gate[:, :, :, :],
                                        gsum.rearrange("p a (h y) -> p a h y", y=1).broadcast_to([P, 2, 8, 16]), ALU.mult))
            dve.sem_inc(S("gate_done"), 1)
            dve.wait_ge(S("routing_turned"), 1)
            dve.tensor_copy(i0T[:, :], bank[4][:, 0:TOK]).then_inc(S("i0T"), 1)
            splits(EXP_U + TOP_FIRST, NKEY - TOP_FIRST)
            def hots(b, i=0):
                if b >= 2:
                    dve.wait_ge(S("dense"), b - 1 + 2 * i)
                for k in range(4):
                    if isinstance(i, int):
                        e, g = (bank[p_][:, off + 4 * b + k:off + 4 * b + k + 1] for p_, off in ((4, 256), (5, 0)))
                    else:
                        e, g = (bank[p_][:, bass.ds(i * 8 + (off + 4 * b + k), 1)] for p_, off in ((4, 256), (5, 0)))
                    ins_ = dve.tensor_scalar(hotB[:, b % 2, k], iota, e, g, ALU.is_equal, ALU.mult)
                ins_.then_inc(S("hotB"), 1)

            def mix(b, i=0):
                dve.wait_ge(S("dense"), b + 1 + 2 * i)
                at = 4 * b
                h3 = arena[:, :].rearrange("p (e t) -> p t e", t=TOK)
                dst = h3[:, at:at + 4] if isinstance(i, int) else h3[:, bass.ds(i * 8 + at, 4)]
                dve.tensor_tensor(dst, bank[b % 2][:, :].rearrange("p (t e) -> p t e", t=4), dst, ALU.mult).then_inc(S("g_mixed"), 1)

            dve.wait_ge(S("h_taken"), NKEY)
            dve.wait_ge(S("routing_turned"), 1)
            dve.wait_ge(S("spilled"), 16)
            hots(0)
            hots(1)
            with dve.Fori(0, 31) as i:
                for b in range(2):
                    mix(b, i)
                    hots(b + 2, i)
            mix(62)
            mix(63)

            def v_lo(n, i=0):
                at = n * TOK
                src = arena[:, at:at + TOK] if isinstance(i, int) else arena[:, bass.ds(i * 1024 + at, TOK)]
                dve.wait_ge(S("g_hi"), n + 1 + 4 * i)
                dve.tensor_tensor(x_lo[:, n % 4], src, x_hi[:, n % 4].bitcast(F32), ALU.subtract).then_inc(S("g_lo"), 1)

            for n in range(3):
                v_lo(n)
            with dve.Fori(0, NKEY // 4 - 1) as i:
                for p in range(4):
                    split(EXP_V + p + AHEAD, i)
                    v_lo(p + 3, i)
            for p in range(4):
                n = NKEY - 4 + p
                split(EXP_V + n + AHEAD)
                if n + 3 < NKEY:
                    v_lo(n + 3)
            dve.wait_ge(chunk_used, CHUNKS)
            dve.wait_ge(S("x_back"), 16)
            for k in range(KT):
                dve.scalar_tensor_tensor(xres[:, k], bank[4 + k // 2][:, (k % 2) * TOK:(k % 2) * TOK + TOK], mod[:, 40 + k:41 + k],
                                         xres[:, k], ALU.mult, ALU.add).then_inc(S("x_final"), 1)
            dve.wait_ge(S("norm_std"), 5)
            fr = arena[:, 4096:4096 + TOK]
            own.after(dve.reciprocal(fr, fr))
            for k in range(KT):
                own.mark(dve.scalar_tensor_tensor(arena[:, k * TOK:k * TOK + TOK], xres[:, k], V("final_g_2", 1, k), fr, ALU.mult, ALU.mult))
            own.wait()
            dve.sem_inc(S("out_ready"), 1)

        @block.gpsimd
        def _(pool):
            own = Chain(pool, S("pool_step"))

            def lo_part(b, i=0):
                pool.wait_ge(hi_ready, b + 1 + RING * i)
                pool.wait_ge(chunk_used, b - RING + 1 + RING * i)
                pool.tensor_tensor(w_lo[:, b % RING], raw[:, b % RING], w_hi[:, b % RING].bitcast(F32), ALU.subtract)\
                    .then_inc(lo_ready, 1)

            pool.wait_ge(S("tile_taken"), 16)
            pool.wait_ge(S("consts_landed"), 16)
            own.after(pool.tensor_tensor(pw1[:, :, 1:272], upool[:, :, 1:272], upool[:, :, 0:271], ALU.add))
            own.after(pool.tensor_tensor(pw2[:, 1:4, 3:272], pw1[:, 1:4, 3:272], pw1[:, 1:4, 1:270], ALU.add))
            own.after(pool.tensor_tensor(pw1[:, 2:4, 7:272], pw2[:, 2:4, 7:272], pw2[:, 2:4, 3:268], ALU.add))
            own.after(pool.tensor_tensor(pw2[:, 3:4, 15:272], pw1[:, 3:4, 15:272], pw1[:, 3:4, 7:264], ALU.add))
            ic = C("inv_count").rearrange("p (g t) -> p g t", g=4)
            for g, w in enumerate((pw1, pw2, pw1, pw2)):
                own.mark(pool.tensor_tensor(w[:, g, 16:272], w[:, g, 16:272], ic[:, g], ALU.mult))
            own.wait()
            for g, w in enumerate((pw1, pw2, pw1, pw2)):
                own.mark(pool.tensor_tensor(w[:, g, 16:272], w[:, g, 16:272], upool[:, g, 16:272], ALU.subtract))
            own.wait()
            pool.sem_inc(S("pooled"), 1)
            pool.wait_ge(lo_ready, MIX + AHEAD)
            with pool.Fori(0, 5) as i:
                for p in range(RING):
                    lo_part(MIX + p + AHEAD, i)
            for p in range(20, 22):
                lo_part(MIX + p + AHEAD)
            pool.wait_ge(S("conv_begun"), 3)
            weight = V("conv_dw_w_2", 4 * 31).rearrange("p (f k) -> p f k", f=4)
            for tap in range(1, 31):
                own.after(pool.tensor_tensor(tap_product, cy[:, 0:3, tap:tap + 256], weight[:, 0:3, tap:tap + 1].broadcast_to([P, 3, TOK]), ALU.mult))
                own.after(pool.tensor_tensor(co[:, 0:3], co[:, 0:3], tap_product, ALU.add))
            pool.sem_inc(S("conv_out"), 1)
            pool.wait_ge(lo_ready, EXP_U + AHEAD)
            with pool.Fori(0, POOL_SPLITS // RING) as i:
                for p in range(RING):
                    lo_part(EXP_U + p + AHEAD, i)
            def hots(b, i=0):
                if b >= 2:
                    pool.wait_ge(S("hot_sq"), b - 1 + 2 * i)
                src = i0T[:, 4 * b:4 * b + 4] if isinstance(i, int) else i0T[:, bass.ds(i * 8 + 4 * b, 4)]
                pool.tensor_tensor(hot_d[:, b % 2], iota.rearrange("p (a s) -> p a s", a=1).broadcast_to([P, 4, 128]),
                                   src.rearrange("p (a s) -> p a s", s=1).broadcast_to([P, 4, 128]), ALU.subtract)\
                    .then_inc(S("hot_diff"), 1)

            pool.wait_ge(S("i0T"), 1)
            pool.wait_ge(S("h_taken"), NKEY)
            hots(0)
            hots(1)
            with pool.Fori(0, 31) as i:
                for b in range(2):
                    hots(b + 2, i)

        @block.tensor
        def _(pe):
            def three(o, w, wl, xh, xl, start, stop_):
                pe.matmul(o, w, xh, start=start, stop=False, skip_group_check=True)
                pe.matmul(o, w, xl, start=False, stop=False, skip_group_check=True)
                return pe.matmul(o, wl, xh, start=False, stop=stop_, skip_group_check=True)

            def reduce(b, o, i=0, per=RING, xh=x_hi, xl=x_lo):
                s = b % RING
                pe.wait_ge(lo_ready, b + 1 + per * i)
                for k in range(KT):
                    c = slice(k * P, k * P + P)
                    m = three(o, w_hi[:, s, c], w_lo[:, s, c], xh[:, k], xl[:, k], k == 0, k == KT - 1)
                m.then_inc(chunk_used, 1)

            def spread(b, banks, xh, xl, first, last, i=0, per=RING):
                s = b % RING
                pe.wait_ge(lo_ready, b + 1 + per * i)
                for n in range(8):
                    c = slice(n * P, n * P + P)
                    o = banks[n // 2][:, (n % 2) * TOK:(n % 2) * TOK + TOK]
                    m = three(o, w_hi[:, s, c], w_lo[:, s, c], xh, xl, first and n % 2 == 0, last)
                m.then_inc(chunk_used, 1)

            ada_steps = iter(range(ADA))

            def modulation(count):
                for _, n in zip(range(count), ada_steps):
                    pe.wait_ge(ada_landed[n % ADA_RING], 16 * (n // ADA_RING + 1))
                    k = n % KT
                    if k == 0 and n:
                        pe.wait_ge(S("ada_read"), n // KT)
                    for e in range(2):
                        m = pe.matmul(bank[6 + e][:, :], c_wide[:, k], ada_raw[:, n % ADA_RING, e * 512:e * 512 + 512],
                                      start=k == 0, stop=k == KT - 1)
                    m.then_inc(S("ada_used"), 1)

            def sum_squares(n, k, s_):
                pe.wait_ge(S("norm_sq"), KT * n + k + 1)
                m = pe.matmul(bank[7][:, 0:TOK], ones, s_[:, k], start=k == 0, stop=k == KT - 1, skip_group_check=True)
                if k == KT - 1:
                    m.then_inc(S("norm_ssq"), 1)

            def sum_summed(n, s_):
                pe.wait_ge(S("norm_sum"), n)
                pe.matmul(bank[7][:, 0:TOK], ones, s_[:, 0], start=True, stop=True).then_inc(S("norm_ssq"), 1)

            def reduce_fresh(b, o, ready, before=0):
                s = b % RING
                pe.wait_ge(lo_ready, b + 1)
                for k in range(KT):
                    pe.wait_ge(S(ready), before + k + 1)
                    c = slice(k * P, k * P + P)
                    m = three(o, w_hi[:, s, c], w_lo[:, s, c], x_hi[:, k], x_lo[:, k], k == 0, k == KT - 1)
                m.then_inc(chunk_used, 1)

            pe.wait_ge(S("kept_landed"), 16)
            sum_summed(1, sq)
            reduce_fresh(0, bank[0][:, 0:TOK], "norm_lo")
            for j in range(1, 4):
                reduce(j, bank[j][:, 0:TOK])
            with pe.Fori(0, 7) as i:
                for p in range(4):
                    pe.wait_ge(S("tile_taken"), p + 1 + 4 * i)
                    reduce(4 + p, bank[p][:, 0:TOK], i)
            pe.wait_ge(S("pooled"), 1)
            pe.wait_ge(S("wpool_landed"), 16)
            for g, w in enumerate((pw1, pw2, pw1, pw2)):
                m = pe.matmul(bank[6 + g // 2][:, (g % 2) * TOK:(g % 2) * TOK + TOK], wpool[:, g], w[:, g, 16:272], start=True, stop=True)
            m.then_inc(S("pool_mixed"), 1)
            pe.wait_ge(S("consts_landed"), 16)
            pe.wait_ge(S("tile_taken"), 32)
            for n in range(8):
                pe.wait_ge(S("qk_sq"), n // 2 + 1)
                m = pe.matmul(bank[2 + n // 2][:, (n % 2) * TOK:(n % 2) * TOK + TOK], C("head"), sq[:, n], start=True, stop=True)
                if n % 2:
                    m.then_inc(S("qk_ssq"), 1)
            for t in range(2):
                for f in range(4):
                    m = pe.transpose(bank[t][:, f * P:f * P + P], qkv[:, 8 + f, t * P:t * P + P], ident)
                m.then_inc(S("v_turned"), 1)
            pe.wait_ge(S("c_wide"), KT)
            pe.wait_ge(S("pool_lo"), 4)
            modulation(ADA_BEFORE_ROT)
            for n in range(8):
                pe.wait_ge(S("qk_normed"), n // 4 + 1)
                m = pe.matmul(bank[2 + n // 2][:, (n % 2) * TOK:(n % 2) * TOK + TOK], C("rot"), rs[:, n], start=True, stop=True)
                if n % 2:
                    m.then_inc(S("qk_turned"), 1)

            def score(h):
                f, p0, b = h // 2, 64 * (h % 2), h % 2
                if h >= 2:
                    pe.wait_ge(S("neg_max"), h - 1)
                r = slice(p0, p0 + 64)
                pe.matmul(bank[b][:, 0:128], qkv[r, f, 0:128], qkv[r, 4 + f, 0:128], start=True, stop=True)
                pe.matmul(bank[b][:, 128:384], qkv[r, f, 128:256], qkv[r, 4 + f, :], start=True, stop=True)\
                  .then_inc(S("qk_scored"), 1)

            def turn(h):
                b = h % 2
                pe.wait_ge(S("p_rows"), h + 1)
                if h >= 2:
                    pe.wait_ge(S("pT"), h - 1)
                for n in range(3):
                    m = pe.transpose(bank[2 + b][:, n * P:n * P + P], pex[:, b, n * P:n * P + P], ident)
                m.then_inc(S("p_turned"), 1)

            def attend(h):
                f, p0, b = h // 2, 64 * (h % 2), h % 2
                pe.wait_ge(S("pT"), h + 1)
                o = bank[4 + f // 2][p0:p0 + 64, (f % 2) * TOK:(f % 2) * TOK + TOK]
                v = slice(h * 64, h * 64 + 64)
                pe.matmul(o[:, 0:128], v_tok[:, 0, v], pT[:, b, 0:128], start=True, stop=True)
                pe.matmul(o[:, 128:256], v_tok[:, 0, v], pT[:, b, 128:256], start=True, stop=False)
                pe.matmul(o[:, 128:256], v_tok[:, 1, v], pT[:, b, 256:384], start=False, stop=True).then_inc(S("head_out"), 1)

            modulation(ADA_BEFORE_SCORES)
            pe.wait_ge(S("qk_rotated"), 4)
            pe.wait_ge(S("v_tok"), 2)
            score(0)
            for h in range(HEADS):
                if h + 1 < HEADS:
                    score(h + 1)
                modulation(2)
                turn(h)
                modulation(2)
                attend(h)
                modulation(ADA_PER_HEAD - 4)
            for k in range(4):
                pe.wait_ge(S("attn_lo"), 4)
                spread(BRANCH + k, bank[0:4], x_hi[:, k], x_lo[:, k], k == 0, k == 3)
            pe.wait_ge(S("ada_read"), ADA // KT)
            for k in range(4):
                spread(BRANCH + 4 + k, bank[4:8], x_hi[:, 4 + k], x_lo[:, 4 + k], k == 0, k == 3)
            reduce_fresh(W_OUT, bank[0][:, 0:TOK], "mixed_lo")
            for k in range(1, KT):
                if k >= 4:
                    pe.wait_ge(S("x_added"), k - 3)
                reduce(W_OUT + k, bank[k % 4][:, 0:TOK])
                if k >= 2:
                    sum_squares(1, k - 2, sq)
            sum_squares(1, KT - 2, sq)
            sum_squares(1, KT - 1, sq)
            reduce_fresh(FFN, bank[0][:, 0:TOK], "norm_lo", KT)
            reduce(FFN + 1, bank[1][:, 0:TOK])

            def ffn_step(q, i=0):
                b = FFN + 3 * q - 1
                for h in range(2):
                    pe.wait_ge(S("up_taken"), 2 * q - 1 + h + 8 * i)
                    reduce(b + h, bank[h][:, 0:TOK], i, 12)
                pe.wait_ge(S("ffn_lo"), q + 4 * i)
                spread(b + 2, bank[4:8], f_hi[:, :], f_lo[:, :], q == 1, False, i, 12)

            ffn_step(1)
            with pe.Fori(0, (NF - 2) // 4) as i:
                for q in range(2, 6):
                    ffn_step(q, i)
            pe.wait_ge(S("ffn_lo"), NF)
            spread(MIX - 1, bank[4:8], f_hi[:, :], f_lo[:, :], False, True)
            sum_summed(2, sq3)
            reduce_fresh(MIX, bank[0][:, 0:TOK], "norm_lo", 2 * KT)
            reduce(MIX + 1, bank[1][:, 0:TOK])

            def mix(n0, n1):
                for n in range(n0, n1):
                    if n < 20:
                        pe.wait_ge(S("mix_taken"), n - 1)
                    else:
                        pe.wait_ge(S("conv_in"), n - 19)
                    reduce(MIX + n, bank[n % 2][:, 0:TOK])

            mix(2, 7)
            pe.wait_ge(S("lora_in"), 1)
            pe.wait_ge(S("lora_landed"), 16)
            for f in range(4):
                pe.matmul(bank[2 + f // 2][:, (f % 2) * TOK:(f % 2) * TOK + TOK], lora_sb[0:64, f * P:f * P + P], xs[0:64, 0], start=True, stop=True)
            for f in range(4):
                m = pe.matmul(bank[4 + f // 2][:, (f % 2) * TOK:(f % 2) * TOK + TOK], lora_sb[64:128, f * P:f * P + P], xs[64:128, 0],
                              start=True, stop=True)
            m.then_inc(S("lora_out"), 1)
            pe.wait_ge(S("lora_in"), 2)
            for f in range(4):
                m = pe.matmul(bank[6 + f // 2][:, (f % 2) * TOK:(f % 2) * TOK + TOK], lora_sb[:, 512 + f * P:512 + f * P + P], xs[:, 1],
                              start=True, stop=True)
            m.then_inc(S("lora_out"), 1)
            mix(7, 11)
            pe.wait_ge(S("kk_sq"), 1)
            for f in range(4):
                m = pe.matmul(bank[2 + f // 2][:, (f % 2) * TOK:(f % 2) * TOK + TOK], C("head"), rf[:, f], start=True, stop=True)
                if f % 2:
                    m.then_inc(S("kk_ssq"), 1)
            mix(11, 18)
            pe.wait_ge(S("rk"), 1)
            for f in range(4):
                m = pe.matmul(bank[4 + f // 2][:, (f % 2) * TOK:(f % 2) * TOK + TOK], C("head"), aa[:, f], start=True, stop=True)
                if f % 2:
                    m.then_inc(S("bonus_sum"), 1)
            mix(18, 22)
            pe.wait_ge(S("factors"), 1)
            pe.wait_ge(S("kk_norm"), 2)
            pe.wait_ge(S("bonus_read"), 1)
            pe.wait_ge(S("g_out"), 2)
            for n, src in enumerate((zf, bf, kf, xs[:, 10:14])):
                if n == 3:
                    pe.wait_ge(S("conv_in"), 4)
                for t in range(2):
                    for f in range(4):
                        m = pe.transpose(bank[(2 * n + 2 + t) % 8][:, f * P:f * P + P], src[:, f, t * P:t * P + P], ident)
                    m.then_inc(S("turned"), 1)
            pe.wait_ge(S("tok_major"), 8)
            feat = dict(Z=zf, B=bf, K=kf, R=rf)

            def fm(x, b, k):
                t, p0 = b // 2, 64 * (b % 2)
                return x[p0:p0 + 64, k, t * P:t * P + P]

            for n, ((l, r), _) in enumerate(GRAM):
                for b in range(4):
                    if n >= 2:
                        pe.wait_ge(S("gram_masked"), 4 * (n - 2) + b + 1)
                    for k in range(4):
                        m = pe.matmul(bank[2 * b + n % 2][:, k * P:k * P + P], fm(feat[l], b, k), fm(feat[r], b, k), start=True, stop=True)
                    m.then_inc(S("gram"), 1)
            pe.wait_ge(S("neu_start"), 1)
            for s, step in enumerate(NEUMANN):
                for b in range(4):
                    if s > 0:
                        nd, na = DONE[s, b]
                        if nd:
                            pe.wait_ge(S("neu_dve"), nd)
                        if na:
                            pe.wait_ge(S("neu_act"), na)
                    for k, (lhs, rhs, dst, how) in enumerate(step):
                        for u in range(4):
                            o = bank[2 * b + k][:, u * P:u * P + P]
                            if rhs == "turn":
                                m = pe.transpose(o, MAT[lhs][:, b, u], ident)
                            else:
                                m = pe.matmul(o, MAT[lhs][:, b, u], MAT[rhs][:, b, u], start=True, stop=True)
                        m.then_inc(S("neu_prod"), 1)
            pe.wait_ge(S("neu_act"), sum(h == "act" for s_ in NEUMANN for *_, h in s_) * 4)
            for t in range(2):
                for h in range(8):
                    b, k = 2 * t + h % 2, h // 2
                    m = pe.matmul(bank[t][:, h * 64:h * 64 + 64], R_[:, b, k], zt[:, t, h * 64:h * 64 + 64], start=True, stop=True)
                m.then_inc(S("m1_prod"), 1)
            for t in range(2):
                for h in range(8):
                    b, k, p0 = 2 * t + h % 2, h // 2, 64 * (h % 2)
                    m = pe.matmul(bank[2 + t][p0:p0 + 64, (h // 2) * P:(h // 2) * P + P], zt[:, t, h * 64:h * 64 + 64], R_[:, b, k],
                                  start=True, stop=True)
                m.then_inc(S("m1T_prod"), 1)
            for t in range(2):
                for h in range(8):
                    b, k = 2 * t + h % 2, h // 2
                    m = pe.matmul(bank[4 + t][:, h * 64:h * 64 + 64], AK[:, b, k], vt[:, t, h * 64:h * 64 + 64], start=True, stop=True)
                m.then_inc(S("w1_prod"), 1)
            for t in range(2):
                pe.wait_ge(S("w1"), t + 1)
                for h in range(8):
                    b, k = 2 * t + h % 2, h // 2
                    m = pe.matmul(bank[6 + t][:, h * 64:h * 64 + 64], R_[:, b, k], w1[:, t, h * 64:h * 64 + 64], start=True, stop=True)
                m.then_inc(S("m2_prod"), 1)
            pe.wait_ge(S("m1"), 2)
            pe.wait_ge(S("m1T"), 2)
            for c in range(4):
                t, r = c // 2, slice(64 * (c % 2), 64 * (c % 2) + 64)
                for h in range(8):
                    o = bank[c][64 * (h % 2):64 * (h % 2) + 64, (h // 2) * 64:(h // 2) * 64 + 64]
                    v = slice(h * 64, h * 64 + 64)
                    m = pe.matmul(o, m1[r, t, v], bt[r, t, v], start=True, stop=True)
                m.then_inc(S("phi_prod"), 1)
            pe.wait_ge(S("m2"), 2)
            for c in range(4):
                t, r = c // 2, slice(64 * (c % 2), 64 * (c % 2) + 64)
                for h in range(8):
                    o = bank[4 + c][64 * (h % 2):64 * (h % 2) + 64, (h // 2) * 64:(h // 2) * 64 + 64]
                    v = slice(h * 64, h * 64 + 64)
                    pe.matmul(o, bt[r, t, v], m2[r, t, v], start=True, stop=False)
                    m = pe.matmul(o, kt_[r, t, v], vt[r, t, v], start=False, stop=True)
                m.then_inc(S("u_prod"), 1)
            pe.wait_ge(S("phi"), 4)
            pe.wait_ge(S("w1"), 2)
            pe.wait_ge(S("conv_out"), 1)
            pe.wait_ge(S("conv_begun"), 34)
            for f in range(4):
                m = pe.matmul(bank[1][:, 0:TOK], ones, co[:, f], start=f == 0, stop=f == 3)
            m.then_inc(S("ln_mean"), 1)
            for c in range(1, 3):
                pe.wait_ge(S("state"), c)
                for h in range(8):
                    r = slice(64 * (h % 2), 64 * (h % 2) + 64)
                    m = pe.matmul(bank[0][r, (h // 2) * 64:(h // 2) * 64 + 64], phi[r, c, h // 2], st[r, c, h // 2], start=True, stop=True)
                m.then_inc(S("phi_state"), 1)
            pe.wait_ge(S("ln_sq"), 4)
            for f in range(4):
                m = pe.matmul(bank[1][:, 0:TOK], ones, cy[:, f, 0:TOK], start=f == 0, stop=f == 3)
            m.then_inc(S("ln_var"), 1)
            pe.wait_ge(S("state"), 3)
            for c in range(4):
                t = c // 2
                for h in range(8):
                    r = slice(64 * (h % 2), 64 * (h % 2) + 64)
                    m = pe.matmul(bank[4 + 2 * t + h % 2][64 * (c % 2):64 * (c % 2) + 64, (h // 2) * 64:(h // 2) * 64 + 64], m1T[r, h // 2, 64 * c:64 * c + 64],
                                  st[r, c, h // 2], start=True, stop=True)
                if c % 2:
                    m.then_inc(S("sa_prod"), 1)
            pe.wait_ge(S("ln_std"), 1)
            for h in range(8):
                r, f = slice(64 * (h % 2), 64 * (h % 2) + 64), h // 2
                for t in range(2):
                    pe.wait_ge(S("sa"), 2 * t + 2)
                    o = bank[f // 2][r, (f % 2) * TOK + t * P:(f % 2) * TOK + t * P + P]
                    b, k, v = 2 * t + h % 2, h // 2, slice(h * 64, h * 64 + 64)
                    for c in range(2):
                        pe.matmul(o[:, 64 * c:64 * c + 64], st[r, 2 * t + c, f], rf[r, f, t * P + 64 * c:t * P + 64 * c + 64],
                                  start=c == 0, stop=False, skip_group_check=True)
                    pe.matmul(o, sa[:, t, v], RB[:, b, k], start=False, stop=False, skip_group_check=True)
                    m = pe.matmul(o, vt[:, t, v], RK[:, b, k], start=False, stop=True, skip_group_check=True)
            m.then_inc(S("y_prod"), 1)
            for f in range(4):
                pe.wait_ge(S("y_out"), f // 2 + 1)
                m = pe.matmul(bank[2 + f // 2][:, (f % 2) * TOK:(f % 2) * TOK + TOK], C("head"), yy[:, f], start=True, stop=True)
                if f % 2:
                    m.then_inc(S("y_mean"), 1)
            pe.wait_ge(S("y_sq"), 1)
            for f in range(4):
                m = pe.matmul(bank[4 + f // 2][:, (f % 2) * TOK:(f % 2) * TOK + TOK], C("head"), ysq[:, f], start=True, stop=True)
                if f % 2:
                    m.then_inc(S("y_var"), 1)
            reduce_fresh(W_OUT2, bank[0][:, 0:TOK], "mix_lo")
            for k in range(1, KT):
                if k >= 4:
                    pe.wait_ge(S("x_mixed2"), k - 3)
                reduce(W_OUT2 + k, bank[k % 4][:, 0:TOK])
                if k >= 2:
                    sum_squares(3, k - 2, sq3)
            sum_squares(3, KT - 2, sq3)
            sum_squares(3, KT - 1, sq3)
            reduce_fresh(W_Q, bank[0][:, 0:TOK], "norm_lo", 3 * KT)
            for j in range(1, 16):
                if j >= 4:
                    pe.wait_ge(S("q_taken"), j - 3)
                reduce(W_Q + j, bank[j % 4][:, 0:TOK])
            pe.wait_ge(S("q_taken"), 16)
            pe.wait_ge(S("keys_landed"), 16)
            for n in range(8):
                for k in range(4):
                    b = 4 * (n % 4) + k
                    m = pe.matmul(bank[n][:, k * P:k * P + P], qT[:, b, (n // 4) * P:(n // 4) * P + P], keys[:, b], start=True, stop=True)
                m.then_inc(S("scored"), 1)
            pe.wait_ge(S("scores"), 8)
            for j in range(4):
                reduce(EXP_U + j, bank[j][:, 0:TOK])
            def h_loop(n0, count):
                with pe.Fori(0, count // 4) as i:
                    for p in range(4):
                        pe.wait_ge(S("h_taken"), n0 - 3 + p + 4 * i)
                        reduce(EXP_U + n0 + p, bank[p][:, 0:TOK], i)

            h_loop(4, TOP_FIRST - 4)
            pe.wait_ge(S("gate_done"), 1)
            for c in range(2):
                for a in range(2):
                    pe.transpose(bank[4][:, c * TOK + a * P:c * TOK + a * P + P], isel[:, c, a].rearrange("p h k -> p (h k)"), ident)
            for a in range(2):
                m = pe.transpose(bank[5][:, a * P:a * P + P], gate[:, a].rearrange("p h k -> p (h k)"), ident)
            m.then_inc(S("routing_turned"), 1)
            h_loop(TOP_FIRST, NKEY - TOP_FIRST)
            def dense(b, i=0):
                pe.wait_ge(S("hotA"), b + 1 + 2 * i)
                pe.wait_ge(S("hotB"), b + 1 + 2 * i)
                if b >= 2:
                    pe.wait_ge(S("g_mixed"), b - 1 + 2 * i)
                for k in range(4):
                    m = pe.matmul(bank[b % 2][:, k * P:k * P + P], hotA[:, b % 2, k], hotB[:, b % 2, k], start=True, stop=True)
                m.then_inc(S("dense"), 1)

            pe.wait_ge(S("h_taken"), NKEY)
            dense(0)
            dense(1)
            with pe.Fori(0, 31) as i:
                for b in range(2):
                    dense(b + 2, i)
            def v_step(n, i=0, first=False, last=False):
                pe.wait_ge(S("g_lo"), n + 1 + 4 * i)
                spread(EXP_V + n, bank[4:8], x_hi[:, n % 4], x_lo[:, n % 4], first, last, i)

            v_step(0, first=True)
            for n in range(1, 4):
                v_step(n)
            with pe.Fori(0, NKEY // 4 - 2) as i:
                for p in range(4):
                    v_step(4 + p, i)
            for n in range(NKEY - 4, NKEY):
                v_step(n, last=n == NKEY - 1)
            for k in range(KT):
                pe.wait_ge(S("norm_sq"), 4 * KT + k + 1)
                m = pe.matmul(bank[0][:, 0:TOK], ones, arena[:, 2048 + k * TOK:2304 + k * TOK], start=k == 0, stop=k == KT - 1)
            m.then_inc(S("norm_ssq"), 1)


def constants():
    import numpy as np

    q = np.arange(P)
    p, f = q[:, None], q[None, :]
    c = {"ident": p == f, "ones": np.ones((P, P)), "iota": np.broadcast_to(f, (P, P)), "head": p // 64 == f // 64}
    rot = np.zeros((P, P))
    for h in range(2):
        for d in range(8):
            rot[64 * h + d + 8, 64 * h + d] = -1
            rot[64 * h + d, 64 * h + d + 8] = 1
    c["rot"] = rot
    same16, same64 = p // 16 == f // 16, p // 64 == f // 64
    c["m16u"] = same16 & (p < f)
    c["m16l"] = same16 & (f < p)
    c["mel"] = same64 & ~same16 & (f < p)
    c["msu"] = same64 & (p < f)
    c["miu"] = same64 & (p <= f)
    c["eye64"] = p % 64 == np.arange(64)[None, :]
    t = np.arange(TOK, dtype=np.float32)
    inv = np.float32(500000.0) ** (-np.arange(8, dtype=np.float32) / np.float32(8))
    ang = (t[None, :] * inv[:, None]).astype(np.float32)
    cos, sin = np.ones((64, TOK)), np.zeros((64, TOK))
    cos[0:8] = cos[8:16] = np.cos(ang)
    sin[0:8] = sin[8:16] = np.sin(ang)
    c["cos"], c["sin"] = np.tile(cos, (2, 1)), np.tile(sin, (2, 1))
    c["inv_count"] = np.broadcast_to(np.concatenate([1 / np.minimum(t + 1, w) for w in (2, 4, 8, 16)])[None], (P, 4 * TOK))
    c["reset"] = np.broadcast_to((t % 64 != 0)[None], (P, TOK))
    k = np.arange(TOK)[None, :]
    c["causal"] = np.concatenate([np.where(k[:, 0:P] <= p, 0, -1e30), np.where(k <= P + p, 0, -1e30)], 1)
    return np.concatenate([np.asarray(c[n], np.float32).reshape(P, w) for n, w in CONSTS], 1)


def kernel(**inputs):
    import concourse.bacc as bacc
    import numpy as np
    from concourse.bass_utils import run_bass_kernel_spmd

    g = {k: np.asarray(v) for k, v in inputs.items()}

    def reduce_tiles(w):
        return w.reshape(KT, P, -1, P).transpose(2, 1, 0, 3).reshape(-1, P, CHUNK)

    def columns(v):
        return v.reshape(-1, P).T

    up = reduce_tiles(g["w_up"][0]).reshape(2, NF, P, CHUNK).transpose(1, 0, 2, 3).reshape(2 * NF, P, CHUNK)
    conv_w = g["conv_w"][0].reshape(3, 2, NF, P).transpose(3, 2, 1, 0).reshape(P, -1)
    conv_b = g["conv_b"][0].reshape(2, NF, P).transpose(2, 1, 0).reshape(P, -1)
    order = list(range(20, 22)) + list(range(12, 16)) + list(range(8, 12)) + list(range(16, 20)) + list(range(4, 8)) + list(range(0, 4))
    mu = columns(g["rwkv_mu_2"])[:, [n - 8 for n in order[:14]]]
    vectors = {
        "q_norm_g": np.tile(g["q_norm_g"], 2).T, "k_norm_g": np.tile(g["k_norm_g"], 2).T,
        "conv_w": conv_w, "conv_b": conv_b,
        "conv_dw_w_2": g["conv_dw_w_2"][0].reshape(31, 4, P).transpose(2, 1, 0).reshape(P, -1), "rwkv_mu_2": mu,
        "eps": np.broadcast_to(np.array([[1e-6, 64e-5, 1e-5]], np.float32), (P, 3)),
    }
    lora = np.concatenate([np.concatenate([g["rwkv_w2_2"][0], g["rwkv_a2_2"][0]], 0), g["rwkv_g2_2"][0]], 1)
    arrays = {
        "xT": g["x"][0].T.reshape(KT, P, TOK).transpose(1, 0, 2).reshape(P, -1),
        "vec": np.concatenate([vectors[n] if n in vectors else columns(g[n]) for n, _ in VECTORS], 1),
        "consts": constants(),
        "lora": lora,
        "w_pool": g["w_pool"][0].transpose(1, 0, 2).reshape(P, -1),
        "keys": g["peer_sub_keys_2"].reshape(16, NKEY, P).transpose(2, 0, 1).reshape(P, -1),
        "w_in": reduce_tiles(g["w_in"][0]),
        "w_branch": np.concatenate([g["w_branch_attn"][0], g["w_branch_pool"][0]], 0).reshape(8, P, CHUNK),
        "w_out": reduce_tiles(g["w_out"][0]),
        "w_up": up,
        "w_down": g["w_down"].reshape(NF, P, CHUNK),
        "ada": g["ada_w_2"][0].reshape(KT, P, 6, CHUNK).transpose(2, 0, 1, 3).reshape(ADA, P, CHUNK),
        "w_in2": reduce_tiles(g["w_in_2"][0])[order],
        "w_out2": reduce_tiles(g["w_out_2"][0]),
        "w_q": reduce_tiles(g["peer_w_q_2"][0]),
        "u": g["peer_u_2"].reshape(NKEY, NKEY, KT, P).transpose(1, 3, 2, 0).reshape(NKEY, P, CHUNK),
        "v": g["peer_v_2"].reshape(NKEY, NKEY, D).transpose(1, 0, 2),
    }
    arrays = {"in_" + n: np.ascontiguousarray(a) for n, a in arrays.items()}
    nc = bacc.Bacc("TRN2", target_bir_lowering=False, num_devices=1)
    aps = {n[3:]: nc.dram_tensor(n, a.shape, F32, kind="ExternalInput").ap() for n, a in arrays.items()}
    aps["spill"] = nc.dram_tensor("x_spill", (P, KT * TOK), F32, kind="Internal").ap()
    out = nc.dram_tensor("out", (P, KT * TOK), F32, kind="ExternalOutput").ap()
    build(nc, aps, out)
    r = run_bass_kernel_spmd(nc, [arrays], core_ids=[0])
    got = np.asarray(r.results[0]["out"])
    return got.reshape(P, KT, TOK).transpose(2, 1, 0).reshape(1, TOK, D)
```
